# Optimizing a Trainium2 kernel written in Bass

```python
import jax, jax.numpy as jnp
from jax import lax
import numpy as np

D_MODEL = 1024
BATCH = 1
SEQ = 1024
DEPTH = 1

GRID_W = 64
CTX_LEN = 256
D_MIX = D_MODEL
A_W = D_MIX // 2
A_GROUPS = 8
A_HEAD = A_W // A_GROUPS
CHUNK = 128
B_W = D_MIX - A_W
B_HEADS = 8
B_HEAD = B_W // B_HEADS
DECAY_LORA = 64
AAA_LORA = 64
GATE_LORA = 128
CONV_K = 3
OFF_K = 0
OFF_V = B_W
OFF_R = 2 * B_W
OFF_WD = 3 * B_W
OFF_AD = OFF_WD + 2 * DECAY_LORA
OFF_GD = OFF_AD + 2 * AAA_LORA
OFF_U = OFF_GD + GATE_LORA
OFF_VA = OFF_U + A_W
D_IN = OFF_VA + A_W
N_GROUPS = 4
EXPERTS_PER_GROUP = 8
N_EXPERTS = N_GROUPS * EXPERTS_PER_GROUP
TOP_K_IN_GROUP = 2
D_EXPERT = 256
NORM_EPS = 1e-6
LN_EPS = 1e-5
GN_EPS = 64e-5

kernel_name = "hymba_gmlp_rwkv7_hmoe_dit_layer"

def rms_norm(x, g):
    x32 = x.astype(jnp.float32)
    y = x32 * lax.rsqrt(jnp.mean(x32 * x32, axis=-1, keepdims=True) + NORM_EPS)
    return (y * g.astype(jnp.float32)).astype(x.dtype)

def adaln(cond, w_mod, b_mod, n_chunks):
    m = jax.nn.silu(cond) @ w_mod[:, : n_chunks * D_MODEL] + b_mod[: n_chunks * D_MODEL]
    return jnp.split(m, n_chunks, axis=-1)

def modulate(h, shift, scale):
    return h * (1.0 + scale) + shift

def grid_dwconv(z, kernel, width):
    b, t, ch = z.shape
    rows = t // width
    img = z.reshape(b, rows, width, ch)
    out = lax.conv_general_dilated(
        img, kernel[:, :, None, :].astype(z.dtype), (1, 1), "SAME",
        dimension_numbers=("NHWC", "HWIO", "NHWC"), feature_group_count=ch)
    return out.reshape(b, t, ch)

def chunk_gmlp(u, v, ln_g, ln_b, w_s, b_s):
    b, t, _ = u.shape
    n_chunks = t // CHUNK
    uh = jax.nn.gelu(u).reshape(b, n_chunks, CHUNK, A_GROUPS, A_HEAD)
    v32 = jax.nn.gelu(v).astype(jnp.float32).reshape(b, n_chunks, CHUNK, A_GROUPS, A_HEAD)
    mu = jnp.mean(v32, axis=-1, keepdims=True)
    var = jnp.mean(jnp.square(v32 - mu), axis=-1, keepdims=True)
    vn = (v32 - mu) * lax.rsqrt(var + LN_EPS)
    vn = (vn * ln_g.reshape(A_GROUPS, A_HEAD) + ln_b.reshape(A_GROUPS, A_HEAD)).astype(u.dtype)
    s = jnp.einsum("gpq,bcqgd->bcpgd", w_s, vn) + b_s.T[:, :, None]
    return (uh * s).reshape(b, t, A_W)

def to_heads(z):
    return z.reshape(z.shape[0], z.shape[1], B_HEADS, B_HEAD)

def zero_state(b):
    return jnp.zeros((b, B_HEADS, B_HEAD, B_HEAD), jnp.float32)

def rwkv_prepare(k, lora, p):
    kk = to_heads(k * p["k_k"]).astype(jnp.float32)
    kk = kk * lax.rsqrt(jnp.maximum(jnp.sum(kk * kk, axis=-1, keepdims=True), 1e-24))
    dirs = []
    for d in range(2):
        lw = lora[..., d * DECAY_LORA:(d + 1) * DECAY_LORA]
        la = lora[..., 2 * DECAY_LORA + d * AAA_LORA: 2 * DECAY_LORA + (d + 1) * AAA_LORA]
        w = -jax.nn.softplus(-(p["decay_w0"][d] + jnp.tanh(lw) @ p["decay_up"][d])) - 0.5
        decay = jnp.exp(-jnp.exp(w.astype(jnp.float32)))
        a = jax.nn.sigmoid(p["iclr_a0"][d] + la @ p["iclr_up"][d])
        k_mod = k * (1.0 + (a - 1.0) * p["k_a"][d])
        dirs.append((to_heads(decay), to_heads(a), to_heads(k_mod)))
    return kk, dirs

def _state_update(S, w_t, kk_t, kka_t, k_t, v_t):
    s_kk = jnp.einsum("bhvk,bhk->bhv", S, kk_t)
    return (S * w_t[:, :, None, :] - s_kk[..., None] * kka_t[:, :, None, :]
            + v_t[..., None] * k_t[:, :, None, :])

def _time_major(a):
    return jnp.moveaxis(a.astype(jnp.float32), 1, 0)

def rwkv_scan(state0, decay, kk, kka, k, v, r, reverse):
    xs = (_time_major(decay), _time_major(kk), _time_major(kka), _time_major(k),
          _time_major(v), _time_major(r))

    def step(S, inp):
        S = _state_update(S, *inp[:5])
        return S, jnp.einsum("bhvk,bhk->bhv", S, inp[5])

    s_final, ys = lax.scan(step, state0, xs, reverse=reverse)
    return jnp.moveaxis(ys, 0, 1), s_final

def rwkv_final_state(state0, decay, kk, kka, k, v, reverse):
    xs = (_time_major(decay), _time_major(kk), _time_major(kka), _time_major(k), _time_major(v))

    def step(S, inp):
        return _state_update(S, *inp), None

    s_final, _ = lax.scan(step, state0, xs, reverse=reverse)
    return s_final

def rwkv_mix(k, v, r, lora, gd, p, states0):
    b, t, _ = k.shape
    kk, dirs = rwkv_prepare(k, lora, p)
    vh, rh = to_heads(v), to_heads(r)
    ys, bonus, finals = [], [], []
    for d, (decay, a, k_mod) in enumerate(dirs):
        y_d, s_d = rwkv_scan(states0[d], decay, kk, kk * a, k_mod, vh, rh, reverse=(d == 1))
        ys.append(y_d)
        finals.append(s_d)
        bonus.append(jnp.sum(rh * k_mod * p["r_k"], axis=-1, keepdims=True))
    y = ys[0] + ys[1]
    mu = jnp.mean(y, axis=-1, keepdims=True)
    var = jnp.mean(jnp.square(y - mu), axis=-1, keepdims=True)
    y = (y - mu) * lax.rsqrt(var + GN_EPS)
    y = y * p["lnx_g"].reshape(B_HEADS, B_HEAD) + p["lnx_b"].reshape(B_HEADS, B_HEAD)
    y = y.astype(k.dtype) + (bonus[0] + bonus[1]) * vh
    gate = jax.nn.sigmoid(gd) @ p["outgate_up"]
    return y.reshape(b, t, B_W) * gate, finals

def token_mixer(h, p, width, states0):
    z = h @ p["w_in"]
    rkv = grid_dwconv(z[..., OFF_K:OFF_WD], p["conv_rkv"], width)
    k, v, r = rkv[..., :B_W], rkv[..., B_W:2 * B_W], rkv[..., 2 * B_W:]
    out_b, finals = rwkv_mix(k, v, r, z[..., OFF_WD:OFF_GD], z[..., OFF_GD:OFF_U], p, states0)
    out_a = chunk_gmlp(z[..., OFF_U:OFF_VA], z[..., OFF_VA:], p["gm_ln_g"], p["gm_ln_b"],
                       p["w_spatial"], p["b_spatial"])
    return jnp.concatenate([out_a, out_b], axis=-1) @ p["w_out"], finals

def context_states(h_ctx, p):
    kv = grid_dwconv(h_ctx @ p["w_in"][:, OFF_K:OFF_R], p["conv_rkv"][..., OFF_K:OFF_R], CTX_LEN)
    k, v = kv[..., :B_W], kv[..., B_W:]
    kk, dirs = rwkv_prepare(k, h_ctx @ p["w_in"][:, OFF_WD:OFF_GD], p)
    s0 = zero_state(h_ctx.shape[0])
    vh = to_heads(v)
    return [rwkv_final_state(s0, decay, kk, kk * a, k_mod, vh, reverse=(d == 1))
            for d, (decay, a, k_mod) in enumerate(dirs)]

def hier_moe(h, p):
    shape = h.shape
    h2 = h.reshape(-1, D_MODEL)
    n = h2.shape[0]
    grp_logits = (h2 @ p["w_router_grp"] + p["b_router_grp"]).astype(jnp.float32)
    g_w, g_i = lax.top_k(jax.nn.softmax(grp_logits, axis=-1), 1)
    exp_logits = (h2 @ p["w_router_exp"] + p["b_router_exp"]).astype(jnp.float32)
    exp_logits = exp_logits.reshape(n, N_GROUPS, EXPERTS_PER_GROUP)
    sel = jnp.take_along_axis(exp_logits, g_i[:, :, None], axis=1)[:, 0]
    e_w, e_i = lax.top_k(jax.nn.softmax(sel, axis=-1), TOP_K_IN_GROUP)
    e_w = e_w / jnp.sum(e_w, axis=-1, keepdims=True)
    weights = g_w * e_w
    expert_id = g_i * EXPERTS_PER_GROUP + e_i
    combine = jnp.einsum("nke,nk->ne", jax.nn.one_hot(expert_id, N_EXPERTS, dtype=jnp.float32),
                         weights).astype(h.dtype)
    y = jnp.zeros_like(h2)
    for e in range(N_EXPERTS):
        hid = jax.nn.silu(h2 @ p["w_gate"][e]) * (h2 @ p["w_up"][e])
        y = y + combine[:, e:e + 1] * (hid @ p["w_down"][e])
    return y.reshape(shape)

def setup_inputs(seed: int = 0) -> dict:
    key = jax.random.key(seed)
    ks = iter(jax.random.split(key, 40))

    def nrm(shape, scale):
        return scale * jax.random.normal(next(ks), shape, jnp.float32)

    L, D = DEPTH, D_MODEL
    return {
        "x": nrm((BATCH, SEQ, D), 1.0),
        "c": nrm((BATCH, D), 1.0),
        "ctx": nrm((BATCH, CTX_LEN, D), 1.0),
        "c_ctx": nrm((D,), 1.0),
        "w_mod": nrm((L, D, 6 * D), 0.5 * D ** -0.5),
        "b_mod": nrm((L, 6 * D), 0.01),
        "g_pre1": 1.0 + nrm((L, D), 0.05),
        "g_post1": 1.0 + nrm((L, D), 0.05),
        "g_pre2": 1.0 + nrm((L, D), 0.05),
        "g_post2": 1.0 + nrm((L, D), 0.05),
        "w_in": nrm((L, D, D_IN), D ** -0.5),
        "conv_rkv": nrm((L, CONV_K, CONV_K, 3 * B_W), 1.0 / 3.0),
        "gm_ln_g": 1.0 + nrm((L, A_W), 0.05),
        "gm_ln_b": nrm((L, A_W), 0.01),
        "w_spatial": nrm((L, A_GROUPS, CHUNK, CHUNK), CHUNK ** -0.5),
        "b_spatial": 1.0 + nrm((L, A_GROUPS, CHUNK), 0.05),
        "decay_w0": jax.random.uniform(next(ks), (L, 2, B_W), jnp.float32, -6.0, 0.0),
        "decay_up": nrm((L, 2, DECAY_LORA, B_W), 0.5 * DECAY_LORA ** -0.5),
        "iclr_a0": nrm((L, 2, B_W), 0.5),
        "iclr_up": nrm((L, 2, AAA_LORA, B_W), 0.5 * AAA_LORA ** -0.5),
        "k_k": 1.0 + nrm((L, B_W), 0.1),
        "k_a": 1.0 + nrm((L, 2, B_W), 0.1),
        "r_k": nrm((L, B_HEADS, B_HEAD), 0.1),
        "outgate_up": nrm((L, GATE_LORA, B_W), GATE_LORA ** -0.5),
        "lnx_g": 1.0 + nrm((L, B_W), 0.05),
        "lnx_b": nrm((L, B_W), 0.01),
        "w_out": nrm((L, D_MIX, D), D_MIX ** -0.5),
        "w_router_grp": nrm((L, D, N_GROUPS), D ** -0.5),
        "b_router_grp": nrm((L, N_GROUPS), 0.01),
        "w_router_exp": nrm((L, D, N_EXPERTS), D ** -0.5),
        "b_router_exp": nrm((L, N_EXPERTS), 0.01),
        "w_gate": nrm((L, N_EXPERTS, D, D_EXPERT), D ** -0.5),
        "w_up": nrm((L, N_EXPERTS, D, D_EXPERT), D ** -0.5),
        "w_down": nrm((L, N_EXPERTS, D_EXPERT, D), D_EXPERT ** -0.5),
    }

def reference(x, c, ctx, c_ctx, w_mod, b_mod, g_pre1, g_post1, g_pre2, g_post2, w_in, conv_rkv,
              gm_ln_g, gm_ln_b, w_spatial, b_spatial, decay_w0, decay_up, iclr_a0, iclr_up,
              k_k, k_a, r_k, outgate_up, lnx_g, lnx_b, w_out, w_router_grp, b_router_grp,
              w_router_exp, b_router_exp, w_gate, w_up, w_down):
    for layer in range(DEPTH):
        p = {
            "w_in": w_in[layer], "conv_rkv": conv_rkv[layer],
            "gm_ln_g": gm_ln_g[layer], "gm_ln_b": gm_ln_b[layer],
            "w_spatial": w_spatial[layer], "b_spatial": b_spatial[layer],
            "decay_w0": decay_w0[layer], "decay_up": decay_up[layer],
            "iclr_a0": iclr_a0[layer], "iclr_up": iclr_up[layer],
            "k_k": k_k[layer], "k_a": k_a[layer], "r_k": r_k[layer],
            "outgate_up": outgate_up[layer], "lnx_g": lnx_g[layer], "lnx_b": lnx_b[layer],
            "w_out": w_out[layer],
            "w_router_grp": w_router_grp[layer], "b_router_grp": b_router_grp[layer],
            "w_router_exp": w_router_exp[layer], "b_router_exp": b_router_exp[layer],
            "w_gate": w_gate[layer], "w_up": w_up[layer], "w_down": w_down[layer],
        }
        last = layer == DEPTH - 1
        shift1, scale1, gate1, shift2, scale2, gate2 = adaln(c[:, None, :], w_mod[layer], b_mod[layer], 6)
        if last:
            cshift1, cscale1 = adaln(c_ctx, w_mod[layer], b_mod[layer], 2)
            h_ctx = modulate(rms_norm(ctx, g_pre1[layer]), cshift1, cscale1)
            states = context_states(h_ctx, p)
        else:
            cshift1, cscale1, cgate1, cshift2, cscale2, cgate2 = adaln(c_ctx, w_mod[layer], b_mod[layer], 6)
            h_ctx = modulate(rms_norm(ctx, g_pre1[layer]), cshift1, cscale1)
            zs = zero_state(ctx.shape[0])
            y_ctx, states = token_mixer(h_ctx, p, CTX_LEN, [zs, zs])
            ctx = ctx + cgate1 * rms_norm(y_ctx, g_post1[layer])
            h_ctx = modulate(rms_norm(ctx, g_pre2[layer]), cshift2, cscale2)
            ctx = ctx + cgate2 * rms_norm(hier_moe(h_ctx, p), g_post2[layer])
        h = modulate(rms_norm(x, g_pre1[layer]), shift1, scale1)
        y, _ = token_mixer(h, p, GRID_W, states)
        x = x + gate1 * rms_norm(y, g_post1[layer])
        h = modulate(rms_norm(x, g_pre2[layer]), shift2, scale2)
        x = x + gate2 * rms_norm(hier_moe(h, p), g_post2[layer])
    return x


_drawn_inputs = setup_inputs


def setup_inputs(seed=0):
    import zlib

    import numpy as np

    out = dict(_drawn_inputs(seed))
    spreads = {}
    factors = {'g_post2': 3.791,
     'gm_ln_b': 4.964,
     'lnx_b': 4.711,
     'b_router_grp': 6.555,
     'b_router_exp': 3.01}
    for name, (base, spread) in spreads.items():
        noise = np.random.default_rng([zlib.crc32(name.encode()), seed]).standard_normal(out[name].shape)
        drawn = base * np.exp(spread * noise) if base else spread * noise
        out[name] = __import__('jax').numpy.asarray(drawn.astype(out[name].dtype))
    for name, factor in factors.items():
        out[name] = (out[name] * factor).astype(out[name].dtype)
    return out
```

```python
from contextlib import ExitStack

import numpy as np
import concourse.bass as bass
from concourse import mybir

F32 = mybir.dt.float32
I32 = mybir.dt.int32
U32 = mybir.dt.uint32
ACT = mybir.ActivationFunctionType
ALU = mybir.AluOpType
AX = mybir.AxisListType

P = 128
D = 1024
KT = D // P
SEQ, CTX = 1024, 256
TL, TC = SEQ // P, CTX // P
TT = TL + TC
NTOK = SEQ + CTX
GRID = 64
ROWS = SEQ // GRID
AW = 512
BW = 512
HD = 64
J = BW // P
D_IN = 3 * BW + 3 * P + 2 * AW
OFF_U = 3 * BW + 3 * P
NE, NG, EPG = 32, 4, 8
DE = 256
EPS, LN_EPS, GN_EPS = 1e-6, 1e-5, 64e-5
KAPPA = float(np.exp(-0.5))
CAP = 128
NOVER = 2 * SEQ // (CAP + 1)
LEVELS = (2, 4, 8, 16, 32, 64)
PADW = GRID + 2
ZC = CTX + 2
ZL = (ROWS + 2) * PADW
CH = P + 1


def constants():
    s = np.arange(P)[:, None]
    t = np.arange(P)[None, :]
    out, at = [], {}

    def put(name, a):
        a = np.asarray(a, np.float32).reshape(P, -1)
        at[name] = (sum(x.shape[1] for x in out), a.shape[1])
        out.append(a)

    put("ident", s == t)
    put("ones", np.ones((P, P)))
    put("headblock", (s // HD) == (t // HD))
    put("headcol", (s // HD) == np.arange(2)[None, :])
    put("tri", np.stack([t > s, t >= s, t < s, t <= s], 1))
    lev = np.zeros((P, len(LEVELS), 2, HD))
    for li, m in enumerate(LEVELS):
        for d in range(2):
            for c in range(HD):
                b = c // m
                even, odd = b * 2 * m, b * 2 * m + m
                partner = odd if d == 0 else even
                lev[partner:partner + m, li, d, c] = 1
    put("level", lev)
    pair = np.zeros((P, 2, P))
    for a in range(0, P, 2):
        pair[a, 0, a + 1] = -1
        pair[a + 1, 1, a] = -1
    pair += np.eye(P)[:, None, :]
    put("pair", pair)
    reset = np.ones((P, 2, TT, CH))
    reset[:, 0, :, 0] = 0
    reset[:, 1, :, P] = 0
    put("reset", reset)
    put("slotrow", np.broadcast_to(np.arange(P)[None], (P, P)))
    put("partition", np.arange(P)[:, None])
    put("erow", np.broadcast_to(np.arange(NE)[None], (P, NE)))
    put("tilerow", np.broadcast_to(np.arange(NE + NOVER)[None], (P, NE + NOVER)))
    return np.concatenate(out, 1), at


CONSTS, CAT = constants()


class Chain:

    def __init__(self, eng, sem):
        self.eng, self.sem, self.done, self.base, self.n = eng, sem, 0, 0, 0

    def loop(self, i, per):
        self.base, self.n, self.per = self.done + i * per, 0, per

    def leave(self, passes):
        assert self.n == self.per, (self.n, self.per)
        self.done += passes * self.per
        self.base, self.n = self.done, 0

    def link(self, ins):
        self.n += 1
        ins.then_inc(self.sem, 1)
        self.eng.wait_ge(self.sem, self.base + self.n)


def backwards(ap):
    (ps, pn), (fs, fn) = ap.ap
    return bass.AP(ap.tensor, ap.offset + fs * (fn - 1), [[ps, pn], [-fs, fn]])


def passes(eng, n, body):
    body(0, True)
    with eng.Fori(1, n) as i:
        body(i, False)


def ends(eng, n, body, lead=1):
    for i in range(lead):
        body(i, i == 0, False)
    with eng.Fori(lead, n - 1) as i:
        body(i, False, False)
    body(n - 1, False, True)


def program(nc, a, out, scratch, dbg):
    top = ExitStack()

    def sb(ctx, name, shape, dt=F32):
        return ctx.enter_context(nc.sbuf_tensor(name, shape, dt))

    def pb(ctx, name, shape, dt=F32):
        return ctx.enter_context(nc.psum_tensor(name, shape, dt))

    taken = {}

    def sem(ctx, name):
        if id(ctx) not in taken:
            taken[id(ctx)] = mine = []

            def give_back():
                nc.clear_and_free_semaphores(mine)
                nc.all_engine_barrier()
                del taken[id(ctx)]

            ctx.callback(give_back)
        taken[id(ctx)].append(nc.alloc_semaphore(name))
        return taken[id(ctx)][-1]

    def const(tile, name, first="ident"):
        o, n = CAT[name]
        o -= CAT[first][0]
        return tile[:, o:o + n]

    with top:
        cst = sb(top, "cst", [P, CAT["reset"][0]])
        ident, ones = const(cst, "ident"), const(cst, "ones")
        headblock, headcol = const(cst, "headblock"), const(cst, "headcol")
        mod = sb(top, "mod", [P, 48, 2])
        vec1 = sb(top, "vec1", [P, 80])
        convw = sb(top, "convw", [P, 9, 12])
        vec3 = sb(top, "vec3", [P, 40])
        g1 = sb(top, "g1", [P, KT, 2])
        rstd1 = sb(top, "rstd1", [P, TT])
        eps = sb(top, "eps", [P, 4])
        SH1, SC1, GT1, SH2, SC2, GT2 = (i * KT for i in range(6))

        vt = sb(top, "vt", [P, TT, BW])
        bon = sb(top, "bon", [P, 2, TL, 8])
        mixer = ExitStack()
        with mixer:
            kvr = sb(mixer, "kvr", [P, 12, NTOK])
            la = sb(mixer, "la", [P, NTOK])
            head = ExitStack()
            with head:
                lw = sb(head, "lw", [P, NTOK])
                sg = sb(head, "sg", [P, NTOK])
                hT = sb(head, "hT", [P, KT, NTOK])
                with ExitStack() as c1:
                    RING = 3
                    wm = [sb(c1, f"wm{i}", [P, KT, 512]) for i in range(RING)]
                    cc = sb(c1, "cc", [P, 2, KT])
                    cs = sb(c1, "cs", [P, 2, KT])
                    rows = sb(c1, "rows", [P, 3, P])
                    room = kvr[:, :, :].rearrange("p a b -> p (a b)")
                    xa = room[:, 0:TT * D].rearrange("p (t d) -> p t d", d=D)
                    xn = room[:, TT * D:(TT + 2) * D].rearrange("p (t d) -> p t d", d=D)
                    sqj = room[:, (TT + 2) * D:(TT + 3) * D]
                    ssq = sb(c1, "ssq", [P, 2, TT])
                    psM = pb(c1, "psM", [P, 48, 2])
                    psV = pb(c1, "psV", [P, 3, P])
                    psX = [pb(c1, f"psX{i}", [P, KT, P]) for i in range(2)]
                    s_cst, s_cc, s_rows, s_x = (sem(c1, n) for n in ("s_cst", "s_cc", "s_rows", "s_xin"))
                    s_wm = [sem(c1, f"s_wm{i}") for i in range(RING)]
                    s_silu, s_mm, s_vt, s_vec, s_mod, s_modps = (
                        sem(c1, n) for n in ("s_silu", "s_mm", "s_vt", "s_vec", "s_mod", "s_modps"))
                    s_ssq, s_rstd, s_xn, s_xt, s_evA, s_evV, s_eps, s_act, s_dve = (
                        sem(c1, n) for n in ("s_ssq", "s_rstd", "s_xn", "s_xt", "s_evA", "s_evV", "s_eps", "s_act", "s_dve"))
                    NM = 6 * D // 512
                    wmod = a["w_mod"][0].rearrange("(p k) n -> p k n", k=KT)
                    block = c1.enter_context(nc.Block())

                    @block.sync
                    def _(sp):
                        sp.dma_start(cst[:, :], a["consts"][:, 0:CAT["reset"][0]]).then_inc(s_cst, 16)
                        sp.dma_start(cc[:, 0, :], a["c"].rearrange("a (p k) -> p (a k)", k=KT)).then_inc(s_cc, 16)
                        sp.dma_start(cc[:, 1, :], a["c_ctx"].rearrange("(p k) -> p k", k=KT)).then_inc(s_cc, 16)

                        def load(i, first):
                            for b in range(RING):
                                n = i * RING + b
                                if not first:
                                    sp.wait_ge(s_mm, n - RING + 1)
                                sp.dma_start(wm[b][:, :, :], wmod[:, :, bass.ds(n * 512, 512)]).then_inc(s_wm[b], 16)

                        passes(sp, NM // RING, load)

                    @block.gpsimd
                    def _(gp):
                        gp.dma_start(xa[:, 0:TC, :], a["ctx"][0].rearrange("(t p) d -> p t d", p=P)).then_inc(s_x, 16)
                        gp.dma_start(xa[:, TC:TT, :], a["x"][0].rearrange("(t p) d -> p t d", p=P)).then_inc(s_x, 16)
                        r = [("b_mod", 0, 0, 48), ("g_pre1", 0, 48, 8), ("g_post1", 0, 56, 8), ("g_pre2", 0, 64, 8),
                             ("g_post2", 0, 72, 8)]
                        for name, z, at, n in r:
                            gp.dma_start(rows[at:at + n, z, :], a[name][0].rearrange("(n p) -> n p", p=P)).then_inc(s_rows, 16)
                        gp.dma_start(rows[0:108, 1, :], a["conv_rkv"][0].rearrange("y x (n p) -> (y x n) p", p=P)).then_inc(s_rows, 16)
                        at = 0
                        for name in ("decay_w0", "iclr_a0", "k_k", "k_a", "r_k", "b_spatial"):
                            src = a[name][0]
                            if len(src.shape) == 2 and src.shape[1] == P:
                                src = src
                            elif len(src.shape) == 2:
                                src = src.rearrange("a b -> (a b)").rearrange("(n p) -> n p", p=P)
                            else:
                                src = src.rearrange("(n p) -> n p", p=P)
                            n = src.shape[0]
                            gp.dma_start(rows[at:at + n, 2, :], src).then_inc(s_rows, 16)
                            at += n
                        assert at == 40

                    @block.tensor
                    def _(pe):
                        pe.wait_ge(s_cst, 16)
                        pe.wait_ge(s_rows, 12 * 16)
                        for z, n in enumerate((80, 108, 40)):
                            last = pe.transpose(psV[:, z, 0:n], rows[0:n, z, :], ident[0:n, 0:n])
                        last.then_inc(s_vt, 1)
                        pe.wait_ge(s_silu, 1)
                        for n in range(NM):
                            pe.wait_ge(s_wm[n % RING], 16 * (n // RING + 1))
                            for q in range(4):
                                for k in range(KT):
                                    last = pe.matmul(psM[:, 4 * n + q, :], wm[n % RING][:, k, q * P:(q + 1) * P],
                                                     cs[:, :, k], start=(k == 0), stop=(k == KT - 1))
                            last.then_inc(s_mm, 1)

                        def turn(i, first):
                            for b in range(2):
                                t = 2 * i + b
                                pe.wait_ge(s_xn, t + 1)
                                if not first:
                                    pe.wait_ge(s_evA, t - 1)
                                    pe.wait_ge(s_evV, t - 1)
                                for k in range(KT):
                                    last = pe.transpose(psX[b][:, k, :], xn[:, b, k * P:(k + 1) * P], ident)
                                last.then_inc(s_xt, 1)

                        passes(pe, TT // 2, turn)

                    @block.scalar
                    def _(act):
                        act.wait_ge(s_cc, 32)
                        act.activation(cs[:, :, :], cc[:, :, :], ACT.Silu).then_inc(s_silu, 1)
                        act.wait_ge(s_x, 32)
                        for t in range(TT):
                            if t:
                                act.wait_ge(s_ssq, t)
                            act.activation(sqj, xa[:, t, :], ACT.Square, accum_out=ssq[:, 0, t:t + 1]).then_inc(s_ssq, 1)
                        act.wait_ge(s_eps, 1)
                        act.wait_ge(s_ssq, TT)
                        act.activation(ssq[:, 1, :], ssq[:, 0, :], ACT.Sqrt, scale=1.0 / D, bias=eps[:, 0:1]).then_inc(s_act, 1)
                        act.wait_ge(s_mod, 1)
                        for t in range(TT):
                            act.wait_ge(s_xt, t + 1)
                            z = 1 if t < TC else 0
                            for k in range(0, KT // 2):
                                last = act.activation(hT[:, k, t * P:(t + 1) * P], psX[t % 2][:, k, :], ACT.Identity,
                                                      scale=g1[:, k, z:z + 1], bias=mod[:, SH1 + k, z:z + 1])
                            last.then_inc(s_evA, 1)

                    @block.vector
                    def _(dve):
                        ch = Chain(dve, s_dve)
                        for i, e in enumerate((EPS, LN_EPS, GN_EPS, 0.0)):
                            last = dve.memset(eps[:, i:i + 1], e)
                        last.then_inc(s_eps, 1)
                        dve.wait_ge(s_vt, 1)
                        ch.link(dve.tensor_copy(vec1[:, :], psV[:, 0, 0:80]))
                        ch.link(dve.tensor_copy(convw[:, :, :].rearrange("p a b -> p (a b)"), psV[:, 1, 0:108]))
                        ch.link(dve.tensor_copy(vec3[:, :], psV[:, 2, 0:40]))
                        dve.wait_ge(s_act, 1)
                        ch.link(dve.reciprocal(rstd1[:, :], ssq[:, 1, :]))
                        dve.wait_ge(s_mm, NM)
                        for z in range(2):
                            ch.link(dve.tensor_tensor(mod[:, :, z], psM[:, :, z], vec1[:, 0:48], ALU.add))
                        for z in range(2):
                            last = dve.scalar_tensor_tensor(out=g1[:, :, z], in0=mod[:, SC1:SC1 + KT, z], scalar=1.0,
                                                            in1=vec1[:, 48:56], op0=ALU.add, op1=ALU.mult)
                            ch.link(last)
                        dve.tensor_copy(eps[:, 3:4], eps[:, 0:1]).then_inc(s_mod, 1)

                        def norm(t):
                            if t >= 2:
                                dve.wait_ge(s_xt, t - 1)
                            dve.tensor_scalar(xn[:, t % 2, :], xa[:, t, :], rstd1[:, t:t + 1], None, ALU.mult).then_inc(s_xn, 1)

                        norm(0)
                        for t in range(TT):
                            if t + 1 < TT:
                                norm(t + 1)
                            dve.wait_ge(s_xt, t + 1)
                            z = 1 if t < TC else 0
                            for k in range(KT // 2, KT):
                                last = dve.tensor_scalar(hT[:, k, t * P:(t + 1) * P], psX[t % 2][:, k, :],
                                                         g1[:, k, z:z + 1], mod[:, SH1 + k, z:z + 1], ALU.mult, ALU.add)
                            last.then_inc(s_evV, 1)

                with ExitStack() as c2:
                    wr = [sb(c2, f"wr{i}", [P, KT, P]) for i in range(2)]
                    zp = [sb(c2, f"zp{i}", [P, ZC + ZL]) for i in range(2)]
                    psZ = [pb(c2, f"psZ{i}", [P, 3, 512]) for i in range(2)]
                    s_zero, s_pz, s_zev, s_conv, s_dve = (sem(c2, n) for n in ("s_zero", "s_pz", "s_zev", "s_conv", "s_cch"))
                    s_wr = [sem(c2, f"s_wr{i}") for i in range(2)]
                    NF = 15
                    kv2 = kvr[:, :, :].rearrange("p a b -> p (a b)")
                    win = a["w_in"][0].rearrange("(k p) n -> p k n", p=P)
                    block = c2.enter_context(nc.Block())

                    @block.sync
                    def _(sp):
                        def load(i, first):
                            for b in range(2):
                                f = 2 * i + b
                                if not first:
                                    sp.wait_ge(s_pz, f - 1)
                                sp.dma_start(wr[b][:, :, :], win[:, :, bass.ds(f * P, P)]).then_inc(s_wr[b], 16)

                        passes(sp, 7, load)
                        sp.wait_ge(s_pz, NF - 2)
                        sp.dma_start(wr[0][:, :, :], win[:, :, 14 * P:15 * P]).then_inc(s_wr[0], 16)

                    @block.gpsimd
                    def _(gp):
                        for b in range(2):
                            gp.memset(zp[b][:, :], 0.0).then_inc(s_zero, 1)

                    @block.tensor
                    def _(pe):
                        def tile(i, b, first):
                            pe.wait_ge(s_wr[b], 16 * (i + 1))
                            if not first:
                                pe.wait_ge(s_zev, 2 * i + b - 1)
                            for q, (n0, n) in enumerate(((0, 512), (512, 512), (1024, 256))):
                                for k in range(KT):
                                    last = pe.matmul(psZ[b][:, q, 0:n], wr[b][:, k, :], hT[:, k, n0:n0 + n],
                                                     start=(k == 0), stop=(k == KT - 1))
                            last.then_inc(s_pz, 1)

                        def pair(i, first):
                            tile(i, 0, first)
                            tile(i, 1, first)

                        passes(pe, 7, pair)
                        tile(7, 0, False)

                    @block.scalar
                    def _(act):
                        act.wait_ge(s_zero, 2)

                        def spread(i, first):
                            for b in range(2):
                                f = 2 * i + b
                                act.wait_ge(s_pz, f + 1)
                                if not first:
                                    act.wait_ge(s_conv, f - 1)
                                z = psZ[b][:, :, :].rearrange("p a b -> p (a b)")
                                act.activation(zp[b][:, 1:1 + CTX], z[:, 0:CTX], ACT.Copy)
                                g = zp[b][:, ZC:ZC + ZL].rearrange("p (r c) -> p r c", c=PADW)
                                act.activation(g[:, 1:1 + ROWS, 1:1 + GRID],
                                               z[:, CTX:NTOK].rearrange("p (r c) -> p r c", c=GRID),
                                               ACT.Copy).then_inc(s_zev, 1)

                        passes(act, 6, spread)
                        for f, (dst, fn) in enumerate(((lw, ACT.Tanh), (la, ACT.Copy), (sg, ACT.Sigmoid))):
                            act.wait_ge(s_pz, 13 + f)
                            z = psZ[f % 2][:, :, :].rearrange("p a b -> p (a b)")[:, 0:NTOK]
                            act.activation(dst[:, :], z, fn).then_inc(s_zev, 1)

                    @block.vector
                    def _(dve):
                        ch = Chain(dve, s_dve)

                        def conv(i, first):
                            ch.loop(i, 2 * 9)
                            for b in range(2):
                                f = 2 * i + b
                                dve.wait_ge(s_zev, f + 1)
                                g = zp[b][:, ZC:ZC + ZL].rearrange("p (r c) -> p r c", c=PADW)
                                og = kv2[:, bass.ds(f * NTOK + CTX, SEQ)].rearrange("p (r c) -> p r c", c=GRID)
                                oc = kv2[:, bass.ds(f * NTOK, CTX)]
                                for tap in range(9):
                                    y, x = tap // 3, tap % 3
                                    w = convw[:, tap, bass.ds(f, 1)]
                                    src = g[:, y:y + ROWS, x:x + GRID]
                                    if tap == 0:
                                        ins = dve.tensor_scalar(og, src, w, None, ALU.mult)
                                    else:
                                        ins = dve.scalar_tensor_tensor(out=og, in0=src, scalar=w, in1=og,
                                                                       op0=ALU.mult, op1=ALU.add)
                                    if y == 1:
                                        src = zp[b][:, x:x + CTX]
                                        if x == 0:
                                            ins = dve.tensor_scalar(oc, src, w, None, ALU.mult)
                                        else:
                                            ins = dve.scalar_tensor_tensor(out=oc, in0=src, scalar=w, in1=oc,
                                                                           op0=ALU.mult, op1=ALU.add)
                                    ch.link(ins)
                                dve.nop().then_inc(s_conv, 1)

                        passes(dve, 6, conv)

                with ExitStack() as c3:
                    wa = [sb(c3, f"wa{i}", [P, KT, 256]) for i in range(2)]
                    uh = vt[:, 0:TL, :]
                    vn = sb(c3, "vn", [P, TL, AW])
                    ws = sb(c3, "ws", [P, 8, P])
                    wsT = sb(c3, "wsT", [P, 8, P])
                    lnrow = sb(c3, "lnrow", [P, 2, AW])
                    sq = sb(c3, "sq", [P, 4 * AW])
                    st = sb(c3, "st", [P, 4, 2, 32])
                    psA = [pb(c3, f"psA{i}", [P, 512]) for i in range(4)]
                    psT = pb(c3, "psT", [P, 2, 4, P])
                    psG = [pb(c3, f"psG{i}", [P, TL, HD]) for i in range(2)]
                    s_ws, s_ln, s_wst, s_wse, s_pa, s_gelu, s_var, s_std, s_vn, s_sp, s_oa, s_dve, s_st = (
                        sem(c3, n) for n in ("s_ws", "s_ln", "s_wst", "s_wse", "s_pa", "s_gelu", "s_var", "s_std",
                                             "s_vn", "s_sp", "s_oa", "s_ach", "s_st"))
                    s_wa = [sem(c3, f"s_wa{i}") for i in range(2)]
                    quarters = [(vn, OFF_U + AW, 0), (vn, OFF_U + AW, 1), (uh, OFF_U, 0), (uh, OFF_U, 1)]
                    block = c3.enter_context(nc.Block())

                    @block.sync
                    def _(sp):
                        sp.dma_start(ws[:, :, :], a["w_spatial"][0].rearrange("g p q -> p g q")).then_inc(s_ws, 16)
                        for n, (_, off, h) in enumerate(quarters):
                            if n >= 2:
                                sp.wait_ge(s_pa, TL * (n - 1))
                            sp.dma_start(wa[n % 2][:, :, :], win[:, :, off + 256 * h:off + 256 * h + 256]).then_inc(s_wa[n % 2], 16)
                        sp.dma_start(scratch["lw"], lw[:, :]).then_inc(s_st, 16)
                        sp.dma_start(scratch["sg"], sg[:, :]).then_inc(s_st, 16)
                        sp.wait_ge(s_oa, 8)
                        sp.dma_start(scratch["oA"].rearrange("(t p) n -> p t n", p=P), uh).then_inc(s_st, 16)
                        sp.wait_ge(s_st, 48)

                    @block.gpsimd
                    def _(gp):
                        for i, n in enumerate(("gm_ln_g", "gm_ln_b")):
                            gp.dma_start(lnrow[:, i, :], a[n][0:1, :].partition_broadcast(P) if False
                                         else bass.AP(a[n].tensor, 0, [[0, P], [1, AW]])).then_inc(s_ln, 16)

                    @block.tensor
                    def _(pe):
                        pe.wait_ge(s_ws, 16)
                        for g in range(8):
                            last = pe.transpose(psT[:, g // 4, g % 4, :], ws[:, g, :], ident)
                        last.then_inc(s_wst, 1)
                        for n in range(4):
                            pe.wait_ge(s_wa[n % 2], 16 * (n // 2 + 1))
                            for t in range(TL):
                                m = n * TL + t
                                if m >= 4:
                                    pe.wait_ge(s_gelu, m - 3)
                                for k in range(KT):
                                    last = pe.matmul(psA[m % 4][:, 0:256], hT[:, k, CTX + t * P:CTX + (t + 1) * P],
                                                     wa[n % 2][:, k, :], start=(k == 0), stop=(k == KT - 1))
                                last.then_inc(s_pa, 1)
                        pe.wait_ge(s_wse, 1)
                        pe.wait_ge(s_vn, 2)
                        for g in range(8):
                            if g >= 2:
                                pe.wait_ge(s_oa, g - 1)
                            pe.matmul(psG[g % 2][:, :, :], wsT[:, g, :], vn[:, :, g * HD:(g + 1) * HD],
                                      start=True, stop=True).then_inc(s_sp, 1)

                    @block.scalar
                    def _(act):
                        act.wait_ge(s_wst, 1)
                        act.activation(wsT[:, :, :], psT[:, :, :, :].rearrange("p a b c -> p (a b) c"), ACT.Copy).then_inc(s_wse, 1)
                        for n, (dst, _, h) in enumerate(quarters):
                            for t in range(TL):
                                m = n * TL + t
                                act.wait_ge(s_pa, m + 1)
                                act.activation(dst[:, t, h * 256:(h + 1) * 256], psA[m % 4][:, 0:256],
                                               ACT.Gelu_apprx_tanh).then_inc(s_gelu, 1)
                            if n == 2:
                                for hf in range(2):
                                    act.wait_ge(s_var, hf + 1)
                                    act.activation(st[:, 2, hf, :], st[:, 1, hf, :], ACT.Sqrt, scale=1.0 / HD,
                                                   bias=eps[:, 1:2]).then_inc(s_std, 1)

                    @block.vector
                    def _(dve):
                        ch = Chain(dve, s_dve)
                        dve.wait_ge(s_ln, 32)
                        dve.wait_ge(s_gelu, 2 * TL)
                        for hf in range(2):
                            v = vn[:, 4 * hf:4 * hf + 4, :].rearrange("p t (g d) -> p (t g) d", d=HD)
                            q = sq[:, :].rearrange("p (n d) -> p n d", d=HD)
                            ch.link(dve.reduce_sum(st[:, 0, hf, :], v, AX.X))
                            ch.link(dve.tensor_scalar(st[:, 0, hf, :], st[:, 0, hf, :], 1.0 / HD, None, ALU.mult))
                            ch.link(dve.tensor_tensor(v, v, st[:, 0, hf, :].unsqueeze(2).broadcast_to([P, 32, HD]), ALU.subtract))
                            ch.link(dve.tensor_tensor(q, v, v, ALU.mult))
                            dve.reduce_sum(st[:, 1, hf, :], q, AX.X).then_inc(s_var, 1)
                        for hf in range(2):
                            v = vn[:, 4 * hf:4 * hf + 4, :].rearrange("p t (g d) -> p (t g) d", d=HD)
                            w = vn[:, 4 * hf:4 * hf + 4, :]
                            dve.wait_ge(s_std, hf + 1)
                            ch.link(dve.reciprocal(st[:, 3, hf, :], st[:, 2, hf, :]))
                            ch.link(dve.tensor_tensor(v, v, st[:, 3, hf, :].unsqueeze(2).broadcast_to([P, 32, HD]), ALU.mult))
                            ch.link(dve.tensor_tensor(w, w, lnrow[:, 0, :].unsqueeze(1).broadcast_to([P, 4, AW]), ALU.mult))
                            dve.tensor_tensor(w, w, lnrow[:, 1, :].unsqueeze(1).broadcast_to([P, 4, AW]), ALU.add).then_inc(s_vn, 1)
                        dve.wait_ge(s_gelu, 4 * TL)
                        for g in range(8):
                            dve.wait_ge(s_sp, g + 1)
                            o = uh[:, :, g * HD:(g + 1) * HD]
                            dve.scalar_tensor_tensor(out=o, in0=psG[g % 2][:, :, :], scalar=vec3[:, 32 + g:33 + g],
                                                     in1=o, op0=ALU.add, op1=ALU.mult).then_inc(s_oa, 1)

            cum = sb(mixer, "cum", [P, 2, J, TT * CH])
            em = sb(mixer, "em", [P, 2, J, TT])
            em2 = sb(mixer, "em2", [P, 2, J, TT])
            kmid = sb(mixer, "kmid", [P, 2, 2, J, TT])
            iup = sb(mixer, "iup", [P, BW])
            rkm = sb(mixer, "rkm", [P, J, 2])
            omk = sb(mixer, "omk", [P, 8])
            with ExitStack() as c4:
                lwb = sb(c4, "lwb", [P, NTOK])
                dup = sb(c4, "dup", [P, BW])
                rst = sb(c4, "rst", [P, 2, TT * CH])
                dwb = [sb(c4, f"dwb{i}", [P, TT * CH]) for i in range(2)]
                kr = [sb(c4, f"kr{i}", [P, NTOK]) for i in range(2)]
                ks = [sb(c4, f"ks{i}", [P, NTOK]) for i in range(2)]
                psD = [pb(c4, f"psD{i}", [P, 3, 512]) for i in range(2)]
                psT = [pb(c4, f"psVT{i}", [P, J, P]) for i in range(2)]
                s_in, s_zero, s_vt, s_ve, s_pd, s_dw, s_cum, s_kr, s_sq, s_pk, s_mx, s_rt, s_dve, s_em = (
                    sem(c4, n) for n in ("s4_in", "s4_zero", "s4_vt", "s4_ve", "s4_pd", "s4_dw", "s4_cum", "s4_kr",
                                         "s4_sq", "s4_pk", "s4_mx", "s4_rt", "s4_ch", "s4_em"))
                block = c4.enter_context(nc.Block())
                cols = ((0, 512), (512, 512), (1024, 256))

                @block.sync
                def _(sp):
                    sp.dma_start(lwb[:, :], scratch["lw"]).then_inc(s_in, 16)
                    sp.dma_start(dup[:, :], a["decay_up"][0].rearrange("d l n -> (d l) n")).then_inc(s_in, 16)
                    sp.dma_start(iup[:, :], a["iclr_up"][0].rearrange("d l n -> (d l) n")).then_inc(s_in, 16)
                    sp.dma_start(rst[:, :, :], a["consts"][:, CAT["reset"][0]:CAT["slotrow"][0]]).then_inc(s_in, 16)

                @block.gpsimd
                def _(gp):
                    for b in range(2):
                        gp.memset(dwb[b][:, :], 0.0).then_inc(s_zero, 1)

                @block.tensor
                def _(pe):
                    pe.wait_ge(s_in, 64)
                    for j in range(J):
                        for d in range(2):
                            n = 2 * j + d
                            if n >= 2:
                                pe.wait_ge(s_dw, n - 1)
                            for q, (n0, w) in enumerate(cols):
                                last = pe.matmul(psD[n % 2][:, q, 0:w], dup[64 * d:64 * d + 64, j * P:(j + 1) * P],
                                                 lwb[64 * d:64 * d + 64, n0:n0 + w], start=True, stop=True)
                            last.then_inc(s_pd, 1)
                    for t in range(TT):
                        if t >= 2:
                            pe.wait_ge(s_ve, t - 1)
                        for j in range(J):
                            last = pe.transpose(psT[t % 2][:, j, :], kvr[:, J + j, t * P:(t + 1) * P], ident)
                        last.then_inc(s_vt, 1)
                    pe.wait_ge(s_dw, 2 * J)
                    for j in range(J):
                        pe.wait_ge(s_sq, j + 1)
                        if j >= 2:
                            pe.wait_ge(s_mx, j - 1)
                        for q, (n0, w) in enumerate(cols):
                            last = pe.matmul(psD[j % 2][:, q, 0:w], headblock, ks[j % 2][:, n0:n0 + w],
                                             start=True, stop=True)
                        last.then_inc(s_pk, 1)

                @block.scalar
                def _(act):
                    act.wait_ge(s_zero, 2)
                    for j in range(J):
                        for d in range(2):
                            n = 2 * j + d
                            act.wait_ge(s_pd, n + 1)
                            if n >= 2:
                                act.wait_ge(s_cum, n - 1)
                            o = dwb[n % 2][:, :].rearrange("p (c k) -> p c k", k=CH)[:, :, 1 - d:1 - d + P]
                            z = psD[n % 2][:, :, :].rearrange("p a b -> p (a b)")[:, 0:NTOK]
                            act.activation(o, z.rearrange("p (c k) -> p c k", k=P), ACT.Sigmoid,
                                           bias=vec3[:, d * J + j:d * J + j + 1]).then_inc(s_dw, 1)
                    for t in range(TT):
                        act.wait_ge(s_vt, t + 1)
                        act.activation(vt[:, t, :], psT[t % 2][:, :, :].rearrange("p a b -> p (a b)"), ACT.Copy).then_inc(s_ve, 1)
                    act.wait_ge(s_cum, 2 * J)
                    act.wait_ge(s_em, 1)
                    act.activation(em[:, :, :, :], kmid[:, 1, :, :, :], ACT.Exp).then_inc(s_em, 1)
                    for j in range(J):
                        act.wait_ge(s_kr, j + 1)
                        act.activation(ks[j % 2][:, :], kr[j % 2][:, :], ACT.Square).then_inc(s_sq, 1)
                        act.wait_ge(s_mx, j + 1)
                        act.activation(ks[j % 2][:, :], ks[j % 2][:, :], ACT.Sqrt).then_inc(s_rt, 1)

                @block.vector
                def _(dve):
                    ch = Chain(dve, s_dve)
                    dve.wait_ge(s_in, 64)
                    for j in range(J):
                        last = dve.tensor_scalar(rkm[:, j, :], headcol, vec3[:, 28 + j:29 + j], None, ALU.mult)
                    ch.link(dve.tensor_scalar(omk[:, :], vec3[:, 20:28], -1.0, 1.0, ALU.mult, ALU.add))
                    for j in range(J):
                        for d in range(2):
                            n = 2 * j + d
                            dve.wait_ge(s_dw, n + 1)
                            if d == 0:
                                o, m, i = cum[:, d, j, :], rst[:, d, :], dwb[n % 2][:, :]
                            else:
                                o, m, i = (backwards(x) for x in (cum[:, d, j, :], rst[:, d, :], dwb[n % 2][:, :]))
                            dve.tensor_tensor_scan(o, m, i, 0.0, ALU.mult, ALU.add).then_inc(s_cum, 1)
                    dve.wait_ge(s_cum, 2 * J)
                    for d in range(2):
                        end = cum[:, d, :, :].rearrange("p j (c k) -> p j c k", k=CH)[:, :, :, P if d == 0 else 0]
                        last = dve.tensor_scalar(kmid[:, 0, d, :, :], end, KAPPA / 2, None, ALU.mult)
                        last = dve.tensor_scalar(kmid[:, 1, d, :, :], end, -KAPPA / 2, None, ALU.mult)
                    last.then_inc(s_em, 1)
                    dve.wait_ge(s_em, 2)
                    dve.tensor_tensor(em2[:, 0, :, 0:TT - 1], em[:, 0, :, 0:TT - 1], em[:, 0, :, 1:TT], ALU.mult)
                    dve.tensor_tensor(em2[:, 1, :, 1:2], em[:, 1, :, 1:2], em[:, 1, :, 0:1], ALU.mult)
                    dve.tensor_tensor(em2[:, 1, :, 0:1], em[:, 1, :, 0:1], em[:, 1, :, TT - 1:TT], ALU.mult)
                    ch.link(dve.tensor_tensor(em2[:, 1, :, 3:TT], em[:, 1, :, 3:TT], em[:, 1, :, 2:TT - 1], ALU.mult))
                    dve.wait_ge(s_ve, TT)
                    for j in range(J):
                        dve.tensor_scalar(kr[j % 2][:, :], kvr[:, j, :], vec3[:, 16 + j:17 + j], None, ALU.mult).then_inc(s_kr, 1)
                        dve.wait_ge(s_pk, j + 1)
                        z = psD[j % 2][:, :, :].rearrange("p a b -> p (a b)")[:, 0:NTOK]
                        dve.tensor_scalar(ks[j % 2][:, :], z, 1e-24, None, ALU.max).then_inc(s_mx, 1)
                        dve.wait_ge(s_rt, j + 1)
                        ch.link(dve.reciprocal(ks[j % 2][:, :], ks[j % 2][:, :]))
                        ch.link(dve.tensor_tensor(kvr[:, J + j, :], kr[j % 2][:, :], ks[j % 2][:, :], ALU.mult))

            with ExitStack() as c5:
                NL = len(LEVELS)
                lT = sb(c5, "lT", [P, 4, P])
                akT = [sb(c5, f"akT{q}", [P, 4, P]) for q in range(2)]
                rbT = [sb(c5, f"rbT{q}", [P, 4, P]) for q in range(2)]
                rkT = [sb(c5, f"rkT{q}", [P, 4, P]) for q in range(2)]
                inv = [sb(c5, f"inv{q}", [P, 4, P]) for q in range(2)]
                invT = [sb(c5, f"invT{q}", [P, 4, P]) for q in range(2)]
                xl = [sb(c5, f"xl{l}", [P, 2, P]) for l in range(NL)]
                lc = [sb(c5, f"lc{l}", [P, 2, P]) for l in (0, 1, 3, 4)]
                lc = [lc[0], lc[1], lc[0], lc[2], lc[3], lc[1]]
                tc = [sb(c5, f"tc{l}", [P, 2, P]) for l in range(NL - 1)]
                ar = [sb(c5, f"ar{j}", [P, 2, 2, P]) for j in range(J)]
                vs = [sb(c5, f"vs{j}", [P, 2, P]) for j in range(J)]
                bk = [sb(c5, f"bk{q}", [P, 2, 2, P]) for q in range(2)]
                bkt = [sb(c5, f"bkt{q}", [P, 2, 2, P]) for q in range(2)]
                e1 = sb(c5, "e1", [P, 2, CH])
                e2 = sb(c5, "e2", [P, 2, P])
                ag = sb(c5, "ag", [P, 2, P])
                km = sb(c5, "km", [P, 2, P])
                rk = sb(c5, "rk", [P, 2, P])
                las = sb(c5, "las", [P, 2, P])
                un = sb(c5, "un", [P, 4, HD])
                vp = un
                yst = sb(c5, "yst", [P, 4, HD])
                n0 = sb(c5, "n0", [P, J, 2, P])
                psG = pb(c5, "ps5G", [P, 4, 2, 2, P])
                psX = [pb(c5, f"ps5X{q}", [P, 512]) for q in range(2)]
                psT = [pb(c5, f"ps5T{q}", [P, 512]) for q in range(2)]
                names = ("init", "la", "prep", "pch", "amm", "kt", "gram", "t2", "xa", "xb", "ta", "tta", "tb", "ttb",
                         "s1", "s2", "s3", "lt", "tt2", "gr", "xea", "xeb", "ttea", "tteb", "vp", "y", "n", "dch",
                         "sig", "ex", "bkt", "t2e", "tea", "teb", "u", "bonp", "bone", "gate",
                         "lca", "lcb", "tca", "tcb")
                S = {n: sem(c5, f"s5_{n}") for n in names}
                s_y = sem(c5, "s5_yd")
                G = TT * J

                def cols(tile, l, side):
                    m = LEVELS[l]
                    base = tile[:, :, :]
                    ps = base.ap[0][0]
                    first, other = (0, m) if side == 0 else (m, 0)
                    return bass.AP(base.tensor, base.offset + first,
                                   [[ps, P], [2 * P + other - first, 2], [P, 2], [2 * m, HD // m], [1, m]])

                def moving(tile, h, l, side):
                    m = LEVELS[l]
                    base = tile[:, h, :]
                    first, other = (0, m) if side == 0 else (m, 0)
                    return bass.AP(base.tensor, base.offset + first,
                                   [[base.ap[0][0], P], [2 * P + other - first, 2], [2 * m, HD // m], [1, m]])

                def mixed(tile, l):
                    m = LEVELS[l]
                    base = tile[:, 2:, :]
                    return bass.AP(base.tensor, base.offset,
                                   [[base.ap[0][0], P], [P, 2], [2 * m, HD // m], [m - 2 * P, 2], [1, m]])

                def apart(tile, l, h=None):
                    m = LEVELS[l]
                    base = tile[:, h or 0, :]
                    heads = [[P, 2]] if h is None else []
                    return bass.AP(base.tensor, base.offset,
                                   [[base.ap[0][0], P], [m, 2]] + heads + [[2 * m, HD // m], [1, m]])

                def five(tile, l, off=0):
                    m = LEVELS[l]
                    return tile[:, off:off + 256].rearrange("p (h d b i) -> p d h b i", d=2, h=2, i=m)

                def back(c):
                    return (1 - c if c < TC else TT + 1 - c) if isinstance(c, int) else (TT + 1) - c

                def where(c):
                    return c, back(c)

                def run(eng, group):
                    def step(c, last=False):
                        for j in range(J):
                            g = c * J + j
                            prev = (c, j - 1, g - 1) if j else (c - 1, J - 1, g - 1)
                            nxt = (c, j + 1, g + 1) if j + 1 < J else (c + 1, 0, g + 1)
                            if isinstance(c, int) and c == 0 and j == 0:
                                prev = None
                            if last and j == J - 1:
                                nxt = None
                            group(c, j, g, prev, nxt)
                    for c in range(TC + 1):
                        step(c)
                    with eng.Fori(TC + 1, TT - 1) as c:
                        step(c)
                    step(TT - 1, last=True)
                    group(None, None, G, (TT - 1, J - 1, G - 1), None)

                def early(c):
                    return isinstance(c, int) and c < TC

                kflat = kvr[:, :, :].rearrange("p a b -> p (a b)")
                vflat = vt[:, :, :].rearrange("p a b -> p (a b)")
                cumf = cum[:, :, :, :].rearrange("p a b c -> p (a b c)")
                kmf = kmid[:, :, :, :, :].rearrange("p z a b c -> p (z a b c)")
                em2f = em2[:, :, :, :].rearrange("p a b c -> p (a b c)")
                bonf = bon[:, :, :, :].rearrange("p a b c -> p (a b c)")
                block = c5.enter_context(nc.Block())

                @block.gpsimd
                def _(gp):
                    for l in range(NL):
                        gp.memset(xl[l][:, :, :], 0.0)
                    for q in range(2):
                        for m in (akT, rbT, rkT):
                            gp.memset(m[q][:, :, :], 0.0)
                    for u in range(4):
                        gp.tensor_copy(lT[:, u, :], ident)
                    gp.memset(n0[:, :, :, :], 0.0).then_inc(S["init"], 1)

                    def prep(c, j, g, first=False):
                        at = where(c)
                        if not first:
                            gp.wait_ge(S["amm"], g)
                        gp.sem_inc(S["gate"], 1)
                        for d in range(2):
                            o = at[d] * P
                            gp.tensor_copy(las[:, d, :], la[:, bass.ds(o, P)])
                        if not (isinstance(g, int) and g < 4):
                            gp.wait_ge(S["s3"], g - 3)
                        gp.sem_inc(S["gate"], 1)
                        for d in range(2):
                            last = gp.tensor_copy(vs[j][:, d, :], vflat[:, bass.ds(at[d] * BW + j * P, P)])
                        last.then_inc(S["la"], 1)
                        q = j % 2
                        gp.wait_ge(S["sig"], g + 1)
                        gp.wait_ge(S["ex"], g + 1)
                        if not (isinstance(g, int) and g < 2):
                            gp.wait_ge(S["gram"], g - 1)
                            gp.wait_ge(S["kt"], g - 1)
                        if not first:
                            gp.wait_ge(S["bonp"], g)
                        gp.sem_inc(S["gate"], 1)
                        for d in range(2):
                            o = at[d] * P
                            kk = kflat[:, bass.ds((J + j) * NTOK + o, P)]
                            r = kflat[:, bass.ds((2 * J + j) * NTOK + o, P)]
                            excl, incl = (0, 1) if d == 0 else (1, 0)
                            gp.tensor_scalar(km[:, d, :], ag[:, d, :], vec3[:, 20 + 4 * d + j:21 + 4 * d + j],
                                             omk[:, 4 * d + j:4 * d + j + 1], ALU.mult, ALU.add)
                            gp.tensor_tensor(ar[j][:, d, 0, :], kk, e1[:, d, excl:excl + P], ALU.mult)
                            gp.tensor_tensor(ar[j][:, d, 1, :], r, e1[:, d, incl:incl + P], ALU.mult)
                            last = gp.tensor_tensor(bk[q][:, d, 0, :], kk, ag[:, d, :], ALU.mult)
                        last.then_inc(S["pch"], 1)
                        gp.wait_ge(S["pch"], 2 * g + 1)
                        gp.sem_inc(S["gate"], 1)
                        for d in range(2):
                            k = kflat[:, bass.ds(j * NTOK + at[d] * P, P)]
                            gp.tensor_tensor(km[:, d, :], km[:, d, :], k, ALU.mult)
                            last = gp.tensor_tensor(bk[q][:, d, 0, :], bk[q][:, d, 0, :], e2[:, d, :], ALU.mult)
                        last.then_inc(S["pch"], 1)
                        gp.wait_ge(S["pch"], 2 * g + 2)
                        gp.sem_inc(S["gate"], 1)
                        for d in range(2):
                            r = kflat[:, bass.ds((2 * J + j) * NTOK + at[d] * P, P)]
                            gp.tensor_tensor(rk[:, d, :], km[:, d, :], r, ALU.mult)
                            last = gp.tensor_tensor(bk[q][:, d, 1, :], km[:, d, :], e2[:, d, :], ALU.mult)
                        last.then_inc(S["prep"], 1)

                    prep(0, 0, 0, True)

                    def group(c, j, g, prev, nxt):
                        if nxt:
                            prep(*nxt)

                    run(gp, group)

                @block.tensor
                def _(pe):
                    def rates(c, j, g):
                        pe.wait_ge(S["la"], g + 1)
                        if not (isinstance(g, int) and g < 1):
                            pe.wait_ge(S["gr"], g)
                        for d in range(2):
                            last = pe.matmul(psG[:, d, 0, 0, :], iup[64 * d:64 * d + 64, j * P:(j + 1) * P],
                                             las[64 * d:64 * d + 64, d, :], start=True, stop=True)
                        last.then_inc(S["amm"], 1)

                    def mul(out, left, right, s):
                        for h in range(2):
                            last = pe.matmul(out[:, h * P:(h + 1) * P], left[:, h, :], right(h), start=True, stop=True)
                        last.then_inc(s, 1)

                    def mul_x(q, l, s):
                        mul(psT[q][:, 256:512], lc[l], lambda h: moving(inv[q], h, l, 0), s)

                    def mul_tt(q, l, s):
                        mul(psX[q][:, 256:512], xl[l], lambda h: moving(invT[q], h, l, 1), s)

                    def mul_t(q, l, s):
                        mul(psT[q][:, 0:256], tc[l], lambda h: apart(xl[l], l, h), s)

                    pe.wait_ge(S["init"], 1)
                    rates(0, 0, 0)

                    def group(c, j, g, prev, nxt):
                        q = None if c is None else j % 2
                        if prev:
                            cp, jp, gp_ = prev
                            qp = jp % 2
                        if c is not None:
                            pe.wait_ge(S["prep"], g + 1)
                            if not (isinstance(g, int) and g < 2):
                                pe.wait_ge(S["u"], g - 1)
                            for d in range(2):
                                for z in range(2):
                                    last = pe.transpose(psT[q][:, (2 * d + z) * P:(2 * d + z + 1) * P], bk[q][:, d, z, :], ident)
                            last.then_inc(S["kt"], 1)
                            if not (isinstance(g, int) and g < 1):
                                pe.wait_ge(S["gr"], g)
                                pe.wait_ge(S["bone"], g)
                            pe.wait_ge(S["sig"], g + 1)
                            w = 1 if early(c) else 2
                            for u in range(4):
                                d, h = u // 2, u % 2
                                rows = slice(64 * h, 64 * h + 64)
                                for z in range(2):
                                    last = pe.matmul(psG[:, u, z, 0:w, :], bk[q][rows, d, z, :], ar[j][rows, d, 0:w, :],
                                                     start=True, stop=True)
                            last.then_inc(S["gram"], 1)
                        if prev:
                            pe.wait_ge(S["tea"], 4 * gp_ + 4)
                            pe.wait_ge(S["lcb"], 2 * gp_ + 1)
                            mul_x(qp, 4, S["xb"])
                        if c is not None:
                            pe.wait_ge(S["tt2"], g + 1)
                            if not (isinstance(g, int) and g < 2):
                                pe.wait_ge(S["n"], g - 1)
                            for u in range(4):
                                last = pe.transpose(psX[q][:, u * P:(u + 1) * P], invT[q][:, u, :], ident)
                            last.then_inc(S["t2"], 1)
                        if prev:
                            pe.wait_ge(S["xeb"], 2 * gp_ + 1)
                            pe.wait_ge(S["tcb"], gp_ + 1)
                            mul_t(qp, 4, S["tb"])
                            mul_tt(qp, 4, S["ttb"])
                        for l in range(4):
                            if c is not None:
                                if l == 0:
                                    pe.wait_ge(S["t2e"], g + 1)
                                    pe.wait_ge(S["bkt"], g + 1)
                                else:
                                    pe.wait_ge(S["tea"], 4 * g + l)
                                pe.wait_ge(S["lca"], 4 * g + l + 1)
                                mul_x(q, l, S["xa"])
                            if prev and l == 0:
                                pe.wait_ge(S["teb"], gp_ + 1)
                                pe.wait_ge(S["lcb"], 2 * gp_ + 2)
                                mul_x(qp, 5, S["xb"])
                            if prev and l == 1:
                                pe.wait_ge(S["tteb"], 2 * gp_ + 2)
                                pe.wait_ge(S["gr"], gp_ + 1)
                                if not (isinstance(gp_, int) and gp_ < 4):
                                    pe.wait_ge(S["n"], gp_ - 3)
                                for d in range(2):
                                    pe.matmul(psX[qp][:, d * P:(d + 1) * P], ar[jp][:, d, 0, :], n0[:, jp, d, :],
                                              start=True, stop=False)
                                    for h in range(2):
                                        u = 2 * d + h
                                        last = pe.matmul(psX[qp][:, u * HD:(u + 1) * HD], akT[qp][:, u, :],
                                                         vs[jp][:, d, h * HD:(h + 1) * HD], start=False, stop=(h == 1))
                                last.then_inc(S["s1"], 1)
                            if prev and l == 2:
                                pe.wait_ge(S["u"], gp_ + 1)
                                pe.wait_ge(S["bkt"], gp_ + 1)
                                if not early(cp):
                                    for d in range(2):
                                        o = 256 + d * P
                                        pe.matmul(psX[qp][:, o:o + P], ar[jp][:, d, 1, :], n0[:, jp, d, :],
                                                  start=True, stop=False)
                                        for h in range(2):
                                            u = 2 * d + h
                                            o = 256 + u * HD
                                            pe.matmul(psX[qp][:, o:o + HD], rkT[qp][:, u, :],
                                                      vs[jp][:, d, h * HD:(h + 1) * HD], start=False, stop=False)
                                            pe.matmul(psX[qp][:, o:o + HD], rbT[qp][:, u, :], un[:, u, :],
                                                      start=False, stop=(h == 1))
                                for d in range(2):
                                    o = psX[qp][:, d * P:(d + 1) * P]
                                    pe.matmul(o, bkt[qp][:, d, 1, :], vs[jp][:, d, :], start=True, stop=False)
                                    last = pe.matmul(o, bkt[qp][:, d, 0, :],
                                                     un[:, 2 * d:2 * d + 2, :].rearrange("p a b -> p (a b)"),
                                                     start=False, stop=True)
                                last.then_inc(S["s3"], 1)
                            if c is not None:
                                pe.wait_ge(S["xea"], 4 * g + l + 1)
                                pe.wait_ge(S["tca"], 4 * g + l + 1)
                                mul_t(q, l, S["ta"])
                                mul_tt(q, l, S["tta"])
                            if prev and l == 0:
                                pe.wait_ge(S["xeb"], 2 * gp_ + 2)
                                pe.wait_ge(S["tteb"], 2 * gp_ + 1)
                                mul_tt(qp, 5, S["ttb"])
                            if prev and l == 1:
                                pe.wait_ge(S["vp"], gp_ + 1)
                                for u in range(4):
                                    last = pe.matmul(psT[qp][:, u * HD:(u + 1) * HD], invT[qp][:, u, :], vp[:, u, :],
                                                     start=True, stop=True)
                                last.then_inc(S["s2"], 1)
                            if c is not None and l == 0:
                                pe.wait_ge(S["gr"], g + 1)
                                for d in range(2):
                                    last = pe.matmul(psG[:, 1, 0, 0, 2 * d:2 * d + 2], rk[:, d, :], rkm[:, j, :],
                                                     start=True, stop=True)
                                last.then_inc(S["bonp"], 1)
                            if nxt and l == 2:
                                rates(*nxt)

                    run(pe, group)

                @block.vector
                def _(dve):
                    def mask(name, d, z):
                        return const(cst, name)

                    tri = const(cst, "tri").rearrange("p (d z t) -> p d z t", d=2, z=2)
                    pairm = const(cst, "pair").rearrange("p (d t) -> p d t", d=2)
                    lev = const(cst, "level").rearrange("p (l d i) -> p l d i", l=NL, d=2)
                    dve.wait_ge(S["init"], 1)

                    def keep(dst, z, w, strict):
                        for d in range(2):
                            m = tri[:, d, 0 if strict else 1, :].unsqueeze(1).broadcast_to([P, 2, P]).bitcast(U32)
                            last = dve.copy_predicated(dst[:, 2 * d:2 * d + 2, :], m, psG[:, 2 * d:2 * d + 2, z, w, :])
                        return last

                    def fill(dst, l, side, src, s):
                        dve.sem_inc(S["gate"], 1)
                        o, step = (0, HD) if side == 0 else (HD, -HD)
                        m = bass.AP(lev.tensor, lev[:, l, :, :].offset + o,
                                    [[lev.ap[0][0], P], [step, 2], [0, 2], [LEVELS[l], HD // LEVELS[l]], [1, LEVELS[l]]])
                        dve.copy_predicated(dst, m.bitcast(U32), src).then_inc(s, 1)

                    def x_out(q, l, s):
                        fill(apart(xl[l], l), l, 0, five(psT[q], l, 256), s)

                    def t_out(q, l, s):
                        fill(cols(inv[q], l, 0), l, 0, five(psT[q], l), s)

                    def tt_out(q, l, s):
                        fill(cols(invT[q], l, 1), l, 1, five(psX[q], l, 256), s)

                    def group(c, j, g, prev, nxt):
                        q = None if c is None else j % 2
                        if prev:
                            cp, jp, gp_ = prev
                            qp = jp % 2
                        if c is not None:
                            dve.wait_ge(S["gram"], g + 1)
                            dve.sem_inc(S["gate"], 1)
                            if not (isinstance(g, int) and g < 1):
                                dve.wait_ge(S["lcb"], 2 * g)
                                dve.sem_inc(S["gate"], 1)
                            keep(lT, 0, 0, True).then_inc(S["lt"], 1)
                            dve.wait_ge(S["lt"], g + 1)
                            for d in range(2):
                                last = dve.tensor_tensor(invT[q][:, 2 * d:2 * d + 2, :], lT[:, 2 * d:2 * d + 2, :],
                                                         pairm[:, d, :].unsqueeze(1).broadcast_to([P, 2, P]), ALU.mult)
                            last.then_inc(S["tt2"], 1)
                        if prev:
                            dve.wait_ge(S["xb"], 2 * gp_ + 1)
                            x_out(qp, 4, S["xeb"])
                        if c is not None:
                            last = keep(akT[q], 1, 0, True)
                            if not early(c):
                                keep(rbT[q], 0, 1, False)
                                last = keep(rkT[q], 1, 1, False)
                            last.then_inc(S["gr"], 1)
                        if prev:
                            dve.wait_ge(S["tb"], gp_ + 1)
                            t_out(qp, 4, S["teb"])
                            dve.wait_ge(S["ttb"], 2 * gp_ + 1)
                            tt_out(qp, 4, S["tteb"])
                        for l in range(4):
                            if c is not None:
                                dve.wait_ge(S["xa"], 4 * g + l + 1)
                                x_out(q, l, S["xea"])
                            if prev and l == 0:
                                dve.wait_ge(S["xb"], 2 * gp_ + 2)
                                x_out(qp, 5, S["xeb"])
                            if prev and l == 1:
                                dve.wait_ge(S["s1"], gp_ + 1)
                                dve.tensor_copy(vp[:, :, :], psX[qp][:, 0:256].rearrange("p (u i) -> p u i", u=4)).then_inc(S["vp"], 1)
                            if prev and l == 2:
                                dve.wait_ge(S["s3"], gp_ + 1)
                                dve.tensor_tensor(n0[:, jp, :, :], psX[qp][:, 0:2 * P].rearrange("p (d i) -> p d i", d=2),
                                                  n0[:, jp, :, :], ALU.add).then_inc(S["dch"], 1)
                                if not early(cp):
                                    if not (isinstance(gp_, int) and gp_ < TC * J + 1):
                                        dve.wait_ge(s_y, 32 * (gp_ - TC * J))
                                    dve.tensor_copy(yst[:, :, :], psX[qp][:, 256:512].rearrange("p (u i) -> p u i", u=4)).then_inc(S["y"], 1)
                                dve.wait_ge(S["dch"], gp_ + 1)
                                if isinstance(cp, int) and cp == TT - 1:
                                    dve.nop().then_inc(S["n"], 1)
                                else:
                                    at = where(cp)
                                    for d in range(2):
                                        last = dve.scalar_tensor_tensor(
                                            out=n0[:, jp, d, :], in0=n0[:, jp, d, :],
                                            scalar=em2f[:, bass.ds((d * J + jp) * TT + at[d], 1)],
                                            in1=headblock, op0=ALU.mult, op1=ALU.mult)
                                    last.then_inc(S["n"], 1)
                            if c is not None:
                                dve.wait_ge(S["ta"], 4 * g + l + 1)
                                t_out(q, l, S["tea"])
                                dve.wait_ge(S["tta"], 4 * g + l + 1)
                                tt_out(q, l, S["ttea"])
                            if prev and l == 0:
                                dve.wait_ge(S["ttb"], 2 * gp_ + 2)
                                tt_out(qp, 5, S["tteb"])
                            if c is not None and l == 0:
                                dve.wait_ge(S["bonp"], g + 1)
                                if early(c):
                                    dve.nop().then_inc(S["bone"], 1)
                                else:
                                    at = where(c)
                                    for d in range(2):
                                        last = dve.tensor_copy(bonf[:, bass.ds(d * TL * 8 + (at[d] - TC) * 8 + 2 * j, 2)],
                                                               psG[:, 1, 0, 0, 2 * d:2 * d + 2])
                                    last.then_inc(S["bone"], 1)

                    run(dve, group)

                @block.scalar
                def _(act):
                    def decays(c, j, g):
                        at = where(c)
                        if not (isinstance(g, int) and g < 1):
                            act.wait_ge(S["prep"], g)
                        for d in range(2):
                            o = (d * J + j) * TT * CH + at[d] * CH
                            i = (d * J + j) * TT + at[d]
                            act.activation(e1[:, d, :], cumf[:, bass.ds(o, CH)], ACT.Exp, scale=-KAPPA,
                                           bias=kmf[:, bass.ds(i, 1)])
                            last = act.activation(e2[:, d, :], cumf[:, bass.ds(o + (1 - d), P)], ACT.Exp, scale=KAPPA,
                                                  bias=kmf[:, bass.ds(2 * J * TT + i, 1)])
                        last.then_inc(S["ex"], 1)
                        act.wait_ge(S["amm"], g + 1)
                        for d in range(2):
                            last = act.activation(ag[:, d, :], psG[:, d, 0, 0, :], ACT.Sigmoid,
                                                  bias=vec3[:, 8 + 4 * d + j:9 + 4 * d + j])
                        last.then_inc(S["sig"], 1)

                    def mix(dst, src, l, s, scale=1.0):
                        o = dst[:, :, :].rearrange("p h (b e i) -> p h b e i", e=2, i=LEVELS[l])
                        act.activation(o, mixed(src, l), ACT.Copy, scale=scale).then_inc(s, 1)

                    decays(0, 0, 0)

                    def group(c, j, g, prev, nxt):
                        q = None if c is None else j % 2
                        if prev:
                            cp, jp, gp_ = prev
                            qp = jp % 2
                        if c is not None:
                            act.wait_ge(S["kt"], g + 1)
                            act.activation(bkt[q][:, :, :, :].rearrange("p a b c -> p (a b c)"), psT[q][:, :], ACT.Copy).then_inc(S["bkt"], 1)
                            start = isinstance(g, int) and g < 1
                            act.wait_ge(S["lt"], g + 1)
                            if not start:
                                act.wait_ge(S["xa"], 4 * g - 1)
                            mix(lc[0], lT, 0, S["lca"], -1.0)
                            act.wait_ge(S["tt2"], g + 1)
                            if not start:
                                act.wait_ge(S["ta"], 4 * g - 3)
                            mix(tc[0], invT[q], 0, S["tca"])
                            act.wait_ge(S["t2"], g + 1)
                            act.activation(inv[q][:, :, :].rearrange("p a b -> p (a b)"), psX[q][:, :], ACT.Copy).then_inc(S["t2e"], 1)
                        for l in range(4):
                            if c is not None:
                                if l < 3:
                                    if l == 1:
                                        act.wait_ge(S["xa"], 4 * g + 1)
                                    elif not start:
                                        if l == 0:
                                            act.wait_ge(S["xb"], 2 * g)
                                        else:
                                            act.wait_ge(S["xa"], 4 * g)
                                    mix(lc[l + 1], lT, l + 1, S["lca"], -1.0)
                                if l == 1:
                                    if not start:
                                        act.wait_ge(S["xb"], 2 * g - 1)
                                    mix(lc[4], lT, 4, S["lcb"], -1.0)
                                if l == 2:
                                    act.wait_ge(S["xa"], 4 * g + 2)
                                    mix(lc[5], lT, 5, S["lcb"], -1.0)
                                act.wait_ge(S["ttea"], 4 * g + l + 1)
                                if not start:
                                    act.wait_ge(S["ta" if l < 3 else "tb"], 4 * g + l - 2 if l < 3 else g)
                                mix(tc[l + 1], invT[q], l + 1, S["tca" if l < 3 else "tcb"])
                            if prev and l == 1:
                                act.wait_ge(S["s2"], gp_ + 1)
                                act.activation(un[:, :, :], psT[qp][:, 0:256].rearrange("p (u i) -> p u i", u=4),
                                               ACT.Copy, scale=-1.0).then_inc(S["u"], 1)
                            if nxt and l == 2:
                                decays(*nxt)

                    run(act, group)

                @block.sync
                def _(sp):
                    def group(c, j, g, prev, nxt):
                        if prev and not early(prev[0]):
                            cp, jp, gp_ = prev
                            at = where(cp)
                            sp.wait_ge(S["y"], gp_ - TC * J + 1)
                            for d, y in enumerate(("yf", "yb")):
                                sp.dma_start(scratch[y][bass.ds((at[d] - TC) * P, P), jp * P:(jp + 1) * P],
                                             yst[:, 2 * d:2 * d + 2, :].rearrange("p a b -> p (a b)")).then_inc(s_y, 16)

                    run(sp, group)
                    sp.wait_ge(s_y, 32 * TL * J)

        x1 = sb(top, "x1", [P, TL, D])
        g2row = sb(top, "g2row", [P, D])
        logit = sb(top, "logit", [P, TL, 36])
        with ExitStack() as c6:
            wo = sb(c6, "wo", [P, KT, D])
            sgb = sb(c6, "sgb", [P, NTOK])
            og = sb(c6, "og", [P, BW])
            lnx = sb(c6, "lnx", [P, 2, BW])
            g1row, r2row, s2row = (sb(c6, n, [P, D]) for n in ("g1row", "r2row", "s2row"))
            g1c, g2c, r2c = (sb(c6, n, [P, KT]) for n in ("g1c", "g2c", "r2c"))
            diag = [sb(c6, f"diag{i}", [P, 4, P]) for i in range(2)]
            wrt = sb(c6, "wrt", [P, KT, 36])
            brt = sb(c6, "brt", [P, 36])
            yin = [sb(c6, f"yin{i}", [P, 2, BW]) for i in range(2)]
            oin = [sb(c6, f"oin{i}", [P, BW]) for i in range(2)]
            bv = sb(c6, "bv", [P, BW])
            sq6 = sb(c6, "sq6", [P, BW])
            sqj6 = sb(c6, "sqj6", [P, D])
            st6 = sb(c6, "st6", [P, 6, 8])
            rs6 = sb(c6, "rs6", [P, TL, 8])
            bs = sb(c6, "bs", [P, TL, 8])
            oT = [sb(c6, f"oT{i}", [P, KT, P]) for i in range(2)]
            h2 = [sb(c6, f"h2_{i}", [P, D]) for i in range(2)]
            h2T = sb(c6, "h2T", [P, KT, P])
            psA = pb(c6, "ps6A", [P, BW])
            psO = pb(c6, "ps6O", [P, KT, P])
            psY = pb(c6, "ps6Y", [P, 2, 512])
            psH = pb(c6, "ps6H", [P, KT, P])
            psL = pb(c6, "ps6L", [P, 36])
            S = {n: sem(c6, f"s6_{n}") for n in (
                "par", "wo", "row", "diag", "rps", "gate", "a", "std1", "var1", "ob", "tr", "oT", "y", "ssq", "std2", "x1a",
                "x1", "ssq3", "std3", "h2a", "h2", "tr2", "h2T", "lg", "lge", "ch", "bv", "st", "rd", "pch", "sqa")}
            s_yin = [sem(c6, f"s6_yin{i}") for i in range(2)]
            s_xin = sem(c6, "s6_xin")
            s_st = [sem(c6, f"s6_st{i}") for i in range(2)]
            block = c6.enter_context(nc.Block())
            NPAR = 8

            @block.sync
            def _(sp):
                sp.dma_start(sgb[:, :], scratch["sg"]).then_inc(S["par"], 16)
                sp.dma_start(og[:, :], a["outgate_up"][0]).then_inc(S["par"], 16)
                for i, n in enumerate(("lnx_g", "lnx_b")):
                    sp.dma_start(lnx[:, i, :], bass.AP(a[n].tensor, 0, [[0, P], [1, BW]])).then_inc(S["par"], 16)
                sp.dma_start(wrt[:, :, 0:4], a["w_router_grp"][0].rearrange("(k p) n -> p k n", p=P)).then_inc(S["par"], 16)
                sp.dma_start(wrt[:, :, 4:36], a["w_router_exp"][0].rearrange("(k p) n -> p k n", p=P)).then_inc(S["par"], 16)
                sp.dma_start(brt[:, 0:4], bass.AP(a["b_router_grp"].tensor, 0, [[0, P], [1, 4]])).then_inc(S["par"], 16)
                sp.dma_start(brt[:, 4:36], bass.AP(a["b_router_exp"].tensor, 0, [[0, P], [1, 32]])).then_inc(S["par"], 16)
                sp.dma_start(x1[:, :, :], a["x"][0].rearrange("(t p) d -> p t d", p=P)).then_inc(s_xin, 16)
                for t in range(TL):
                    if t >= 2:
                        sp.wait_ge(S["tr"], t - 1)
                    rows = slice(t * P, (t + 1) * P)
                    for dst, src in ((yin[t % 2][:, 0, :], "yf"), (yin[t % 2][:, 1, :], "yb"), (oin[t % 2][:, :], "oA")):
                        sp.dma_start(dst, scratch[src][rows, :]).then_inc(s_yin[t % 2], 16)
                    if t == 1:
                        sp.dma_start(wo[:, :, :], a["w_out"][0].rearrange("(k p) n -> p k n", p=P)).then_inc(S["wo"], 16)

            @block.gpsimd
            def _(gp):
                gp.tensor_tensor(bs[:, :, :], bon[:, 0, :, :], bon[:, 1, :, :], ALU.add).then_inc(S["pch"], 1)
                gp.wait_ge(S["pch"], 1)

                def bonus(t):
                    if t:
                        gp.wait_ge(S["ob"], t)
                    gp.tensor_tensor(bv[:, :].rearrange("p (h d) -> p h d", h=8),
                                     vt[:, TC + t, :].rearrange("p (h d) -> p h d", h=8),
                                     bs[:, t, :].unsqueeze(2).broadcast_to([P, 8, HD]), ALU.mult).then_inc(S["bv"], 1)

                bonus(0)
                for t in range(TL):
                    if t + 1 < TL:
                        bonus(t + 1)
                    gp.wait_ge(S["h2"], t + 1)
                    gp.dma_start(scratch["h2"][t * P:(t + 1) * P, :], h2[t % 2][:, :]).then_inc(s_st[t % 2], 16)
                for i in range(2):
                    gp.wait_ge(s_st[i], 16 * TL // 2)

            @block.tensor
            def _(pe):
                for n in range(8):
                    pe.wait_ge(S["diag"], n + 1)
                    if n >= 2:
                        pe.wait_ge(S["row"], n - 1)
                    pe.matmul(psY[:, n % 2, :], ones, diag[n % 2][:, :, :].rearrange("p a b -> p (a b)"),
                              start=True, stop=True).then_inc(S["rps"], 1)
                pe.wait_ge(S["par"], 16 * NPAR)

                def turn(t):
                    if t:
                        pe.wait_ge(S["ob"], t)
                    pe.matmul(psA[:, :], sgb[:, CTX + t * P:CTX + (t + 1) * P], og[:, :], start=True,
                              stop=True).then_inc(S["gate"], 1)
                    pe.wait_ge(s_yin[t % 2], 48 * (t // 2 + 1))
                    if t:
                        pe.wait_ge(S["oT"], t)
                    for k in range(4):
                        pe.transpose(psO[:, k, :], oin[t % 2][:, k * P:(k + 1) * P], ident)
                    pe.wait_ge(S["ob"], t + 1)
                    for k in range(4):
                        last = pe.transpose(psO[:, 4 + k, :], yin[t % 2][:, 0, k * P:(k + 1) * P], ident)
                    last.then_inc(S["tr"], 1)

                def project(t):
                    pe.wait_ge(S["oT"], t + 1)
                    if t == 0:
                        pe.wait_ge(S["wo"], 16)
                        pe.wait_ge(S["row"], 8)
                    else:
                        pe.wait_ge(S["x1a"], t)
                    for n in range(2):
                        for k in range(KT):
                            last = pe.matmul(psY[:, n, :], oT[t % 2][:, k, :], wo[:, k, n * 512:(n + 1) * 512],
                                             start=(k == 0), stop=(k == KT - 1))
                    last.then_inc(S["y"], 1)

                def route(t):
                    pe.wait_ge(S["h2"], t + 1)
                    if t:
                        pe.wait_ge(S["h2T"], t)
                    for k in range(KT):
                        last = pe.transpose(psH[:, k, :], h2[t % 2][:, k * P:(k + 1) * P], ident)
                    last.then_inc(S["tr2"], 1)
                    pe.wait_ge(S["h2T"], t + 1)
                    if t:
                        pe.wait_ge(S["lge"], t)
                    for k in range(KT):
                        last = pe.matmul(psL[:, :], h2T[:, k, :], wrt[:, k, :], start=(k == 0), stop=(k == KT - 1))
                    last.then_inc(S["lg"], 1)

                turn(0)
                for t in range(TL):
                    if t + 1 < TL:
                        turn(t + 1)
                    project(t)
                    if t:
                        route(t - 1)
                route(TL - 1)

            @block.scalar
            def _(act):
                for n in range(8):
                    act.wait_ge(S["rps"], n + 1)
                    dst = (g1row, r2row, s2row, g2row)[n // 2]
                    act.activation(dst[:, (n % 2) * 512:(n % 2) * 512 + 512], psY[:, n % 2, :], ACT.Copy).then_inc(S["row"], 1)

                def pre(t):
                    act.wait_ge(S["var1"], t + 1)
                    act.activation(st6[:, 2, :], st6[:, 1, :], ACT.Sqrt, scale=1.0 / HD, bias=eps[:, 2:3]).then_inc(S["std1"], 1)
                    act.wait_ge(S["tr"], t + 1)
                    act.activation(oT[t % 2][:, :, :], psO[:, :, :], ACT.Copy).then_inc(S["oT"], 1)

                def post(t):
                    act.wait_ge(S["y"], t + 1)
                    act.activation(sqj6[:, :], psY[:, :, :].rearrange("p a b -> p (a b)"), ACT.Square,
                                   accum_out=rs6[:, t, 0:1]).then_inc(S["sqa"], 1)
                    act.wait_ge(S["sqa"], 2 * t + 1)
                    act.activation(rs6[:, t, 1:2], rs6[:, t, 0:1], ACT.Sqrt, scale=1.0 / D, bias=eps[:, 0:1]).then_inc(S["std2"], 1)
                    act.wait_ge(S["x1"], t + 1)
                    act.activation(sqj6[:, :], x1[:, t, :], ACT.Square, accum_out=rs6[:, t, 3:4]).then_inc(S["sqa"], 1)
                    act.wait_ge(S["sqa"], 2 * t + 2)
                    act.activation(rs6[:, t, 4:5], rs6[:, t, 3:4], ACT.Sqrt, scale=1.0 / D, bias=eps[:, 0:1]).then_inc(S["std3"], 1)

                def feat(t):
                    act.wait_ge(S["tr2"], t + 1)
                    if t:
                        act.wait_ge(S["lg"], t)
                    act.activation(h2T[:, :, :], psH[:, :, :], ACT.Copy).then_inc(S["h2T"], 1)

                pre(0)
                for t in range(TL):
                    if t + 1 < TL:
                        pre(t + 1)
                    post(t)
                    if t:
                        feat(t - 1)
                feat(TL - 1)

            @block.vector
            def _(dve):
                ch = Chain(dve, S["ch"])
                dve.tensor_tensor(g1c[:, :], mod[:, GT1:GT1 + KT, 0], vec1[:, 56:64], ALU.mult)
                dve.tensor_tensor(g2c[:, :], mod[:, GT2:GT2 + KT, 0], vec1[:, 72:80], ALU.mult)
                ch.link(dve.scalar_tensor_tensor(out=r2c[:, :], in0=mod[:, SC2:SC2 + KT, 0], scalar=1.0, in1=vec1[:, 64:72],
                                                 op0=ALU.add, op1=ALU.mult))
                for n in range(8):
                    if n >= 2:
                        dve.wait_ge(S["rps"], n - 1)
                    for i in range(4):
                        k = 4 * (n % 2) + i
                        v = (g1c[:, k:k + 1], r2c[:, k:k + 1], mod[:, SH2 + k, 0:1], g2c[:, k:k + 1])[n // 2]
                        last = dve.tensor_scalar(diag[n % 2][:, i, :], ident, v, None, ALU.mult)
                    last.then_inc(S["diag"], 1)
                dve.wait_ge(S["par"], 16 * NPAR)

                def heads(ap):
                    return ap.rearrange("p (h d) -> p h d", h=8)

                def over(ap):
                    return ap.unsqueeze(2).broadcast_to([P, 8, HD])

                def pre(t):
                    y = yin[t % 2][:, 0, :]
                    dve.wait_ge(s_yin[t % 2], 48 * (t // 2 + 1))
                    ch.link(dve.tensor_tensor(y, y, yin[t % 2][:, 1, :], ALU.add))
                    ch.link(dve.reduce_sum(st6[:, 0, :], heads(y), AX.X))
                    ch.link(dve.tensor_scalar(st6[:, 0, :], st6[:, 0, :], 1.0 / HD, None, ALU.mult))
                    ch.link(dve.tensor_tensor(heads(y), heads(y), over(st6[:, 0, :]), ALU.subtract))
                    ch.link(dve.tensor_tensor(sq6[:, :], y, y, ALU.mult))
                    dve.reduce_sum(st6[:, 1, :], heads(sq6[:, :]), AX.X).then_inc(S["var1"], 1)
                    dve.wait_ge(S["std1"], t + 1)
                    ch.link(dve.reciprocal(st6[:, 3, :], st6[:, 2, :]))
                    ch.link(dve.tensor_tensor(heads(y), heads(y), over(st6[:, 3, :]), ALU.mult))
                    ch.link(dve.tensor_tensor(y, y, lnx[:, 0, :], ALU.mult))
                    ch.link(dve.tensor_tensor(y, y, lnx[:, 1, :], ALU.add))
                    dve.wait_ge(S["bv"], t + 1)
                    ch.link(dve.tensor_tensor(y, y, bv[:, :], ALU.add))
                    dve.wait_ge(S["gate"], t + 1)
                    dve.tensor_tensor(y, y, psA[:, :], ALU.mult).then_inc(S["ob"], 1)

                def post(t):
                    dve.wait_ge(S["std2"], t + 1)
                    ch.link(dve.reciprocal(rs6[:, t, 2:3], rs6[:, t, 1:2]))
                    if t >= 2:
                        dve.wait_ge(S["tr2"], t - 1)
                        dve.wait_ge(s_st[t % 2], 16 * (t // 2))
                    dve.scalar_tensor_tensor(out=h2[t % 2][:, :], in0=psY[:, :, :].rearrange("p a b -> p (a b)"),
                                             scalar=rs6[:, t, 2:3], in1=g1row[:, :], op0=ALU.mult,
                                             op1=ALU.mult).then_inc(S["x1a"], 1)
                    dve.wait_ge(S["x1a"], t + 1)
                    if t == 0:
                        dve.wait_ge(s_xin, 16)
                    dve.tensor_tensor(x1[:, t, :], x1[:, t, :], h2[t % 2][:, :], ALU.add).then_inc(S["x1"], 1)
                    dve.wait_ge(S["std3"], t + 1)
                    ch.link(dve.reciprocal(rs6[:, t, 5:6], rs6[:, t, 4:5]))
                    ch.link(dve.scalar_tensor_tensor(out=h2[t % 2][:, :], in0=x1[:, t, :], scalar=rs6[:, t, 5:6],
                                                     in1=r2row[:, :], op0=ALU.mult, op1=ALU.mult))
                    dve.tensor_tensor(h2[t % 2][:, :], h2[t % 2][:, :], s2row[:, :], ALU.add).then_inc(S["h2"], 1)

                def logits(t):
                    dve.wait_ge(S["lg"], t + 1)
                    dve.tensor_tensor(logit[:, t, :], psL[:, :], brt[:, :], ALU.add).then_inc(S["lge"], 1)

                pre(0)
                for t in range(TL):
                    if t + 1 < TL:
                        pre(t + 1)
                    post(t)
                    if t:
                        logits(t - 1)
                logits(TL - 1)

        NT = NE + NOVER
        pairw = sb(top, "pairw", [P, 2, TL])
        idxg = sb(top, "idxg", [P, NT], U32)
        idxs = sb(top, "idxs", [P, NT], U32)
        over = sb(top, "over", [1, NOVER + 1], I32)
        with ExitStack() as c7:
            def t7(name, shape, dt=F32):
                return sb(c7, "r_" + name, shape, dt)

            k7 = t7("k7", [P, CONSTS.shape[1] - CAT["slotrow"][0]])
            slotrow, part, erow, tilerow = (const(k7, n, "slotrow") for n in ("slotrow", "partition", "erow", "tilerow"))
            gm, gs, gsm, gex, gsum = t7("gm", [P, TL]), t7("gs", [P, TL, NG]), t7("gsm", [P, TL]), t7("gex", [P, TL, NG]), t7("gsum", [P, TL])
            goh = t7("goh", [P, TL, NG])
            down = t7("down", [P, EPG])
            pick = t7("pick", [P, TL, NG, EPG])
            sel = t7("sel", [P, TL, EPG])
            em_ = t7("em", [P, 2, TL])
            sc, scm = t7("sc", [P, TL, EPG]), t7("scm", [P, TL])
            eoh = t7("eoh", [P, 2, TL, EPG])
            ohk = t7("ohk", [P, 2, TL, NE])
            oh = t7("oh", [P, TL, NE])
            rank = t7("rank", [P, TL, NE])
            tmp = t7("tmp", [P, 2, TL, NE])
            cnt, ov, ovi, ovb = (t7(n, [P, NE]) for n in ("cnt", "ov", "ovi", "ovb"))
            rk_, q_, sl, eid, bs_, til, any_, pid = (t7(n, [P, 2, TL]) for n in ("rk", "q", "sl", "eid", "bs", "til", "any", "pid"))
            asl = [t7(f"asl{i}", [P, P]) for i in range(2)]
            btl = [t7(f"btl{i}", [P, NT]) for i in range(2)]
            lst, pad, tok = (t7(n, [P, NT]) for n in ("lst", "pad", "tok"))
            ovt, ovt2 = t7("ovt", [1, NOVER, NE]), t7("ovt2", [1, NOVER, NE])
            ovid = t7("ovid", [1, NOVER + 1])
            psR = pb(c7, "ps7R", [P, TL, NE])
            psC = pb(c7, "ps7C", [P, NE])
            psP = pb(c7, "ps7P", [P, NT])
            s_k7, s_ch, s_ex, s_exd, s_oh, s_rk, s_ab, s_pp = (sem(c7, "s7_" + n) for n in ("k7", "ch", "ex", "exd", "oh", "rk", "ab", "pp"))
            block = c7.enter_context(nc.Block())

            @block.sync
            def _(sp):
                sp.dma_start(k7[:, :], a["consts"][:, CAT["slotrow"][0]:]).then_inc(s_k7, 16)

            @block.scalar
            def _(act):
                act.wait_ge(s_ex, 1)
                act.activation(gex[:, :, :], gex[:, :, :], ACT.Exp).then_inc(s_exd, 1)
                act.wait_ge(s_ex, 2)
                act.activation(em_[:, 1, :], em_[:, 1, :], ACT.Exp).then_inc(s_exd, 1)

            @block.tensor
            def _(pe):
                pe.wait_ge(s_oh, 1)
                tri0 = const(cst, "tri")[:, 0:P]
                for t in range(TL):
                    pe.matmul(psR[:, t, :], tri0, oh[:, t, :], start=True, stop=(t == 0))
                    for s in range(t):
                        pe.matmul(psR[:, t, :], ones, oh[:, s, :], start=False, stop=(s == t - 1))
                for t in range(TL):
                    last = pe.matmul(psC[:, :], ones, oh[:, t, :], start=(t == 0), stop=(t == TL - 1))
                last.then_inc(s_rk, 1)
                for n in range(2 * TL):
                    pe.wait_ge(s_ab, n + 1)
                    pe.matmul(psP[:, :], asl[n % 2][:, :], btl[n % 2][:, :], start=(n == 0),
                              stop=(n == 2 * TL - 1)).then_inc(s_pp, 1)

            @block.vector
            def _(dve):
                ch = Chain(dve, s_ch)
                dve.wait_ge(s_k7, 16)

                def spread(ap, shape, axis):
                    return ap.unsqueeze(axis).broadcast_to(shape)

                def first_max(dst, src, best, score, smax, n):
                    w = [P, TL, n]
                    ch.link(dve.tensor_reduce(best, src, AX.X, ALU.max))
                    ch.link(dve.tensor_tensor(score, src, spread(best, w, 2), ALU.is_equal))
                    ch.link(dve.tensor_tensor(score, score, spread(down[:, 0:n] if n == EPG else down[:, 4:8], w, 1), ALU.mult))
                    ch.link(dve.tensor_reduce(smax, score, AX.X, ALU.max))
                    ch.link(dve.tensor_tensor(dst, score, spread(smax, w, 2), ALU.is_equal))

                ch.link(dve.tensor_scalar(down[:, :], erow[:, 0:EPG], -1.0, float(EPG), ALU.mult, ALU.add))
                lg = logit[:, :, 0:NG]
                first_max(goh[:, :, :], lg, gm[:, :], gs[:, :, :], gsm[:, :], NG)
                dve.tensor_tensor(gex[:, :, :], lg, spread(gm[:, :], [P, TL, NG], 2), ALU.subtract).then_inc(s_ex, 1)
                le = logit[:, :, NG:].rearrange("p t (g e) -> p t g e", g=NG)
                ch.link(dve.tensor_tensor(pick[:, :, :, :], le, spread(goh[:, :, :], [P, TL, NG, EPG], 3), ALU.mult))
                ch.link(dve.tensor_reduce(sel[:, :, :], pick[:, :, :, :].rearrange("p t g e -> p t e g"), AX.X, ALU.add))
                first_max(eoh[:, 0, :, :], sel[:, :, :], em_[:, 0, :], sc[:, :, :], scm[:, :], EPG)
                ch.link(dve.scalar_tensor_tensor(out=sel[:, :, :], in0=eoh[:, 0, :, :], scalar=-1e30, in1=sel[:, :, :],
                                                 op0=ALU.mult, op1=ALU.add))
                first_max(eoh[:, 1, :, :], sel[:, :, :], em_[:, 1, :], sc[:, :, :], scm[:, :], EPG)
                ch.link(dve.tensor_tensor(em_[:, 1, :], em_[:, 1, :], em_[:, 0, :], ALU.subtract))
                dve.tensor_copy(em_[:, 0, :], em_[:, 0, :]).then_inc(s_ex, 1)
                for k in range(2):
                    last = dve.tensor_tensor(ohk[:, k, :, :].rearrange("p t (g e) -> p t g e", g=NG),
                                             spread(goh[:, :, :], [P, TL, NG, EPG], 3),
                                             spread(eoh[:, k, :, :], [P, TL, NG, EPG], 2), ALU.mult)
                ch.link(last)
                dve.tensor_tensor(oh[:, :, :], ohk[:, 0, :, :], ohk[:, 1, :, :], ALU.add).then_inc(s_oh, 1)
                dve.wait_ge(s_exd, 2)
                ch.link(dve.tensor_reduce(gsum[:, :], gex[:, :, :], AX.X, ALU.add))
                ch.link(dve.tensor_scalar(gm[:, :], em_[:, 1, :], 1.0, None, ALU.add))
                ch.link(dve.tensor_tensor(gsum[:, :], gsum[:, :], gm[:, :], ALU.mult))
                ch.link(dve.reciprocal(pairw[:, 0, :], gsum[:, :]))
                ch.link(dve.tensor_tensor(pairw[:, 1, :], pairw[:, 0, :], em_[:, 1, :], ALU.mult))
                dve.wait_ge(s_rk, 1)
                dve.tensor_copy(rank[:, :, :], psR[:, :, :])
                ch.link(dve.tensor_copy(cnt[:, :], psC[:, :]))

                def chosen(dst, src):
                    ch.link(dve.tensor_tensor(tmp[:, :, :, :], ohk[:, :, :, :], src, ALU.mult))
                    ch.link(dve.tensor_reduce(dst, tmp[:, :, :, :], AX.X, ALU.add))

                full = [P, 2, TL, NE]
                chosen(rk_[:, :, :], spread(rank[:, :, :], full, 1))
                ch.link(dve.tensor_scalar(q_[:, :, :], rk_[:, :, :], float(CAP), None, ALU.is_ge))
                ch.link(dve.tensor_scalar(ov[:, :], cnt[:, :], float(CAP), None, ALU.is_gt))
                for j in range(2, (SEQ + CAP - 1) // CAP):
                    dve.scalar_tensor_tensor(out=q_[:, :, :], in0=rk_[:, :, :], scalar=float(CAP * j), in1=q_[:, :, :],
                                             op0=ALU.is_ge, op1=ALU.add)
                    ch.link(dve.scalar_tensor_tensor(out=ov[:, :], in0=cnt[:, :], scalar=float(CAP * j), in1=ov[:, :],
                                                     op0=ALU.is_gt, op1=ALU.add))
                ch.link(dve.scalar_tensor_tensor(out=sl[:, :, :], in0=q_[:, :, :], scalar=-float(CAP), in1=rk_[:, :, :],
                                                 op0=ALU.mult, op1=ALU.add))
                ch.link(dve.tensor_tensor_scan(ovi[:, :], ones[:, 0:NE], ov[:, :], 0.0, ALU.mult, ALU.add))
                ch.link(dve.tensor_tensor(ovb[:, :], ovi[:, :], ov[:, :], ALU.subtract))
                chosen(bs_[:, :, :], ovb[:, :].unsqueeze(1).unsqueeze(1).broadcast_to(full))
                chosen(eid[:, :, :], erow.unsqueeze(1).unsqueeze(1).broadcast_to(full))
                dve.tensor_scalar(any_[:, :, :], q_[:, :, :], 1.0, None, ALU.is_ge)
                ch.link(dve.tensor_tensor(til[:, :, :], bs_[:, :, :], q_[:, :, :], ALU.add))
                ch.link(dve.scalar_tensor_tensor(out=til[:, :, :], in0=til[:, :, :], scalar=float(NE - 1), in1=eid[:, :, :],
                                                 op0=ALU.add, op1=ALU.subtract))
                ch.link(dve.tensor_tensor(til[:, :, :], til[:, :, :], any_[:, :, :], ALU.mult))
                ch.link(dve.tensor_tensor(til[:, :, :], til[:, :, :], eid[:, :, :], ALU.add))
                for k in range(2):
                    for t in range(TL):
                        last = dve.tensor_scalar(pid[:, k, t:t + 1], part, float(k * SEQ + t * P + 1), None, ALU.add)
                ch.link(last)
                for n in range(2 * TL):
                    k, t = n // TL, n % TL
                    if n >= 2:
                        dve.wait_ge(s_pp, n - 1)
                    dve.tensor_scalar(asl[n % 2][:, :], slotrow, sl[:, k, t:t + 1], None, ALU.is_equal)
                    dve.tensor_scalar(btl[n % 2][:, :], tilerow, til[:, k, t:t + 1], pid[:, k, t:t + 1],
                                      ALU.is_equal, ALU.mult).then_inc(s_ab, 1)
                dve.wait_ge(s_pp, 2 * TL)
                ch.link(dve.tensor_copy(lst[:, :], psP[:, :]))
                ch.link(dve.tensor_scalar(pad[:, :], lst[:, :], 0.0, float(4 * SEQ + 1), ALU.is_equal, ALU.mult))
                ch.link(dve.scalar_tensor_tensor(out=lst[:, :], in0=lst[:, :], scalar=-1.0, in1=pad[:, :], op0=ALU.add, op1=ALU.add))
                ch.link(dve.tensor_scalar(pad[:, :], lst[:, :], float(SEQ), float(-SEQ), ALU.is_ge, ALU.mult))
                ch.link(dve.tensor_tensor(tok[:, :], lst[:, :], pad[:, :], ALU.add))
                dve.tensor_copy(idxs[:, :], lst[:, :])
                ch.link(dve.tensor_copy(idxg[:, :], tok[:, :]))
                w = [1, NOVER, NE]
                jrow = tilerow[0:1, 0:NOVER].unsqueeze(2).broadcast_to(w)
                dve.tensor_tensor(ovt[:, :, :], jrow, ovb[0:1, :].unsqueeze(1).broadcast_to(w), ALU.is_ge)
                ch.link(dve.tensor_tensor(ovt2[:, :, :], jrow, ovi[0:1, :].unsqueeze(1).broadcast_to(w), ALU.is_lt))
                ch.link(dve.tensor_tensor(ovt[:, :, :], ovt[:, :, :], ovt2[:, :, :], ALU.mult))
                ch.link(dve.tensor_tensor(ovt[:, :, :], ovt[:, :, :], erow[0:1, :].unsqueeze(1).broadcast_to(w), ALU.mult))
                dve.tensor_copy(ovid[:, NOVER:], ovi[0:1, NE - 1:NE])
                ch.link(dve.tensor_reduce(ovid[:, 0:NOVER], ovt[:, :, :], AX.X, ALU.add))
                ch.link(dve.tensor_copy(over[:, :], ovid[:, :]))

        with ExitStack() as c8:
            R = 4
            wgu = [sb(c8, f"wgu{i}", [P, 2, KT, DE]) for i in range(R)]
            wd = [sb(c8, f"wd{i}", [P, 2, D]) for i in range(R)]
            hg = [sb(c8, f"hg{i}", [P, D]) for i in range(R)]
            hgT = [sb(c8, f"hgT{i}", [P, KT, P]) for i in range(2)]
            sgt = sb(c8, "sgt", [P, DE])
            hid = [sb(c8, f"hid{i}", [P, DE]) for i in range(2)]
            hidT = [sb(c8, f"hidT{i}", [P, 2, P]) for i in range(2)]
            yo = [sb(c8, f"yo{i}", [P, D]) for i in range(2)]
            ig, is_ = ([sb(c8, f"{n}{i}", [P, 1], U32) for i in range(R)] for n in ("ig", "is"))
            psT = pb(c8, "ps8T", [P, KT, P])
            psG = [pb(c8, f"ps8G{i}", [P, 2, DE]) for i in range(2)]
            psH = pb(c8, "ps8H", [P, 2, P])
            psY = pb(c8, "ps8Y", [P, 2, 512])
            S = {n: sem(c8, f"s8_{n}") for n in (
                "zero", "tr", "hgT", "gu", "sil", "hid", "trh", "hidT", "dn", "ya", "yv", "gate", "pg", "ps")}
            s_w = [sem(c8, f"s8_w{i}") for i in range(R)]
            s_wd = [sem(c8, f"s8_wd{i}") for i in range(R)]
            s_hg = [sem(c8, f"s8_hg{i}") for i in range(R)]
            s_sc = [sem(c8, f"s8_sc{i}") for i in range(2)]
            tiles = ExitStack()
            block = tiles.enter_context(nc.Block())
            EP = NE // R
            weights = {n: a[n].rearrange("l e r n -> (l e r) n") for n in ("w_gate", "w_up", "w_down")}

            def rows_of(name, e, per):
                r = D if per == KT else DE
                return weights[name][bass.ds(e * r, r), :].rearrange("(p k) n -> p k n", k=per)

            @block.sync
            def _(sp):
                def load(i, first):
                    for b in range(R):
                        e = R * i + b
                        if not first:
                            sp.wait_ge(S["gu"], e - R + 1)
                        sp.dma_start(wgu[b][:, 0, :, :], rows_of("w_gate", e, KT)).then_inc(s_w[b], 16)
                        sp.dma_start(wgu[b][:, 1, :, :], rows_of("w_up", e, KT)).then_inc(s_w[b], 16)
                        if not first:
                            sp.wait_ge(S["dn"], e - R + 1)
                        sp.dma_start(wd[b][:, :, :], rows_of("w_down", e, 2)).then_inc(s_wd[b], 16)

                passes(sp, EP, load)

            @block.gpsimd
            def _(gp):
                for b in range(R):
                    gp.memset(hg[b][:, :], 0.0).then_inc(S["zero"], 1)
                gp.wait_ge(S["zero"], R)

                def gather(e, b, first):
                    if not first:
                        gp.wait_ge(S["tr"], e - R + 1)
                        gp.sem_inc(S["gate"], 1)
                    gp.tensor_copy(ig[b][:, :], idxg[:, bass.ds(e, 1)]).then_inc(S["pg"], 1)
                    gp.wait_ge(S["pg"], e + 1)
                    gp.sem_inc(S["gate"], 1)
                    gp.indirect_dma_start(out=hg[b][:, :], out_offset=None, in_=scratch["h2"][:, :],
                                          in_offset=bass.IndirectOffsetOnAxis(ap=ig[b][:, 0:1], axis=0),
                                          bounds_check=SEQ - 1, oob_is_err=False).then_inc(s_hg[b], 16)

                def scatter(i, b, first):
                    e = R * i + b
                    gp.wait_ge(S["ya"], e + 1)
                    gp.wait_ge(S["yv"], e + 1)
                    if not (first and b < 2):
                        gp.wait_ge(s_sc[b % 2], 16 * (R // 2 * i + b // 2))
                    gp.sem_inc(S["gate"], 1)
                    gp.tensor_copy(is_[b % 2][:, :], idxs[:, bass.ds(e, 1)]).then_inc(S["ps"], 1)
                    gp.wait_ge(S["ps"], e + 1)
                    gp.sem_inc(S["gate"], 1)
                    gp.indirect_dma_start(out=scratch["ypair"][:, :],
                                          out_offset=bass.IndirectOffsetOnAxis(ap=is_[b % 2][:, 0:1], axis=0),
                                          in_=yo[b % 2][:, :], in_offset=None, bounds_check=2 * SEQ - 1,
                                          oob_is_err=False).then_inc(s_sc[b % 2], 16)

                for b in range(R - 1):
                    gather(b, b, True)

                def ring(i, first, last):
                    for b in range(R):
                        if not (last and b):
                            gather(R * i + b + R - 1, (b + R - 1) % R, first and b == 0)
                        scatter(i, b, first)

                ends(gp, EP, ring)
                for b in range(2):
                    gp.wait_ge(s_sc[b], 8 * NE)

            @block.tensor
            def _(pe):
                def turn(i, b, first):
                    e = R * i + b
                    pe.wait_ge(s_hg[b], 16 * (i + 1))
                    if not (first and b == 0):
                        pe.wait_ge(S["hgT"], e)
                    for k in range(KT):
                        last = pe.transpose(psT[:, k, :], hg[b][:, k::KT], ident)
                    last.then_inc(S["tr"], 1)

                def down(i, b, first):
                    e = R * i + b
                    pe.wait_ge(S["hidT"], e + 1)
                    pe.wait_ge(s_wd[b], 16 * (i + 1))
                    if not (first and b == 0):
                        pe.wait_ge(S["ya"], e)
                        pe.wait_ge(S["yv"], e)
                    for n in range(2):
                        for f in range(2):
                            last = pe.matmul(psY[:, n, :], hidT[b % 2][:, f, :], wd[b][:, f, n * 512:(n + 1) * 512],
                                             start=(f == 0), stop=(f == 1))
                    last.then_inc(S["dn"], 1)

                def ring(i, first, last_pass):
                    for b in range(R):
                        e = R * i + b
                        pe.wait_ge(S["hgT"], e + 1)
                        pe.wait_ge(s_w[b], 32 * (i + 1))
                        if not (first and b < 2):
                            pe.wait_ge(S["hid"], e - 1)
                        for k in range(KT):
                            last = pe.matmul(psG[b % 2][:, :, :], hgT[b % 2][:, k, :], wgu[b][:, :, k, :],
                                             start=(k == 0), stop=(k == KT - 1))
                        last.then_inc(S["gu"], 1)
                        if b:
                            down(i, b - 1, first)
                        elif not first:
                            down(i - 1, R - 1, False)
                        if b < R - 1:
                            turn(i, b + 1, first)
                        elif not last_pass:
                            turn(i + 1, 0, False)
                        pe.wait_ge(S["hid"], e + 1)
                        if not (first and b == 0):
                            pe.wait_ge(S["hidT"], e)
                        for f in range(2):
                            last = pe.transpose(psH[:, f, :], hid[b % 2][:, f::2], ident)
                        last.then_inc(S["trh"], 1)

                turn(0, 0, True)
                ends(pe, EP, ring)
                down(EP - 1, R - 1, False)

            @block.scalar
            def _(act):
                def feat(i, b):
                    act.wait_ge(S["tr"], R * i + b + 1)
                    if not (isinstance(i, int) and i == 0 and b < 2):
                        act.wait_ge(S["gu"], R * i + b - 1)
                    act.activation(hgT[b % 2][:, :, :], psT[:, :, :], ACT.Copy).then_inc(S["hgT"], 1)

                def y_out(i, b, first):
                    act.wait_ge(S["dn"], R * i + b + 1)
                    if not (first and b < 2):
                        act.wait_ge(s_sc[b % 2], 16 * (R // 2 * i + b // 2))
                    act.activation(yo[b % 2][:, 0:512], psY[:, 0, :], ACT.Copy).then_inc(S["ya"], 1)

                def ring(i, first, last):
                    for b in range(R):
                        e = R * i + b
                        act.wait_ge(S["gu"], e + 1)
                        if not (first and b == 0):
                            act.wait_ge(S["hid"], e)
                        act.activation(sgt[:, :], psG[b % 2][:, 0, :], ACT.Silu).then_inc(S["sil"], 1)
                        if b:
                            y_out(i, b - 1, first)
                        elif not first:
                            y_out(i - 1, R - 1, False)
                        if b < R - 1:
                            feat(i, b + 1)
                        elif not last:
                            feat(i + 1, 0)

                feat(0, 0)
                ends(act, EP, ring, lead=1)
                y_out(EP - 1, R - 1, False)

            @block.vector
            def _(dve):
                def y_out(i, b, first):
                    dve.wait_ge(S["dn"], R * i + b + 1)
                    if not (first and b < 2):
                        dve.wait_ge(s_sc[b % 2], 16 * (R // 2 * i + b // 2))
                    dve.tensor_copy(yo[b % 2][:, 512:], psY[:, 1, :]).then_inc(S["yv"], 1)

                def ring(i, first, last):
                    for b in range(R):
                        e = R * i + b
                        dve.wait_ge(S["sil"], e + 1)
                        if not (first and b < 2):
                            dve.wait_ge(S["trh"], e - 1)
                        dve.tensor_tensor(hid[b % 2][:, :], sgt[:, :], psG[b % 2][:, 1, :], ALU.mult).then_inc(S["hid"], 1)
                        if b:
                            y_out(i, b - 1, first)
                        elif not first:
                            y_out(i - 1, R - 1, False)
                        dve.wait_ge(S["trh"], e + 1)
                        if not (first and b < 2):
                            dve.wait_ge(S["dn"], e - 1)
                        dve.tensor_copy(hidT[b % 2][:, :, :], psH[:, :, :]).then_inc(S["hidT"], 1)

                ends(dve, EP, ring, lead=1)
                y_out(EP - 1, R - 1, False)

            tiles.close()
            S = {n: sem(c8, f"s9_{n}") for n in (
                "tr", "hgT", "gu", "sil", "hid", "trh", "hidT", "dn", "ya", "yv", "fin", "gate", "w", "hg", "sc", "pg")}
            block = c8.enter_context(nc.Block())

            def overflow(eng, body):
                count = eng.value_load(over[0:1, NOVER:NOVER + 1], min_val=0, max_val=NOVER)
                with eng.Fori(0, NOVER) as j:
                    with eng.If(j < count):
                        body(j)

            @block.sync
            def _(sp):
                def load(j):
                    sp.wait_ge(S["fin"], j + 1)
                    e = sp.value_load(over[0:1, bass.ds(j, 1)], min_val=0, max_val=NE - 1)
                    sp.dma_start(wgu[0][:, 0, :, :], rows_of("w_gate", e, KT)).then_inc(S["w"], 16)
                    sp.dma_start(wgu[0][:, 1, :, :], rows_of("w_up", e, KT)).then_inc(S["w"], 16)
                    sp.dma_start(wd[0][:, :, :], rows_of("w_down", e, 2)).then_inc(S["w"], 16)

                overflow(sp, load)

            @block.gpsimd
            def _(gp):
                gp.sem_inc(S["fin"], 1)

                def tile(j):
                    gp.tensor_copy(ig[0][:, :], idxg[:, bass.ds(j + NE, 1)])
                    gp.tensor_copy(is_[0][:, :], idxs[:, bass.ds(j + NE, 1)]).then_inc(S["pg"], 1)
                    gp.wait_ge(S["pg"], j + 1)
                    gp.sem_inc(S["gate"], 1)
                    gp.indirect_dma_start(out=hg[0][:, :], out_offset=None, in_=scratch["h2"][:, :],
                                          in_offset=bass.IndirectOffsetOnAxis(ap=ig[0][:, 0:1], axis=0),
                                          bounds_check=SEQ - 1, oob_is_err=False).then_inc(S["hg"], 16)
                    gp.wait_ge(S["ya"], j + 1)
                    gp.wait_ge(S["yv"], j + 1)
                    gp.sem_inc(S["gate"], 1)
                    gp.indirect_dma_start(out=scratch["ypair"][:, :],
                                          out_offset=bass.IndirectOffsetOnAxis(ap=is_[0][:, 0:1], axis=0),
                                          in_=yo[0][:, :], in_offset=None, bounds_check=2 * SEQ - 1,
                                          oob_is_err=False).then_inc(S["sc"], 16)
                    gp.wait_ge(S["sc"], 16 * (j + 1))
                    gp.sem_inc(S["fin"], 1)

                overflow(gp, tile)

            @block.tensor
            def _(pe):
                def tile(j):
                    pe.wait_ge(S["hg"], 16 * (j + 1))
                    for k in range(KT):
                        last = pe.transpose(psT[:, k, :], hg[0][:, k::KT], ident)
                    last.then_inc(S["tr"], 1)
                    pe.wait_ge(S["hgT"], j + 1)
                    pe.wait_ge(S["w"], 48 * (j + 1))
                    for k in range(KT):
                        last = pe.matmul(psG[0][:, :, :], hgT[0][:, k, :], wgu[0][:, :, k, :],
                                         start=(k == 0), stop=(k == KT - 1))
                    last.then_inc(S["gu"], 1)
                    pe.wait_ge(S["hid"], j + 1)
                    for f in range(2):
                        last = pe.transpose(psH[:, f, :], hid[0][:, f::2], ident)
                    last.then_inc(S["trh"], 1)
                    pe.wait_ge(S["hidT"], j + 1)
                    for n in range(2):
                        for f in range(2):
                            last = pe.matmul(psY[:, n, :], hidT[0][:, f, :], wd[0][:, f, n * 512:(n + 1) * 512],
                                             start=(f == 0), stop=(f == 1))
                    last.then_inc(S["dn"], 1)

                overflow(pe, tile)

            @block.scalar
            def _(act):
                def tile(j):
                    act.wait_ge(S["tr"], j + 1)
                    act.activation(hgT[0][:, :, :], psT[:, :, :], ACT.Copy).then_inc(S["hgT"], 1)
                    act.wait_ge(S["gu"], j + 1)
                    act.activation(sgt[:, :], psG[0][:, 0, :], ACT.Silu).then_inc(S["sil"], 1)
                    act.wait_ge(S["dn"], j + 1)
                    act.activation(yo[0][:, 0:512], psY[:, 0, :], ACT.Copy).then_inc(S["ya"], 1)

                overflow(act, tile)

            @block.vector
            def _(dve):
                def tile(j):
                    dve.wait_ge(S["sil"], j + 1)
                    dve.tensor_tensor(hid[0][:, :], sgt[:, :], psG[0][:, 1, :], ALU.mult).then_inc(S["hid"], 1)
                    dve.wait_ge(S["trh"], j + 1)
                    dve.tensor_copy(hidT[0][:, :, :], psH[:, :, :]).then_inc(S["hidT"], 1)
                    dve.wait_ge(S["dn"], j + 1)
                    dve.tensor_copy(yo[0][:, 512:], psY[:, 1, :]).then_inc(S["yv"], 1)

                overflow(dve, tile)

        with ExitStack() as c10:
            NB = 4
            yp = [sb(c10, f"yp{i}", [P, 2, D]) for i in range(NB)]
            sqj = sb(c10, "sqj10", [P, D])
            rs = sb(c10, "rs10", [P, TL, 3])
            s_in = [sem(c10, f"s10_in{i}") for i in range(NB)]
            s_sum, s_sq, s_std, s_ch, s_res, s_out = (sem(c10, "s10_" + n) for n in ("sum", "sq", "std", "ch", "res", "out"))
            block = c10.enter_context(nc.Block())

            @block.sync
            def _(sp):
                for t in range(TL):
                    if t >= NB:
                        sp.wait_ge(s_res, t - NB + 1)
                    for k in range(2):
                        o = k * SEQ + t * P
                        sp.dma_start(yp[t % NB][:, k, :], scratch["ypair"][o:o + P, :]).then_inc(s_in[t % NB], 16)

            @block.scalar
            def _(act):
                for t in range(TL):
                    act.wait_ge(s_sum, t + 1)
                    act.activation(sqj[:, :], yp[t % NB][:, 0, :], ACT.Square, accum_out=rs[:, t, 0:1]).then_inc(s_sq, 1)
                    act.wait_ge(s_sq, t + 1)
                    act.activation(rs[:, t, 1:2], rs[:, t, 0:1], ACT.Sqrt, scale=1.0 / D, bias=eps[:, 0:1]).then_inc(s_std, 1)

            @block.vector
            def _(dve):
                ch = Chain(dve, s_ch)

                def mix(t):
                    y = yp[t % NB]
                    dve.wait_ge(s_in[t % NB], 32 * (t // NB + 1))
                    ch.link(dve.tensor_scalar(y[:, 0, :], y[:, 0, :], pairw[:, 0, t:t + 1], None, ALU.mult))
                    dve.scalar_tensor_tensor(out=y[:, 0, :], in0=y[:, 1, :], scalar=pairw[:, 1, t:t + 1],
                                             in1=y[:, 0, :], op0=ALU.mult, op1=ALU.add).then_inc(s_sum, 1)

                mix(0)
                for t in range(TL):
                    if t + 1 < TL:
                        mix(t + 1)
                    y = yp[t % NB]
                    dve.wait_ge(s_std, t + 1)
                    ch.link(dve.reciprocal(rs[:, t, 2:3], rs[:, t, 1:2]))
                    ch.link(dve.scalar_tensor_tensor(out=y[:, 0, :], in0=y[:, 0, :], scalar=rs[:, t, 2:3],
                                                     in1=g2row[:, :], op0=ALU.mult, op1=ALU.mult))
                    dve.tensor_tensor(x1[:, t, :], x1[:, t, :], y[:, 0, :], ALU.add).then_inc(s_res, 1)

            @block.gpsimd
            def _(gp):
                for t in range(TL):
                    gp.wait_ge(s_res, t + 1)
                    gp.dma_start(out[0, t * P:(t + 1) * P, :], x1[:, t, :]).then_inc(s_out, 16)
                gp.wait_ge(s_out, 16 * TL)


INS = ["x", "c", "ctx", "c_ctx", "w_mod", "b_mod", "g_pre1", "g_post1", "g_pre2", "g_post2", "w_in", "conv_rkv",
       "gm_ln_g", "gm_ln_b", "w_spatial", "b_spatial", "decay_w0", "decay_up", "iclr_a0", "iclr_up", "k_k", "k_a",
       "r_k", "outgate_up", "lnx_g", "lnx_b", "w_out", "w_router_grp", "b_router_grp", "w_router_exp",
       "b_router_exp", "w_gate", "w_up", "w_down"]
SCRATCH = {"oA": (SEQ, AW), "yf": (SEQ, BW), "yb": (SEQ, BW), "h2": (SEQ, D), "ypair": (2 * SEQ, D),
           "lw": (P, NTOK), "sg": (P, NTOK)}


def kernel(**inputs):
    import concourse.bacc as bacc
    from concourse.bass_utils import run_bass_kernel_spmd

    nc = bacc.Bacc("TRN2", target_bir_lowering=False, num_devices=1)
    arrays, a = {}, {}
    for name in INS:
        v = np.ascontiguousarray(inputs[name])
        arrays[f"in_{name}"] = v
        a[name] = nc.dram_tensor(f"in_{name}", v.shape, mybir.dt.from_np(v.dtype), kind="ExternalInput").ap()
    arrays["in_consts"] = CONSTS
    a["consts"] = nc.dram_tensor("in_consts", CONSTS.shape, F32, kind="ExternalInput").ap()
    out = nc.dram_tensor("out_0", (1, SEQ, D), F32, kind="ExternalOutput").ap()
    scratch = {n: nc.dram_tensor(f"scratch_{n}", s, F32, kind="Internal").ap() for n, s in SCRATCH.items()}
    program(nc, a, out, scratch, None)
    r = run_bass_kernel_spmd(nc, [arrays], core_ids=[0])
    return r.results[0]["out_0"]
```

```python
from contextlib import ExitStack

import numpy as np
import concourse.bass as bass
from concourse import mybir

F32 = mybir.dt.float32
F32R = mybir.dt.float32r
I32 = mybir.dt.int32
U32 = mybir.dt.uint32
ACT = mybir.ActivationFunctionType
ALU = mybir.AluOpType
AX = mybir.AxisListType

P = 128
D = 1024
KT = D // P
SEQ, CTX = 1024, 256
TL, TC = SEQ // P, CTX // P
TT = TL + TC
NTOK = SEQ + CTX
GRID = 64
ROWS = SEQ // GRID
AW = 512
BW = 512
HD = 64
J = BW // P
D_IN = 3 * BW + 3 * P + 2 * AW
OFF_U = 3 * BW + 3 * P
NE, NG, EPG = 32, 4, 8
DE = 256
EPS, LN_EPS, GN_EPS = 1e-6, 1e-5, 64e-5
KAPPA = float(np.exp(-0.5))
CAP = 128
NOVER = 2 * SEQ // (CAP + 1)
LEVELS = (2, 4, 8, 16, 32, 64)
PADW = GRID + 2
ZC = CTX + 2
ZL = (ROWS + 2) * PADW
CH = P + 1


def constants():
    s = np.arange(P)[:, None]
    t = np.arange(P)[None, :]
    out, at = [], {}

    def put(name, a):
        a = np.asarray(a, np.float32).reshape(P, -1)
        at[name] = (sum(x.shape[1] for x in out), a.shape[1])
        out.append(a)

    put("ident", s == t)
    put("ones", np.ones((P, P)))
    put("headblock", (s // HD) == (t // HD))
    put("headcol", (s // HD) == np.arange(2)[None, :])
    put("tri", np.stack([t > s, t >= s, t < s, t <= s], 1))
    lev = np.zeros((P, len(LEVELS), 2, HD))
    for li, m in enumerate(LEVELS):
        for d in range(2):
            for c in range(HD):
                b = c // m
                even, odd = b * 2 * m, b * 2 * m + m
                partner = odd if d == 0 else even
                lev[partner:partner + m, li, d, c] = 1
    put("level", lev)
    pair = np.zeros((P, 2, P))
    for a in range(0, P, 2):
        pair[a, 0, a + 1] = -1
        pair[a + 1, 1, a] = -1
    pair += np.eye(P)[:, None, :]
    put("pair", pair)
    reset = np.ones((P, 2, TT, CH))
    reset[:, 0, :, 0] = 0
    reset[:, 1, :, P] = 0
    put("reset", reset)
    put("slotrow", np.broadcast_to(np.arange(P)[None], (P, P)))
    put("partition", np.arange(P)[:, None])
    put("erow", np.broadcast_to(np.arange(NE)[None], (P, NE)))
    put("tilerow", np.broadcast_to(np.arange(NE + NOVER)[None], (P, NE + NOVER)))
    return np.concatenate(out, 1), at


CONSTS, CAT = constants()


class Chain:

    def __init__(self, eng, sem):
        self.eng, self.sem, self.done, self.base, self.n = eng, sem, 0, 0, 0

    def loop(self, i, per):
        self.base, self.n, self.per = self.done + i * per, 0, per

    def leave(self, passes):
        assert self.n == self.per, (self.n, self.per)
        self.done += passes * self.per
        self.base, self.n = self.done, 0

    def link(self, ins):
        self.n += 1
        ins.then_inc(self.sem, 1)
        self.eng.wait_ge(self.sem, self.base + self.n)


def backwards(ap):
    (ps, pn), (fs, fn) = ap.ap
    return bass.AP(ap.tensor, ap.offset + fs * (fn - 1), [[ps, pn], [-fs, fn]])


def passes(eng, n, body):
    body(0, True)
    with eng.Fori(1, n) as i:
        body(i, False)


def ends(eng, n, body, lead=1):
    for i in range(lead):
        body(i, i == 0, False)
    with eng.Fori(lead, n - 1) as i:
        body(i, False, False)
    body(n - 1, False, True)


def program(nc, a, out, scratch):
    top = ExitStack()

    def sb(ctx, name, shape, dt=F32):
        return ctx.enter_context(nc.sbuf_tensor(name, shape, dt))

    def pb(ctx, name, shape, dt=F32):
        return ctx.enter_context(nc.psum_tensor(name, shape, dt))

    taken = {}

    def sem(ctx, name):
        if id(ctx) not in taken:
            taken[id(ctx)] = mine = []

            def give_back():
                nc.clear_and_free_semaphores(mine)
                nc.all_engine_barrier()
                del taken[id(ctx)]

            ctx.callback(give_back)
        taken[id(ctx)].append(nc.alloc_semaphore(name))
        return taken[id(ctx)][-1]

    def const(tile, name, first="ident"):
        o, n = CAT[name]
        o -= CAT[first][0]
        return tile[:, o:o + n]

    with top:
        cst = sb(top, "cst", [P, CAT["reset"][0]])
        ident, ones = const(cst, "ident"), const(cst, "ones")
        headblock, headcol = const(cst, "headblock"), const(cst, "headcol")
        mod = sb(top, "mod", [P, 48, 2])
        vec1 = sb(top, "vec1", [P, 80])
        convw = sb(top, "convw", [P, 9, 12])
        vec3 = sb(top, "vec3", [P, 40])
        g1 = sb(top, "g1", [P, KT, 2])
        rstd1 = sb(top, "rstd1", [P, TT])
        eps = sb(top, "eps", [P, 4])
        SH1, SC1, GT1, SH2, SC2, GT2 = (i * KT for i in range(6))

        vt_at = -(-nc.sbuf_base // 32) * 32
        vt = sb(top, "vt", [P, TT, BW])
        bon = sb(top, "bon", [P, 2, TL, 8])
        mixer = ExitStack()
        with mixer:
            kvr = sb(mixer, "kvr", [P, 12, NTOK])
            la = sb(mixer, "la", [P, NTOK])
            head = ExitStack()
            with head:
                lw = sb(head, "lw", [P, NTOK])
                sg = sb(head, "sg", [P, NTOK])
                hT_at = -(-nc.sbuf_base // 32) * 32
                hT = sb(head, "hT", [P, KT, NTOK])
                with ExitStack() as c1:
                    RING = 3
                    wm = [sb(c1, f"wm{i}", [P, KT, 512]) for i in range(RING)]
                    cc = sb(c1, "cc", [P, 2, KT])
                    cs = sb(c1, "cs", [P, 2, KT])
                    rows = sb(c1, "rows", [P, 3, P])
                    room = kvr[:, :, :].rearrange("p a b -> p (a b)")
                    xa = room[:, 0:TT * D].rearrange("p (t d) -> p t d", d=D)
                    xn = room[:, TT * D:(TT + 2) * D].rearrange("p (t d) -> p t d", d=D)
                    sqj = room[:, (TT + 2) * D:(TT + 3) * D]
                    ssq = sb(c1, "ssq", [P, 2, TT])
                    mrow = [sb(c1, f"mrow{i}", [2, 512]) for i in range(2)]
                    psM = pb(c1, "psM", [P, 48, 2])
                    psW = [pb(c1, f"psW{i}", [P, 512]) for i in range(2)]
                    psV = pb(c1, "psV", [P, 3, P])
                    psX = [pb(c1, f"psX{i}", [P, KT, P]) for i in range(2)]
                    s_cst, s_cc, s_rows = (sem(c1, n) for n in ("s_cst", "s_cc", "s_rows"))
                    s_x = [sem(c1, f"s_xin{i}") for i in range(3)]
                    s_mrow, s_mt = (sem(c1, n) for n in ("s_mrow", "s_mt"))
                    parts = ((0, 4), (4, 7), (7, TT))
                    s_wm = [sem(c1, f"s_wm{i}") for i in range(RING)]
                    s_silu, s_mm, s_vt, s_vec, s_mod, s_modps = (
                        sem(c1, n) for n in ("s_silu", "s_mm", "s_vt", "s_vec", "s_mod", "s_modps"))
                    s_ssq, s_rstd, s_xn, s_xt, s_evA, s_evV, s_eps, s_act, s_dve = (
                        sem(c1, n) for n in ("s_ssq", "s_rstd", "s_xn", "s_xt", "s_evA", "s_evV", "s_eps", "s_act", "s_dve"))
                    NM = 6 * D // 512
                    wmod = a["w_mod"][0].rearrange("(p k) n -> p k n", k=KT)
                    block = c1.enter_context(nc.Block())

                    @block.sync
                    def _(sp):
                        sp.dma_start(cst[:, :], a["consts"][:, 0:CAT["reset"][0]]).then_inc(s_cst, 16)
                        sp.dma_start(cc[:, 0, :], a["c"].rearrange("a (p k) -> p (a k)", k=KT)).then_inc(s_cc, 16)
                        sp.dma_start(cc[:, 1, :], a["c_ctx"].rearrange("(p k) -> p k", k=KT)).then_inc(s_cc, 16)

                        def tokens(lo, hi, s):
                            if lo < TC:
                                sp.dma_start(xa[:, 0:TC, :], a["ctx"][0].rearrange("(t p) d -> p t d", p=P)).then_inc(s, 16)
                                lo = TC
                            src = a["x"][0, (lo - TC) * P:(hi - TC) * P, :]
                            sp.dma_start(xa[:, lo:hi, :], src.rearrange("(t p) d -> p t d", p=P)).then_inc(s, 16)

                        for n in range(NM):
                            if n >= RING:
                                sp.wait_ge(s_mm, n - RING + 1)
                            sp.dma_start(wm[n % RING][:, :, :], wmod[:, :, n * 512:(n + 1) * 512]).then_inc(s_wm[n % RING], 16)
                            if n in (1, 2, 3):
                                tokens(*parts[n - 1], s_x[n - 1])

                    @block.tensor
                    def _(pe):
                        def modulation(n):
                            pe.wait_ge(s_wm[n % RING], 16 * (n // RING + 1))
                            if n >= 2:
                                pe.wait_ge(s_mrow, n - 1)
                            for k in range(KT):
                                last = pe.matmul(psW[n % 2][0:2, :], cs[:, :, k], wm[n % RING][:, k, :],
                                                 start=(k == 0), stop=(k == KT - 1))
                            last.then_inc(s_mm, 1)

                        def turn_row(n):
                            pe.wait_ge(s_mrow, n + 1)
                            for q in range(4):
                                last = pe.transpose(psM[:, 4 * n + q, :], mrow[n % 2][:, q * P:(q + 1) * P], ident[0:2, 0:2])
                            last.then_inc(s_mt, 1)

                        def turn(t):
                            pe.wait_ge(s_xn, t + 1)
                            if t >= 2:
                                pe.wait_ge(s_evA, t - 1)
                                pe.wait_ge(s_evV, t - 1)
                            for k in range(KT):
                                last = pe.transpose(psX[t % 2][:, k, :], xn[:, t % 2, k * P:(k + 1) * P], ident)
                            last.then_inc(s_xt, 1)

                        pe.wait_ge(s_cst, 16)
                        pe.wait_ge(s_silu, 1)
                        for n in range(NM):
                            modulation(n)
                            if n:
                                turn_row(n - 1)
                            if n >= 3:
                                turn(n - 3)
                            if n == 6:
                                pe.wait_ge(s_rows, 12 * 16)
                                for z, m in enumerate((80, 108, 40)):
                                    last = pe.transpose(psV[:, z, 0:m], rows[0:m, z, :], ident[0:m, 0:m])
                                last.then_inc(s_vt, 1)
                        turn_row(NM - 1)
                        turn(TT - 1)

                    @block.scalar
                    def _(act):
                        r = [("b_mod", 0, 0, 48), ("g_pre1", 0, 48, 8), ("g_post1", 0, 56, 8), ("g_pre2", 0, 64, 8),
                             ("g_post2", 0, 72, 8)]
                        for name, z, at, n in r:
                            act.dma_start(rows[at:at + n, z, :], a[name][0].rearrange("(n p) -> n p", p=P)).then_inc(s_rows, 16)
                        act.dma_start(rows[0:108, 1, :], a["conv_rkv"][0].rearrange("y x (n p) -> (y x n) p", p=P)).then_inc(s_rows, 16)
                        at = 0
                        for name in ("decay_w0", "iclr_a0", "k_k", "k_a", "r_k", "b_spatial"):
                            src = a[name][0]
                            if len(src.shape) == 2 and src.shape[1] != P:
                                src = src.rearrange("a b -> (a b)")
                            if len(src.shape) == 1:
                                src = src.rearrange("(n p) -> n p", p=P)
                            n = src.shape[0]
                            act.dma_start(rows[at:at + n, 2, :], src).then_inc(s_rows, 16)
                            at += n
                        assert at == 40

                        def squares(i):
                            lo, hi = parts[i]
                            act.wait_ge(s_x[i], 32 if i == 0 else 16)
                            for t in range(lo, hi):
                                if t:
                                    act.wait_ge(s_ssq, t)
                                act.activation(sqj, xa[:, t, :], ACT.Square, accum_out=ssq[:, 0, t:t + 1]).then_inc(s_ssq, 1)
                            act.wait_ge(s_ssq, hi)
                            act.activation(ssq[:, 1, lo:hi], ssq[:, 0, lo:hi], ACT.Sqrt, scale=1.0 / D,
                                           bias=eps[:, 0:1]).then_inc(s_act, 1)

                        act.wait_ge(s_cc, 32)
                        act.activation(cs[:, :, :], cc[:, :, :], ACT.Silu).then_inc(s_silu, 1)
                        act.wait_ge(s_eps, 1)
                        squares(0)
                        for t in range(TT):
                            act.wait_ge(s_xt, t + 1)
                            act.activation(hT[:, 0:KT // 2, t * P:(t + 1) * P], psX[t % 2][:, 0:KT // 2, :],
                                           ACT.Copy).then_inc(s_evA, 1)
                            if t == 0:
                                squares(1)
                            if t == 2:
                                squares(2)
                        act.wait_ge(s_mod, 1)
                        act.wait_ge(s_evA, TT)
                        for k in range(0, KT // 2):
                            for z, cols in ((1, slice(0, CTX)), (0, slice(CTX, NTOK))):
                                act.activation(hT[:, k, cols], hT[:, k, cols], ACT.Identity, scale=g1[:, k, z:z + 1],
                                               bias=mod[:, SH1 + k, z:z + 1])

                    @block.vector
                    def _(dve):
                        ch = Chain(dve, s_dve)
                        for i, e in enumerate((EPS, LN_EPS, GN_EPS, 0.0)):
                            last = dve.memset(eps[:, i:i + 1], e)
                        last.then_inc(s_eps, 1)

                        def norm(t):
                            for i, (lo, hi) in enumerate(parts):
                                if t == lo:
                                    dve.wait_ge(s_act, i + 1)
                                    ch.link(dve.reciprocal(rstd1[:, lo:hi], ssq[:, 1, lo:hi]))
                            if t >= 2:
                                dve.wait_ge(s_xt, t - 1)
                            dve.tensor_scalar(xn[:, t % 2, :], xa[:, t, :], rstd1[:, t:t + 1], None, ALU.mult).then_inc(s_xn, 1)

                        def out(t):
                            dve.wait_ge(s_xt, t + 1)
                            dve.tensor_copy(hT[:, KT // 2:, t * P:(t + 1) * P], psX[t % 2][:, KT // 2:, :]).then_inc(s_evV, 1)

                        for n in range(NM):
                            dve.wait_ge(s_mm, n + 1)
                            if n >= 2:
                                dve.wait_ge(s_mt, n - 1)
                            dve.tensor_copy(mrow[n % 2][:, :], psW[n % 2][0:2, :]).then_inc(s_mrow, 1)
                            if n == 2:
                                norm(0)
                                norm(1)
                            if n >= 3:
                                out(n - 3)
                                if n - 1 < TT:
                                    norm(n - 1)
                            if n == 7:
                                dve.wait_ge(s_vt, 1)
                                ch.link(dve.tensor_copy(vec1[:, :], psV[:, 0, 0:80]))
                                ch.link(dve.tensor_copy(convw[:, :, :].rearrange("p a b -> p (a b)"), psV[:, 1, 0:108]))
                                ch.link(dve.tensor_copy(vec3[:, :], psV[:, 2, 0:40]))
                        dve.wait_ge(s_mt, NM)
                        for z in range(2):
                            ch.link(dve.tensor_tensor(mod[:, :, z], psM[:, :, z], vec1[:, 0:48], ALU.add))
                        for z in range(2):
                            last = dve.scalar_tensor_tensor(out=g1[:, :, z], in0=mod[:, SC1:SC1 + KT, z], scalar=1.0,
                                                            in1=vec1[:, 48:56], op0=ALU.add, op1=ALU.mult)
                            ch.link(last)
                        dve.tensor_copy(eps[:, 3:4], eps[:, 0:1]).then_inc(s_mod, 1)
                        out(TT - 1)
                        dve.wait_ge(s_evV, TT)
                        for k in range(KT // 2, KT):
                            for z, cols in ((1, slice(0, CTX)), (0, slice(CTX, NTOK))):
                                dve.tensor_scalar(hT[:, k, cols], hT[:, k, cols], g1[:, k, z:z + 1],
                                                  mod[:, SH1 + k, z:z + 1], ALU.mult, ALU.add)

                with ExitStack() as c2:
                    wr = [sb(c2, f"wr{i}", [P, KT, P]) for i in range(2)]
                    wh = [sb(c2, f"wh{i}", [P, KT, P], F32R) for i in range(2)]
                    wl = [sb(c2, f"wl{i}", [P, KT, P], F32R) for i in range(2)]
                    zp = [sb(c2, f"zp{i}", [P, ZC + ZL]) for i in range(2)]
                    hx = sb(c2, "hx", [P, KT // 2, NTOK], F32R)
                    hv = nc.alloc_sbuf_tensor_at("hv", [P, KT // 2, NTOK], F32R, offset=vt_at)
                    hl = nc.alloc_sbuf_tensor_at("hl", [P, KT, NTOK], F32R, offset=hT_at)
                    psZ = [pb(c2, f"psZ{i}", [P, 3, 512]) for i in range(2)]
                    s_zero, s_pz, s_zev, s_conv, s_dve, s_gate = (
                        sem(c2, n) for n in ("s_zero", "s_pz", "s_zev", "s_conv", "s_cch", "s_cgate"))
                    s_wr = [sem(c2, f"s_wr{i}") for i in range(2)]
                    s_hh, s_hlv, s_hlg, s_wh, s_wl = (sem(c2, n) for n in ("s_hh", "s_hlv", "s_hlg", "s_wh", "s_wl"))
                    NF = 15
                    H = KT // 2
                    parts = ((0, 512), (512, 512), (1024, 256))
                    kv2 = kvr[:, :, :].rearrange("p a b -> p (a b)")
                    win = a["w_in"][0].rearrange("(k p) n -> p k n", p=P)
                    block = c2.enter_context(nc.Block())

                    @block.sync
                    def _(sp):
                        def load(i, first):
                            for b in range(2):
                                f = 2 * i + b
                                if not first:
                                    sp.wait_ge(s_wl, f - 1)
                                sp.dma_start(wr[b][:, :, :], win[:, :, bass.ds(f * P, P)]).then_inc(s_wr[b], 16)

                        passes(sp, 7, load)
                        sp.wait_ge(s_wl, NF - 2)
                        sp.dma_start(wr[0][:, :, :], win[:, :, 14 * P:15 * P]).then_inc(s_wr[0], 16)

                    @block.gpsimd
                    def _(gp):
                        def low(i, b, first):
                            f = 2 * i + b
                            gp.wait_ge(s_wh, f + 1)
                            if not first:
                                gp.wait_ge(s_pz, f - 1)
                            gp.sem_inc(s_gate, 1)
                            gp.tensor_tensor(wl[b][:, :, :], wr[b][:, :, :], wh[b][:, :, :].bitcast(F32),
                                             ALU.subtract).then_inc(s_wl, 1)

                        low(0, 0, True)
                        for q, (n0, n) in enumerate(parts):
                            gp.wait_ge(s_hh, 2 * q + 2)
                            gp.tensor_tensor(hl[:, H:, n0:n0 + n], hT[:, H:, n0:n0 + n],
                                             hx[:, :, n0:n0 + n].bitcast(F32), ALU.subtract).then_inc(s_hlg, 1)
                        for b in range(2):
                            gp.memset(zp[b][:, :], 0.0).then_inc(s_zero, 1)
                        low(0, 1, True)
                        with gp.Fori(1, 7) as i:
                            low(i, 0, False)
                            low(i, 1, False)
                        low(7, 0, False)
                        gp.wait_ge(s_pz, NF)
                        gp.tensor_tensor(hT[:, KT - 2:, CTX:], hl[:, KT - 2:, CTX:].bitcast(F32), hx[:, H - 2:, CTX:].bitcast(F32), ALU.add)

                    @block.tensor
                    def _(pe):
                        def tile(i, b, first):
                            pe.wait_ge(s_wl, 2 * i + b + 1)
                            if not first:
                                pe.wait_ge(s_zev, 2 * i + b - 1)
                            for q, (n0, n) in enumerate(parts):
                                if first and b == 0:
                                    pe.wait_ge(s_hlv, q + 1)
                                    pe.wait_ge(s_hlg, q + 1)
                                for k in range(KT):
                                    hi = hv[:, k, n0:n0 + n] if k < H else hx[:, k - H, n0:n0 + n]
                                    lo = hl[:, k, n0:n0 + n]
                                    pe.matmul(psZ[b][:, q, 0:n], wh[b][:, k, :], hi, start=(k == 0), stop=False)
                                    pe.matmul(psZ[b][:, q, 0:n], wh[b][:, k, :], lo, start=False, stop=False)
                                    last = pe.matmul(psZ[b][:, q, 0:n], wl[b][:, k, :], hi, start=False, stop=(k == KT - 1))
                            last.then_inc(s_pz, 1)

                        def pair(i, first):
                            tile(i, 0, first)
                            tile(i, 1, first)

                        passes(pe, 7, pair)
                        tile(7, 0, False)

                    @block.scalar
                    def _(act):
                        def high(i, b, first):
                            f = 2 * i + b
                            act.wait_ge(s_wr[b], 16 * (i + 1))
                            if not first:
                                act.wait_ge(s_pz, f - 1)
                            act.activation(wh[b][:, :, :], wr[b][:, :, :], ACT.Copy).then_inc(s_wh, 1)

                        high(0, 0, True)
                        for n0, n in parts:
                            act.activation(hv[:, :, n0:n0 + n], hT[:, 0:H, n0:n0 + n], ACT.Copy).then_inc(s_hh, 1)
                            act.activation(hx[:, :, n0:n0 + n], hT[:, H:, n0:n0 + n], ACT.Copy).then_inc(s_hh, 1)
                        high(0, 1, True)
                        act.wait_ge(s_zero, 2)

                        def spread(i, first):
                            for b in range(2):
                                f = 2 * i + b
                                act.wait_ge(s_pz, f + 1)
                                if not first:
                                    act.wait_ge(s_conv, f - 1)
                                z = psZ[b][:, :, :].rearrange("p a b -> p (a b)")
                                act.activation(zp[b][:, 1:1 + CTX], z[:, 0:CTX], ACT.Copy)
                                g = zp[b][:, ZC:ZC + ZL].rearrange("p (r c) -> p r c", c=PADW)
                                act.activation(g[:, 1:1 + ROWS, 1:1 + GRID],
                                               z[:, CTX:NTOK].rearrange("p (r c) -> p r c", c=GRID),
                                               ACT.Copy).then_inc(s_zev, 1)
                                high(i + 1, b, False)

                        passes(act, 6, spread)
                        for f, (dst, fn) in enumerate(((lw, ACT.Tanh), (la, ACT.Copy), (sg, ACT.Sigmoid))):
                            act.wait_ge(s_pz, 13 + f)
                            z = psZ[f % 2][:, :, :].rearrange("p a b -> p (a b)")[:, 0:NTOK]
                            act.activation(dst[:, :], z, fn).then_inc(s_zev, 1)
                            if f == 0:
                                high(7, 0, False)

                    @block.vector
                    def _(dve):
                        ch = Chain(dve, s_dve)
                        for q, (n0, n) in enumerate(parts):
                            dve.wait_ge(s_hh, 2 * q + 1)
                            dve.tensor_tensor(hl[:, 0:H, n0:n0 + n], hT[:, 0:H, n0:n0 + n],
                                              hv[:, :, n0:n0 + n].bitcast(F32), ALU.subtract).then_inc(s_hlv, 1)

                        def conv(i, first):
                            ch.loop(i, 2 * 9)
                            for b in range(2):
                                f = 2 * i + b
                                dve.wait_ge(s_zev, f + 1)
                                g = zp[b][:, ZC:ZC + ZL].rearrange("p (r c) -> p r c", c=PADW)
                                og = kv2[:, bass.ds(f * NTOK + CTX, SEQ)].rearrange("p (r c) -> p r c", c=GRID)
                                oc = kv2[:, bass.ds(f * NTOK, CTX)]
                                for tap in range(9):
                                    y, x = tap // 3, tap % 3
                                    w = convw[:, tap, bass.ds(f, 1)]
                                    src = g[:, y:y + ROWS, x:x + GRID]
                                    if tap == 0:
                                        ins = dve.tensor_scalar(og, src, w, None, ALU.mult)
                                    else:
                                        ins = dve.scalar_tensor_tensor(out=og, in0=src, scalar=w, in1=og,
                                                                       op0=ALU.mult, op1=ALU.add)
                                    if y == 1:
                                        src = zp[b][:, x:x + CTX]
                                        if x == 0:
                                            ins = dve.tensor_scalar(oc, src, w, None, ALU.mult)
                                        else:
                                            ins = dve.scalar_tensor_tensor(out=oc, in0=src, scalar=w, in1=oc,
                                                                           op0=ALU.mult, op1=ALU.add)
                                    ch.link(ins)
                                dve.nop().then_inc(s_conv, 1)

                        passes(dve, 6, conv)
                        dve.wait_ge(s_pz, NF)
                        dve.tensor_tensor(hT[:, 0:H, CTX:], hl[:, 0:H, CTX:].bitcast(F32), hv[:, :, CTX:].bitcast(F32), ALU.add)
                        dve.tensor_tensor(hT[:, H:KT - 2, CTX:], hl[:, H:KT - 2, CTX:].bitcast(F32), hx[:, 0:H - 2, CTX:].bitcast(F32), ALU.add)

                with ExitStack() as c3:
                    wa = [sb(c3, f"wa{i}", [P, KT, 256]) for i in range(2)]
                    uh = vt[:, 0:TL, :]
                    vn = sb(c3, "vn", [P, TL, AW])
                    ws = sb(c3, "ws", [P, 8, P])
                    wsT = sb(c3, "wsT", [P, 8, P])
                    lnrow = sb(c3, "lnrow", [P, 2, AW])
                    sq = sb(c3, "sq", [P, 4 * AW])
                    st = sb(c3, "st", [P, 4, 2, 32])
                    psA = [pb(c3, f"psA{i}", [P, 512]) for i in range(4)]
                    psT = pb(c3, "psT", [P, 2, 4, P])
                    psG = [pb(c3, f"psG{i}", [P, TL, HD]) for i in range(2)]
                    s_ws, s_ln, s_wst, s_wse, s_pa, s_gelu, s_var, s_std, s_vn, s_sp, s_oa, s_dve, s_st = (
                        sem(c3, n) for n in ("s_ws", "s_ln", "s_wst", "s_wse", "s_pa", "s_gelu", "s_var", "s_std",
                                             "s_vn", "s_sp", "s_oa", "s_ach", "s_st"))
                    s_wa = [sem(c3, f"s_wa{i}") for i in range(2)]
                    quarters = [(vn, OFF_U + AW, 0), (vn, OFF_U + AW, 1), (uh, OFF_U, 0), (uh, OFF_U, 1)]
                    block = c3.enter_context(nc.Block())

                    @block.sync
                    def _(sp):
                        sp.dma_start(ws[:, :, :], a["w_spatial"][0].rearrange("g p q -> p g q")).then_inc(s_ws, 16)
                        for n, (_, off, h) in enumerate(quarters):
                            if n >= 2:
                                sp.wait_ge(s_pa, TL * (n - 1))
                            sp.dma_start(wa[n % 2][:, :, :], win[:, :, off + 256 * h:off + 256 * h + 256]).then_inc(s_wa[n % 2], 16)
                        sp.dma_start(scratch["lw"], lw[:, :]).then_inc(s_st, 16)
                        sp.dma_start(scratch["sg"], sg[:, :]).then_inc(s_st, 16)
                        sp.wait_ge(s_oa, 8)
                        sp.dma_start(scratch["oA"].rearrange("(t p) n -> p t n", p=P), uh).then_inc(s_st, 16)
                        sp.wait_ge(s_st, 48)

                    @block.gpsimd
                    def _(gp):
                        for i, n in enumerate(("gm_ln_g", "gm_ln_b")):
                            gp.dma_start(lnrow[:, i, :], bass.AP(a[n].tensor, 0, [[0, P], [1, AW]])).then_inc(s_ln, 16)

                    @block.tensor
                    def _(pe):
                        pe.wait_ge(s_ws, 16)
                        for g in range(8):
                            last = pe.transpose(psT[:, g // 4, g % 4, :], ws[:, g, :], ident)
                        last.then_inc(s_wst, 1)
                        for n in range(4):
                            pe.wait_ge(s_wa[n % 2], 16 * (n // 2 + 1))
                            for t in range(TL):
                                m = n * TL + t
                                if m >= 4:
                                    pe.wait_ge(s_gelu, m - 3)
                                for k in range(KT):
                                    last = pe.matmul(psA[m % 4][:, 0:256], hT[:, k, CTX + t * P:CTX + (t + 1) * P],
                                                     wa[n % 2][:, k, :], start=(k == 0), stop=(k == KT - 1))
                                last.then_inc(s_pa, 1)
                        pe.wait_ge(s_wse, 1)
                        pe.wait_ge(s_vn, 2)
                        for g in range(8):
                            if g >= 2:
                                pe.wait_ge(s_oa, g - 1)
                            pe.matmul(psG[g % 2][:, :, :], wsT[:, g, :], vn[:, :, g * HD:(g + 1) * HD],
                                      start=True, stop=True).then_inc(s_sp, 1)

                    @block.scalar
                    def _(act):
                        act.wait_ge(s_wst, 1)
                        act.activation(wsT[:, :, :], psT[:, :, :, :].rearrange("p a b c -> p (a b) c"), ACT.Copy).then_inc(s_wse, 1)
                        for n, (dst, _, h) in enumerate(quarters):
                            for t in range(TL):
                                m = n * TL + t
                                act.wait_ge(s_pa, m + 1)
                                act.activation(dst[:, t, h * 256:(h + 1) * 256], psA[m % 4][:, 0:256],
                                               ACT.Gelu_apprx_tanh).then_inc(s_gelu, 1)
                            if n == 2:
                                for hf in range(2):
                                    act.wait_ge(s_var, hf + 1)
                                    act.activation(st[:, 2, hf, :], st[:, 1, hf, :], ACT.Sqrt, scale=1.0 / HD,
                                                   bias=eps[:, 1:2]).then_inc(s_std, 1)

                    @block.vector
                    def _(dve):
                        ch = Chain(dve, s_dve)
                        dve.wait_ge(s_ln, 32)
                        dve.wait_ge(s_gelu, 2 * TL)
                        for hf in range(2):
                            v = vn[:, 4 * hf:4 * hf + 4, :].rearrange("p t (g d) -> p (t g) d", d=HD)
                            q = sq[:, :].rearrange("p (n d) -> p n d", d=HD)
                            ch.link(dve.reduce_sum(st[:, 0, hf, :], v, AX.X))
                            ch.link(dve.tensor_scalar(st[:, 0, hf, :], st[:, 0, hf, :], 1.0 / HD, None, ALU.mult))
                            ch.link(dve.tensor_tensor(v, v, st[:, 0, hf, :].unsqueeze(2).broadcast_to([P, 32, HD]), ALU.subtract))
                            ch.link(dve.tensor_tensor(q, v, v, ALU.mult))
                            dve.reduce_sum(st[:, 1, hf, :], q, AX.X).then_inc(s_var, 1)
                        for hf in range(2):
                            v = vn[:, 4 * hf:4 * hf + 4, :].rearrange("p t (g d) -> p (t g) d", d=HD)
                            w = vn[:, 4 * hf:4 * hf + 4, :]
                            dve.wait_ge(s_std, hf + 1)
                            ch.link(dve.reciprocal(st[:, 3, hf, :], st[:, 2, hf, :]))
                            ch.link(dve.tensor_tensor(v, v, st[:, 3, hf, :].unsqueeze(2).broadcast_to([P, 32, HD]), ALU.mult))
                            ch.link(dve.tensor_tensor(w, w, lnrow[:, 0, :].unsqueeze(1).broadcast_to([P, 4, AW]), ALU.mult))
                            dve.tensor_tensor(w, w, lnrow[:, 1, :].unsqueeze(1).broadcast_to([P, 4, AW]), ALU.add).then_inc(s_vn, 1)
                        dve.wait_ge(s_gelu, 4 * TL)
                        for g in range(8):
                            dve.wait_ge(s_sp, g + 1)
                            o = uh[:, :, g * HD:(g + 1) * HD]
                            dve.scalar_tensor_tensor(out=o, in0=psG[g % 2][:, :, :], scalar=vec3[:, 32 + g:33 + g],
                                                     in1=o, op0=ALU.add, op1=ALU.mult).then_inc(s_oa, 1)

            cum = sb(mixer, "cum", [P, 2, J, TT * CH])
            em = sb(mixer, "em", [P, 2, J, TT])
            em2 = sb(mixer, "em2", [P, 2, J, TT])
            kmid = sb(mixer, "kmid", [P, 2, 2, J, TT])
            iup = sb(mixer, "iup", [P, BW])
            rkm = sb(mixer, "rkm", [P, J, 2])
            omk = sb(mixer, "omk", [P, 8])
            with ExitStack() as c4:
                lwb = sb(c4, "lwb", [P, NTOK])
                dup = sb(c4, "dup", [P, BW])
                rst = sb(c4, "rst", [P, 2, TT * CH])
                dwb = [sb(c4, f"dwb{i}", [P, TT * CH]) for i in range(2)]
                ks = [sb(c4, f"ks{i}", [P, NTOK]) for i in range(2)]
                nrm = sb(c4, "nrm", [P, TT, 2 * J])
                rx = [sb(c4, f"rx{i}", [P, TT, 2, HD]) for i in range(2)]
                psD = [pb(c4, f"psD{i}", [P, 3, 512]) for i in range(2)]
                psT = [pb(c4, f"psVT{i}", [P, J, P]) for i in range(2)]
                s_in, s_zero, s_vt, s_ve, s_pd, s_dw, s_cum, s_sq, s_pn, s_mx, s_rt, s_rc, s_rx, s_px, s_kk, s_dve, s_em = (
                    sem(c4, "s4_" + n) for n in ("in", "zero", "vt", "ve", "pd", "dw", "cum", "sq", "pn", "mx", "rt", "rc",
                                                 "rx", "px", "kk", "ch", "em"))
                psN = psD[0][:, 0, 0:TT * 2 * J].rearrange("p (t h) -> p t h", h=2 * J)
                block = c4.enter_context(nc.Block())
                cols = ((0, 512), (512, 512), (1024, 256))

                @block.sync
                def _(sp):
                    sp.dma_start(lwb[:, :], scratch["lw"]).then_inc(s_in, 16)
                    sp.dma_start(dup[:, :], a["decay_up"][0].rearrange("d l n -> (d l) n")).then_inc(s_in, 16)
                    sp.dma_start(iup[:, :], a["iclr_up"][0].rearrange("d l n -> (d l) n")).then_inc(s_in, 16)
                    sp.dma_start(rst[:, :, :], a["consts"][:, CAT["reset"][0]:CAT["slotrow"][0]]).then_inc(s_in, 16)

                @block.gpsimd
                def _(gp):
                    for b in range(2):
                        gp.memset(dwb[b][:, :], 0.0).then_inc(s_zero, 1)
                    gp.wait_ge(s_rc, 1)
                    for j in range(J):
                        if j >= 2:
                            gp.wait_ge(s_px, j - 1)
                        gp.tensor_copy(rx[j % 2][:, :, :, :],
                                       nrm[:, :, 2 * j:2 * j + 2].unsqueeze(3).broadcast_to([P, TT, 2, HD])).then_inc(s_rx, 1)

                @block.tensor
                def _(pe):
                    for j in range(J):
                        pe.wait_ge(s_sq, j + 1)
                        for t in range(TT):
                            last = pe.matmul(psN[:, t, 2 * j:2 * j + 2], ks[j % 2][:, t * P:(t + 1) * P], headcol,
                                             start=True, stop=True)
                        last.then_inc(s_pn, 1)
                    pe.wait_ge(s_mx, 1)
                    pe.wait_ge(s_in, 64)
                    for j in range(J):
                        for d in range(2):
                            n = 2 * j + d
                            if n >= 2:
                                pe.wait_ge(s_dw, n - 1)
                            for q, (n0, w) in enumerate(cols):
                                last = pe.matmul(psD[n % 2][:, q, 0:w], dup[64 * d:64 * d + 64, j * P:(j + 1) * P],
                                                 lwb[64 * d:64 * d + 64, n0:n0 + w], start=True, stop=True)
                            last.then_inc(s_pd, 1)
                    for t in range(TT):
                        if t >= 2:
                            pe.wait_ge(s_ve, t - 1)
                        for j in range(J):
                            last = pe.transpose(psT[t % 2][:, j, :], kvr[:, J + j, t * P:(t + 1) * P], ident)
                        last.then_inc(s_vt, 1)
                    pe.wait_ge(s_dw, 2 * J)
                    for j in range(J):
                        pe.wait_ge(s_rx, j + 1)
                        if j >= 2:
                            pe.wait_ge(s_kk, j - 1)
                        for t in range(TT):
                            last = pe.transpose(psD[j % 2][:, t // 4, (t % 4) * P:(t % 4 + 1) * P],
                                                rx[j % 2][:, t, :, :].rearrange("p a b -> p (a b)"), ident)
                        last.then_inc(s_px, 1)

                @block.scalar
                def _(act):
                    for j in range(J):
                        if j >= 2:
                            act.wait_ge(s_pn, j - 1)
                        act.activation(ks[j % 2][:, :], kvr[:, j, :], ACT.Square, scale=vec3[:, 16 + j:17 + j]).then_inc(s_sq, 1)
                    act.wait_ge(s_mx, 1)
                    act.activation(nrm[:, :, :], nrm[:, :, :], ACT.Sqrt).then_inc(s_rt, 1)
                    act.wait_ge(s_zero, 2)
                    for j in range(J):
                        for d in range(2):
                            n = 2 * j + d
                            act.wait_ge(s_pd, n + 1)
                            if n >= 2:
                                act.wait_ge(s_cum, n - 1)
                            o = dwb[n % 2][:, :].rearrange("p (c k) -> p c k", k=CH)[:, :, 1 - d:1 - d + P]
                            z = psD[n % 2][:, :, :].rearrange("p a b -> p (a b)")[:, 0:NTOK]
                            act.activation(o, z.rearrange("p (c k) -> p c k", k=P), ACT.Sigmoid,
                                           bias=vec3[:, d * J + j:d * J + j + 1]).then_inc(s_dw, 1)
                    for t in range(TT):
                        act.wait_ge(s_vt, t + 1)
                        act.activation(vt[:, t, :], psT[t % 2][:, :, :].rearrange("p a b -> p (a b)"), ACT.Copy).then_inc(s_ve, 1)
                    act.wait_ge(s_cum, 2 * J)
                    act.wait_ge(s_em, 1)
                    act.activation(em[:, :, :, :], kmid[:, 1, :, :, :], ACT.Exp).then_inc(s_em, 1)

                @block.vector
                def _(dve):
                    ch = Chain(dve, s_dve)
                    dve.wait_ge(s_pn, J)
                    dve.tensor_scalar(nrm[:, :, :], psN, 1e-24, None, ALU.max).then_inc(s_mx, 1)
                    dve.wait_ge(s_rt, 1)
                    dve.reciprocal(nrm[:, :, :], nrm[:, :, :]).then_inc(s_rc, 1)
                    dve.wait_ge(s_in, 64)
                    for j in range(J):
                        last = dve.tensor_scalar(rkm[:, j, :], headcol, vec3[:, 28 + j:29 + j], None, ALU.mult)
                    ch.link(dve.tensor_scalar(omk[:, :], vec3[:, 20:28], -1.0, 1.0, ALU.mult, ALU.add))
                    for j in range(J):
                        for d in range(2):
                            n = 2 * j + d
                            dve.wait_ge(s_dw, n + 1)
                            if d == 0:
                                o, m, i = cum[:, d, j, :], rst[:, d, :], dwb[n % 2][:, :]
                            else:
                                o, m, i = (backwards(x) for x in (cum[:, d, j, :], rst[:, d, :], dwb[n % 2][:, :]))
                            dve.tensor_tensor_scan(o, m, i, 0.0, ALU.mult, ALU.add).then_inc(s_cum, 1)
                    dve.wait_ge(s_cum, 2 * J)
                    for d in range(2):
                        end = cum[:, d, :, :].rearrange("p j (c k) -> p j c k", k=CH)[:, :, :, P if d == 0 else 0]
                        last = dve.tensor_scalar(kmid[:, 0, d, :, :], end, KAPPA / 2, None, ALU.mult)
                        last = dve.tensor_scalar(kmid[:, 1, d, :, :], end, -KAPPA / 2, None, ALU.mult)
                    last.then_inc(s_em, 1)
                    dve.wait_ge(s_em, 2)
                    dve.tensor_tensor(em2[:, 0, :, 0:TT - 1], em[:, 0, :, 0:TT - 1], em[:, 0, :, 1:TT], ALU.mult)
                    dve.tensor_tensor(em2[:, 1, :, 1:2], em[:, 1, :, 1:2], em[:, 1, :, 0:1], ALU.mult)
                    dve.tensor_tensor(em2[:, 1, :, 0:1], em[:, 1, :, 0:1], em[:, 1, :, TT - 1:TT], ALU.mult)
                    ch.link(dve.tensor_tensor(em2[:, 1, :, 3:TT], em[:, 1, :, 3:TT], em[:, 1, :, 2:TT - 1], ALU.mult))
                    dve.wait_ge(s_ve, TT)
                    for j in range(J):
                        dve.wait_ge(s_px, j + 1)
                        z = psD[j % 2][:, :, :].rearrange("p a b -> p (a b)")[:, 0:NTOK]
                        dve.scalar_tensor_tensor(out=kvr[:, J + j, :], in0=kvr[:, j, :], scalar=vec3[:, 16 + j:17 + j],
                                                 in1=z, op0=ALU.mult, op1=ALU.mult).then_inc(s_kk, 1)

            with ExitStack() as c5:
                NL = len(LEVELS)
                lT = sb(c5, "lT", [P, 4, P])
                akT = [sb(c5, f"akT{q}", [P, 4, P]) for q in range(2)]
                rbT = [sb(c5, f"rbT{q}", [P, 4, P]) for q in range(2)]
                rkT = [sb(c5, f"rkT{q}", [P, 4, P]) for q in range(2)]
                inv = [sb(c5, f"inv{q}", [P, 4, P]) for q in range(2)]
                invT = [sb(c5, f"invT{q}", [P, 4, P]) for q in range(2)]
                xl = [sb(c5, f"xl{l}", [P, 2, P]) for l in range(NL)]
                lc = [sb(c5, f"lc{l}", [P, 2, P]) for l in (0, 1, 3, 4)]
                lc = [lc[0], lc[1], lc[0], lc[2], lc[3], lc[1]]
                tc = [sb(c5, f"tc{l}", [P, 2, P]) for l in range(NL - 1)]
                ar = [sb(c5, f"ar{j}", [P, 2, 2, P]) for j in range(J)]
                vs = [sb(c5, f"vs{j}", [P, 2, P]) for j in range(J)]
                bk = [sb(c5, f"bk{q}", [P, 2, 2, P]) for q in range(2)]
                bkt = [sb(c5, f"bkt{q}", [P, 2, 2, P]) for q in range(2)]
                e1 = sb(c5, "e1", [P, 2, CH])
                e2 = sb(c5, "e2", [P, 2, P])
                ag = sb(c5, "ag", [P, 2, P])
                km = sb(c5, "km", [P, 2, P])
                rk = sb(c5, "rk", [P, 2, P])
                las = sb(c5, "las", [P, 2, P])
                un = sb(c5, "un", [P, 4, HD])
                yst = sb(c5, "yst", [P, 4, HD])
                n0 = sb(c5, "n0", [P, J, 2, P])
                psG = pb(c5, "ps5G", [P, 4, 2, 2, P])
                psX = [pb(c5, f"ps5X{q}", [P, 512]) for q in range(2)]
                psT = [pb(c5, f"ps5T{q}", [P, 512]) for q in range(2)]
                names = ("init", "la", "prep", "pch", "amm", "kt", "gram", "t2", "xa", "xb", "ta", "tta", "tb", "ttb",
                         "s1", "s2", "s3", "lt", "tt2", "gr", "xea", "xeb", "ttea", "tteb", "vp", "y", "n", "dch",
                         "sig", "ex", "bkt", "t2e", "tea", "teb", "u", "bonp", "bone", "gate",
                         "lca", "lcb", "tca", "tcb")
                S = {n: sem(c5, f"s5_{n}") for n in names}
                s_y = sem(c5, "s5_yd")
                G = TT * J

                def cols(tile, l, side):
                    m = LEVELS[l]
                    base = tile[:, :, :]
                    ps = base.ap[0][0]
                    first, other = (0, m) if side == 0 else (m, 0)
                    return bass.AP(base.tensor, base.offset + first,
                                   [[ps, P], [2 * P + other - first, 2], [P, 2], [2 * m, HD // m], [1, m]])

                def moving(tile, h, l, side):
                    m = LEVELS[l]
                    base = tile[:, h, :]
                    first, other = (0, m) if side == 0 else (m, 0)
                    return bass.AP(base.tensor, base.offset + first,
                                   [[base.ap[0][0], P], [2 * P + other - first, 2], [2 * m, HD // m], [1, m]])

                def mixed(tile, l):
                    m = LEVELS[l]
                    base = tile[:, 2:, :]
                    return bass.AP(base.tensor, base.offset,
                                   [[base.ap[0][0], P], [P, 2], [2 * m, HD // m], [m - 2 * P, 2], [1, m]])

                def apart(tile, l, h=None):
                    m = LEVELS[l]
                    base = tile[:, h or 0, :]
                    heads = [[P, 2]] if h is None else []
                    return bass.AP(base.tensor, base.offset,
                                   [[base.ap[0][0], P], [m, 2]] + heads + [[2 * m, HD // m], [1, m]])

                def five(tile, l, off=0):
                    m = LEVELS[l]
                    return tile[:, off:off + 256].rearrange("p (h d b i) -> p d h b i", d=2, h=2, i=m)

                def back(c):
                    return (1 - c if c < TC else TT + 1 - c) if isinstance(c, int) else (TT + 1) - c

                def where(c):
                    return c, back(c)

                def run(eng, group):
                    def step(c, last=False):
                        for j in range(J):
                            g = c * J + j
                            prev = (c, j - 1, g - 1) if j else (c - 1, J - 1, g - 1)
                            nxt = (c, j + 1, g + 1) if j + 1 < J else (c + 1, 0, g + 1)
                            if isinstance(c, int) and c == 0 and j == 0:
                                prev = None
                            if last and j == J - 1:
                                nxt = None
                            group(c, j, g, prev, nxt)
                    for c in range(TC + 1):
                        step(c)
                    with eng.Fori(TC + 1, TT - 1) as c:
                        step(c)
                    step(TT - 1, last=True)
                    group(None, None, G, (TT - 1, J - 1, G - 1), None)

                def early(c):
                    return isinstance(c, int) and c < TC

                kflat = kvr[:, :, :].rearrange("p a b -> p (a b)")
                vflat = vt[:, :, :].rearrange("p a b -> p (a b)")
                cumf = cum[:, :, :, :].rearrange("p a b c -> p (a b c)")
                kmf = kmid[:, :, :, :, :].rearrange("p z a b c -> p (z a b c)")
                em2f = em2[:, :, :, :].rearrange("p a b c -> p (a b c)")
                bonf = bon[:, :, :, :].rearrange("p a b c -> p (a b c)")
                block = c5.enter_context(nc.Block())

                @block.gpsimd
                def _(gp):
                    for l in range(NL):
                        gp.memset(xl[l][:, :, :], 0.0)
                    for u in range(4):
                        gp.tensor_copy(lT[:, u, :], ident)
                    gp.memset(n0[:, :, :, :], 0.0).then_inc(S["init"], 1)

                    def prep(c, j, g, first=False):
                        at = where(c)
                        if not first:
                            gp.wait_ge(S["amm"], g)
                        gp.sem_inc(S["gate"], 1)
                        for d in range(2):
                            o = at[d] * P
                            gp.tensor_copy(las[:, d, :], la[:, bass.ds(o, P)])
                        if not (isinstance(g, int) and g < 4):
                            gp.wait_ge(S["s3"], g - 3)
                        gp.sem_inc(S["gate"], 1)
                        for d in range(2):
                            last = gp.tensor_copy(vs[j][:, d, :], vflat[:, bass.ds(at[d] * BW + j * P, P)])
                        last.then_inc(S["la"], 1)
                        q = j % 2
                        gp.wait_ge(S["ex"], g + 1)
                        gp.sem_inc(S["gate"], 1)
                        for d in range(2):
                            o = at[d] * P
                            kk = kflat[:, bass.ds((J + j) * NTOK + o, P)]
                            r = kflat[:, bass.ds((2 * J + j) * NTOK + o, P)]
                            excl, incl = (0, 1) if d == 0 else (1, 0)
                            gp.tensor_tensor(ar[j][:, d, 0, :], kk, e1[:, d, excl:excl + P], ALU.mult)
                            gp.tensor_tensor(ar[j][:, d, 1, :], r, e1[:, d, incl:incl + P], ALU.mult)
                        gp.wait_ge(S["sig"], g + 1)
                        if not (isinstance(g, int) and g < 2):
                            gp.wait_ge(S["gram"], g - 1)
                            gp.wait_ge(S["kt"], g - 1)
                        if not first:
                            gp.wait_ge(S["bonp"], g)
                        gp.sem_inc(S["gate"], 1)
                        for d in range(2):
                            o = at[d] * P
                            kk = kflat[:, bass.ds((J + j) * NTOK + o, P)]
                            gp.tensor_scalar(km[:, d, :], ag[:, d, :], vec3[:, 20 + 4 * d + j:21 + 4 * d + j],
                                             omk[:, 4 * d + j:4 * d + j + 1], ALU.mult, ALU.add)
                            last = gp.tensor_tensor(bk[q][:, d, 0, :], kk, ag[:, d, :], ALU.mult)
                        last.then_inc(S["pch"], 1)
                        gp.wait_ge(S["pch"], 2 * g + 1)
                        gp.sem_inc(S["gate"], 1)
                        for d in range(2):
                            k = kflat[:, bass.ds(j * NTOK + at[d] * P, P)]
                            gp.tensor_tensor(km[:, d, :], km[:, d, :], k, ALU.mult)
                            last = gp.tensor_tensor(bk[q][:, d, 0, :], bk[q][:, d, 0, :], e2[:, d, :], ALU.mult)
                        last.then_inc(S["pch"], 1)
                        gp.wait_ge(S["pch"], 2 * g + 2)
                        gp.sem_inc(S["gate"], 1)
                        for d in range(2):
                            r = kflat[:, bass.ds((2 * J + j) * NTOK + at[d] * P, P)]
                            gp.tensor_tensor(rk[:, d, :], km[:, d, :], r, ALU.mult)
                            last = gp.tensor_tensor(bk[q][:, d, 1, :], km[:, d, :], e2[:, d, :], ALU.mult)
                        last.then_inc(S["prep"], 1)

                    prep(0, 0, 0, True)

                    def group(c, j, g, prev, nxt):
                        if nxt:
                            prep(*nxt)

                    run(gp, group)

                @block.tensor
                def _(pe):
                    def rates(c, j, g):
                        pe.wait_ge(S["la"], g + 1)
                        if not (isinstance(g, int) and g < 1):
                            pe.wait_ge(S["gr"], g)
                        for d in range(2):
                            last = pe.matmul(psG[:, d, 0, 0, :], iup[64 * d:64 * d + 64, j * P:(j + 1) * P],
                                             las[64 * d:64 * d + 64, d, :], start=True, stop=True)
                        last.then_inc(S["amm"], 1)

                    def mul(out, left, right, s):
                        for h in range(2):
                            last = pe.matmul(out[:, h * P:(h + 1) * P], left[:, h, :], right(h), start=True, stop=True)
                        last.then_inc(s, 1)

                    def mul_x(q, l, s):
                        mul(psT[q][:, 256:512], lc[l], lambda h: moving(inv[q], h, l, 0), s)

                    def mul_tt(q, l, s):
                        mul(psX[q][:, 256:512], xl[l], lambda h: moving(invT[q], h, l, 1), s)

                    def mul_t(q, l, s):
                        mul(psT[q][:, 0:256], tc[l], lambda h: apart(xl[l], l, h), s)

                    pe.wait_ge(S["init"], 2)
                    rates(0, 0, 0)

                    def group(c, j, g, prev, nxt):
                        q = None if c is None else j % 2
                        if prev:
                            cp, jp, gp_ = prev
                            qp = jp % 2
                        if c is not None:
                            pe.wait_ge(S["prep"], g + 1)
                            if not (isinstance(g, int) and g < 2):
                                pe.wait_ge(S["u"], g - 1)
                            for d in range(2):
                                for z in range(2):
                                    last = pe.transpose(psT[q][:, (2 * d + z) * P:(2 * d + z + 1) * P], bk[q][:, d, z, :], ident)
                            last.then_inc(S["kt"], 1)
                            if not (isinstance(g, int) and g < 1):
                                pe.wait_ge(S["gr"], g)
                                pe.wait_ge(S["bone"], g)
                            pe.wait_ge(S["sig"], g + 1)
                            w = 1 if early(c) else 2
                            for u in range(4):
                                d, h = u // 2, u % 2
                                rows = slice(64 * h, 64 * h + 64)
                                for z in range(2):
                                    last = pe.matmul(psG[:, u, z, 0:w, :], bk[q][rows, d, z, :], ar[j][rows, d, 0:w, :],
                                                     start=True, stop=True)
                            last.then_inc(S["gram"], 1)
                        if prev:
                            pe.wait_ge(S["tea"], 4 * gp_ + 4)
                            pe.wait_ge(S["lcb"], 2 * gp_ + 1)
                            mul_x(qp, 4, S["xb"])
                        if c is not None:
                            pe.wait_ge(S["tt2"], g + 1)
                            if not (isinstance(g, int) and g < 2):
                                pe.wait_ge(S["n"], g - 1)
                            for u in range(4):
                                last = pe.transpose(psX[q][:, u * P:(u + 1) * P], invT[q][:, u, :], ident)
                            last.then_inc(S["t2"], 1)
                        if prev:
                            pe.wait_ge(S["xeb"], 2 * gp_ + 1)
                            pe.wait_ge(S["tcb"], gp_ + 1)
                            mul_t(qp, 4, S["tb"])
                            mul_tt(qp, 4, S["ttb"])
                        for l in range(4):
                            if c is not None:
                                if l == 0:
                                    pe.wait_ge(S["t2e"], g + 1)
                                    pe.wait_ge(S["bkt"], g + 1)
                                else:
                                    pe.wait_ge(S["tea"], 4 * g + l)
                                pe.wait_ge(S["lca"], 4 * g + l + 1)
                                mul_x(q, l, S["xa"])
                            if prev and l == 0:
                                pe.wait_ge(S["teb"], gp_ + 1)
                                pe.wait_ge(S["lcb"], 2 * gp_ + 2)
                                mul_x(qp, 5, S["xb"])
                            if prev and l == 1:
                                pe.wait_ge(S["tteb"], 2 * gp_ + 2)
                                pe.wait_ge(S["gr"], gp_ + 1)
                                if not (isinstance(gp_, int) and gp_ < 4):
                                    pe.wait_ge(S["n"], gp_ - 3)
                                for d in range(2):
                                    pe.matmul(psX[qp][:, d * P:(d + 1) * P], ar[jp][:, d, 0, :], n0[:, jp, d, :],
                                              start=True, stop=False)
                                    for h in range(2):
                                        u = 2 * d + h
                                        last = pe.matmul(psX[qp][:, u * HD:(u + 1) * HD], akT[qp][:, u, :],
                                                         vs[jp][:, d, h * HD:(h + 1) * HD], start=False, stop=(h == 1))
                                last.then_inc(S["s1"], 1)
                            if c is not None:
                                pe.wait_ge(S["xea"], 4 * g + l + 1)
                                pe.wait_ge(S["tca"], 4 * g + l + 1)
                                mul_t(q, l, S["ta"])
                                mul_tt(q, l, S["tta"])
                            if prev and l == 2:
                                pe.wait_ge(S["u"], gp_ + 1)
                                pe.wait_ge(S["bkt"], gp_ + 1)
                                if not early(cp):
                                    for d in range(2):
                                        o = 256 + d * P
                                        pe.matmul(psX[qp][:, o:o + P], ar[jp][:, d, 1, :], n0[:, jp, d, :],
                                                  start=True, stop=False)
                                        for h in range(2):
                                            u = 2 * d + h
                                            o = 256 + u * HD
                                            pe.matmul(psX[qp][:, o:o + HD], rkT[qp][:, u, :],
                                                      vs[jp][:, d, h * HD:(h + 1) * HD], start=False, stop=False)
                                            pe.matmul(psX[qp][:, o:o + HD], rbT[qp][:, u, :], un[:, u, :],
                                                      start=False, stop=(h == 1))
                                for d in range(2):
                                    o = psX[qp][:, d * P:(d + 1) * P]
                                    pe.matmul(o, bkt[qp][:, d, 1, :], vs[jp][:, d, :], start=True, stop=False)
                                    last = pe.matmul(o, bkt[qp][:, d, 0, :],
                                                     un[:, 2 * d:2 * d + 2, :].rearrange("p a b -> p (a b)"),
                                                     start=False, stop=True)
                                last.then_inc(S["s3"], 1)
                            if prev and l == 0:
                                pe.wait_ge(S["xeb"], 2 * gp_ + 2)
                                pe.wait_ge(S["tteb"], 2 * gp_ + 1)
                                mul_tt(qp, 5, S["ttb"])
                            if prev and l == 1:
                                pe.wait_ge(S["vp"], gp_ + 1)
                                for u in range(4):
                                    last = pe.matmul(psT[qp][:, u * HD:(u + 1) * HD], invT[qp][:, u, :], un[:, u, :],
                                                     start=True, stop=True)
                                last.then_inc(S["s2"], 1)
                            if c is not None and l == 0:
                                pe.wait_ge(S["gr"], g + 1)
                                for d in range(2):
                                    last = pe.matmul(psG[:, 2, 0, 0, 2 * d:2 * d + 2], rk[:, d, :], rkm[:, j, :],
                                                     start=True, stop=True)
                                last.then_inc(S["bonp"], 1)
                            if nxt and l == 0:
                                rates(*nxt)

                    run(pe, group)

                @block.vector
                def _(dve):
                    tri = const(cst, "tri").rearrange("p (d z t) -> p d z t", d=2, z=2)
                    pairm = const(cst, "pair").rearrange("p (d t) -> p d t", d=2)
                    lev = const(cst, "level").rearrange("p (l d i) -> p l d i", l=NL, d=2)
                    for q in range(2):
                        for m in (akT, rbT, rkT):
                            last = dve.memset(m[q][:, :, :], 0.0)
                    last.then_inc(S["init"], 1)
                    dve.wait_ge(S["init"], 2)

                    def keep(dst, z, w, strict):
                        for d in range(2):
                            m = tri[:, d, 0 if strict else 1, :].unsqueeze(1).broadcast_to([P, 2, P]).bitcast(U32)
                            last = dve.copy_predicated(dst[:, 2 * d:2 * d + 2, :], m, psG[:, 2 * d:2 * d + 2, z, w, :])
                        return last

                    def fill(dst, l, side, src, s):
                        dve.sem_inc(S["gate"], 1)
                        o, step = (0, HD) if side == 0 else (HD, -HD)
                        m = bass.AP(lev.tensor, lev[:, l, :, :].offset + o,
                                    [[lev.ap[0][0], P], [step, 2], [0, 2], [LEVELS[l], HD // LEVELS[l]], [1, LEVELS[l]]])
                        dve.copy_predicated(dst, m.bitcast(U32), src).then_inc(s, 1)

                    def x_out(q, l, s):
                        fill(apart(xl[l], l), l, 0, five(psT[q], l, 256), s)

                    def t_out(q, l, s):
                        fill(cols(inv[q], l, 0), l, 0, five(psT[q], l), s)

                    def tt_out(q, l, s):
                        fill(cols(invT[q], l, 1), l, 1, five(psX[q], l, 256), s)

                    def group(c, j, g, prev, nxt):
                        q = None if c is None else j % 2
                        if prev:
                            cp, jp, gp_ = prev
                            qp = jp % 2
                        if c is not None:
                            dve.wait_ge(S["gram"], g + 1)
                            dve.sem_inc(S["gate"], 1)
                            if not (isinstance(g, int) and g < 1):
                                dve.wait_ge(S["lcb"], 2 * g)
                                dve.sem_inc(S["gate"], 1)
                            keep(lT, 0, 0, True).then_inc(S["lt"], 1)
                            dve.wait_ge(S["lt"], g + 1)
                            for d in range(2):
                                last = dve.tensor_tensor(invT[q][:, 2 * d:2 * d + 2, :], lT[:, 2 * d:2 * d + 2, :],
                                                         pairm[:, d, :].unsqueeze(1).broadcast_to([P, 2, P]), ALU.mult)
                            last.then_inc(S["tt2"], 1)
                        if prev:
                            dve.wait_ge(S["xb"], 2 * gp_ + 1)
                            x_out(qp, 4, S["xeb"])
                        if c is not None:
                            last = keep(akT[q], 1, 0, True)
                            if not early(c):
                                keep(rbT[q], 0, 1, False)
                                last = keep(rkT[q], 1, 1, False)
                            last.then_inc(S["gr"], 1)
                        if prev:
                            dve.wait_ge(S["tb"], gp_ + 1)
                            t_out(qp, 4, S["teb"])
                            dve.wait_ge(S["ttb"], 2 * gp_ + 1)
                            tt_out(qp, 4, S["tteb"])
                        for l in range(4):
                            if c is not None:
                                dve.wait_ge(S["xa"], 4 * g + l + 1)
                                x_out(q, l, S["xea"])
                            if prev and l == 0:
                                dve.wait_ge(S["xb"], 2 * gp_ + 2)
                                x_out(qp, 5, S["xeb"])
                            if prev and l == 1:
                                dve.wait_ge(S["s1"], gp_ + 1)
                                dve.tensor_copy(un[:, :, :], psX[qp][:, 0:256].rearrange("p (u i) -> p u i", u=4)).then_inc(S["vp"], 1)
                            if prev and l == 3:
                                dve.wait_ge(S["s3"], gp_ + 1)
                                dve.tensor_tensor(n0[:, jp, :, :], psX[qp][:, 0:2 * P].rearrange("p (d i) -> p d i", d=2),
                                                  n0[:, jp, :, :], ALU.add).then_inc(S["dch"], 1)
                                if not early(cp):
                                    if not (isinstance(gp_, int) and gp_ < TC * J + 1):
                                        dve.wait_ge(s_y, 32 * (gp_ - TC * J))
                                    dve.tensor_copy(yst[:, :, :], psX[qp][:, 256:512].rearrange("p (u i) -> p u i", u=4)).then_inc(S["y"], 1)
                                dve.wait_ge(S["dch"], gp_ + 1)
                                if isinstance(cp, int) and cp == TT - 1:
                                    dve.nop().then_inc(S["n"], 1)
                                else:
                                    at = where(cp)
                                    for d in range(2):
                                        last = dve.scalar_tensor_tensor(
                                            out=n0[:, jp, d, :], in0=n0[:, jp, d, :],
                                            scalar=em2f[:, bass.ds((d * J + jp) * TT + at[d], 1)],
                                            in1=headblock, op0=ALU.mult, op1=ALU.mult)
                                    last.then_inc(S["n"], 1)
                            if c is not None:
                                dve.wait_ge(S["ta"], 4 * g + l + 1)
                                t_out(q, l, S["tea"])
                                dve.wait_ge(S["tta"], 4 * g + l + 1)
                                tt_out(q, l, S["ttea"])
                            if prev and l == 0:
                                dve.wait_ge(S["ttb"], 2 * gp_ + 2)
                                tt_out(qp, 5, S["tteb"])
                            if c is not None and l == 0:
                                dve.wait_ge(S["bonp"], g + 1)
                                if early(c):
                                    dve.nop().then_inc(S["bone"], 1)
                                else:
                                    at = where(c)
                                    for d in range(2):
                                        last = dve.tensor_copy(bonf[:, bass.ds(d * TL * 8 + (at[d] - TC) * 8 + 2 * j, 2)],
                                                               psG[:, 2, 0, 0, 2 * d:2 * d + 2])
                                    last.then_inc(S["bone"], 1)

                    run(dve, group)

                @block.scalar
                def _(act):
                    def decays(c, j, g):
                        at = where(c)
                        if not (isinstance(g, int) and g < 1):
                            act.wait_ge(S["prep"], g)
                        for d in range(2):
                            o = (d * J + j) * TT * CH + at[d] * CH
                            i = (d * J + j) * TT + at[d]
                            act.activation(e1[:, d, :], cumf[:, bass.ds(o, CH)], ACT.Exp, scale=-KAPPA,
                                           bias=kmf[:, bass.ds(i, 1)])
                            last = act.activation(e2[:, d, :], cumf[:, bass.ds(o + (1 - d), P)], ACT.Exp, scale=KAPPA,
                                                  bias=kmf[:, bass.ds(2 * J * TT + i, 1)])
                        last.then_inc(S["ex"], 1)

                    def rates(c, j, g):
                        act.wait_ge(S["amm"], g + 1)
                        for d in range(2):
                            last = act.activation(ag[:, d, :], psG[:, d, 0, 0, :], ACT.Sigmoid,
                                                  bias=vec3[:, 8 + 4 * d + j:9 + 4 * d + j])
                        last.then_inc(S["sig"], 1)

                    def mix(dst, src, l, s, scale=1.0):
                        o = dst[:, :, :].rearrange("p h (b e i) -> p h b e i", e=2, i=LEVELS[l])
                        act.activation(o, mixed(src, l), ACT.Copy, scale=scale).then_inc(s, 1)

                    decays(0, 0, 0)
                    rates(0, 0, 0)

                    def group(c, j, g, prev, nxt):
                        q = None if c is None else j % 2
                        if prev:
                            cp, jp, gp_ = prev
                            qp = jp % 2
                        if nxt:
                            decays(*nxt)
                        if c is not None:
                            act.wait_ge(S["kt"], g + 1)
                            act.activation(bkt[q][:, :, :, :].rearrange("p a b c -> p (a b c)"), psT[q][:, :], ACT.Copy).then_inc(S["bkt"], 1)
                            start = isinstance(g, int) and g < 1
                            act.wait_ge(S["lt"], g + 1)
                            if not start:
                                act.wait_ge(S["xa"], 4 * g - 1)
                            mix(lc[0], lT, 0, S["lca"], -1.0)
                            act.wait_ge(S["tt2"], g + 1)
                            if not start:
                                act.wait_ge(S["ta"], 4 * g - 3)
                            mix(tc[0], invT[q], 0, S["tca"])
                            act.wait_ge(S["t2"], g + 1)
                            act.activation(inv[q][:, :, :].rearrange("p a b -> p (a b)"), psX[q][:, :], ACT.Copy).then_inc(S["t2e"], 1)
                        for l in range(4):
                            if c is not None:
                                if l < 3:
                                    if l == 1:
                                        act.wait_ge(S["xa"], 4 * g + 1)
                                    elif not start:
                                        if l == 0:
                                            act.wait_ge(S["xb"], 2 * g)
                                        else:
                                            act.wait_ge(S["xa"], 4 * g)
                                    mix(lc[l + 1], lT, l + 1, S["lca"], -1.0)
                                if l == 1:
                                    if not start:
                                        act.wait_ge(S["xb"], 2 * g - 1)
                                    mix(lc[4], lT, 4, S["lcb"], -1.0)
                                if l == 2:
                                    act.wait_ge(S["xa"], 4 * g + 2)
                                    mix(lc[5], lT, 5, S["lcb"], -1.0)
                                act.wait_ge(S["ttea"], 4 * g + l + 1)
                                if not start:
                                    act.wait_ge(S["ta" if l < 3 else "tb"], 4 * g + l - 2 if l < 3 else g)
                                mix(tc[l + 1], invT[q], l + 1, S["tca" if l < 3 else "tcb"])
                            if prev and l == 1:
                                act.wait_ge(S["s2"], gp_ + 1)
                                act.activation(un[:, :, :], psT[qp][:, 0:256].rearrange("p (u i) -> p u i", u=4),
                                               ACT.Copy, scale=-1.0).then_inc(S["u"], 1)
                            if nxt and l == 0:
                                rates(*nxt)

                    run(act, group)

                @block.sync
                def _(sp):
                    def group(c, j, g, prev, nxt):
                        if prev and not early(prev[0]):
                            cp, jp, gp_ = prev
                            at = where(cp)
                            sp.wait_ge(S["y"], gp_ - TC * J + 1)
                            for d, y in enumerate(("yf", "yb")):
                                sp.dma_start(scratch[y][bass.ds((at[d] - TC) * P, P), jp * P:(jp + 1) * P],
                                             yst[:, 2 * d:2 * d + 2, :].rearrange("p a b -> p (a b)")).then_inc(s_y, 16)

                    run(sp, group)
                    sp.wait_ge(s_y, 32 * TL * J)

        x1 = sb(top, "x1", [P, TL, D])
        g2row = sb(top, "g2row", [P, D])
        logit = sb(top, "logit", [P, TL, 36])
        with ExitStack() as c6:
            wo = sb(c6, "wo", [P, KT, D])
            sgb = sb(c6, "sgb", [P, NTOK])
            og = sb(c6, "og", [P, BW])
            lnx = sb(c6, "lnx", [P, 2, BW])
            g1row, r2row, s2row = (sb(c6, n, [P, D]) for n in ("g1row", "r2row", "s2row"))
            g1c, g2c, r2c = (sb(c6, n, [P, KT]) for n in ("g1c", "g2c", "r2c"))
            diag = [sb(c6, f"diag{i}", [P, 4, P]) for i in range(2)]
            wrt = sb(c6, "wrt", [P, KT, 36])
            brt = sb(c6, "brt", [P, 36])
            yin = [sb(c6, f"yin{i}", [P, 2, BW]) for i in range(2)]
            oin = [sb(c6, f"oin{i}", [P, BW]) for i in range(2)]
            bv = sb(c6, "bv", [P, BW])
            sq6 = sb(c6, "sq6", [P, BW])
            sqj6 = sb(c6, "sqj6", [P, D])
            st6 = sb(c6, "st6", [P, 6, 8])
            rs6 = sb(c6, "rs6", [P, TL, 8])
            bs = sb(c6, "bs", [P, TL, 8])
            oT = [sb(c6, f"oT{i}", [P, KT, P]) for i in range(2)]
            h2 = [sb(c6, f"h2_{i}", [P, D]) for i in range(2)]
            h2T = sb(c6, "h2T", [P, KT, P])
            psA = pb(c6, "ps6A", [P, BW])
            psO = pb(c6, "ps6O", [P, KT, P])
            psY = pb(c6, "ps6Y", [P, 2, 512])
            psH = pb(c6, "ps6H", [P, KT, P])
            psL = pb(c6, "ps6L", [P, 36])
            S = {n: sem(c6, f"s6_{n}") for n in (
                "par", "wo", "row", "diag", "rps", "gate", "std1", "var1", "ob", "tr", "oT", "y", "std2", "x1a",
                "x1", "std3", "h2", "tr2", "h2T", "lg", "lge", "ch", "bv", "pch", "sqa", "ysum")}
            s_yin = [sem(c6, f"s6_yin{i}") for i in range(2)]
            s_xin = sem(c6, "s6_xin")
            s_st = [sem(c6, f"s6_st{i}") for i in range(2)]
            block = c6.enter_context(nc.Block())
            NPAR = 8

            @block.sync
            def _(sp):
                sp.dma_start(sgb[:, :], scratch["sg"]).then_inc(S["par"], 16)
                sp.dma_start(og[:, :], a["outgate_up"][0]).then_inc(S["par"], 16)
                for i, n in enumerate(("lnx_g", "lnx_b")):
                    sp.dma_start(lnx[:, i, :], bass.AP(a[n].tensor, 0, [[0, P], [1, BW]])).then_inc(S["par"], 16)
                sp.dma_start(wrt[:, :, 0:4], a["w_router_grp"][0].rearrange("(k p) n -> p k n", p=P)).then_inc(S["par"], 16)
                sp.dma_start(wrt[:, :, 4:36], a["w_router_exp"][0].rearrange("(k p) n -> p k n", p=P)).then_inc(S["par"], 16)
                sp.dma_start(brt[:, 0:4], bass.AP(a["b_router_grp"].tensor, 0, [[0, P], [1, 4]])).then_inc(S["par"], 16)
                sp.dma_start(brt[:, 4:36], bass.AP(a["b_router_exp"].tensor, 0, [[0, P], [1, 32]])).then_inc(S["par"], 16)
                for t in range(TL):
                    if t >= 2:
                        sp.wait_ge(S["tr"], t - 1)
                    rows = slice(t * P, (t + 1) * P)
                    for dst, src in ((yin[t % 2][:, 0, :], "yf"), (yin[t % 2][:, 1, :], "yb"), (oin[t % 2][:, :], "oA")):
                        sp.dma_start(dst, scratch[src][rows, :]).then_inc(s_yin[t % 2], 16)
                    if t == 1:
                        sp.dma_start(wo[:, :, :], a["w_out"][0].rearrange("(k p) n -> p k n", p=P)).then_inc(S["wo"], 16)
                        sp.dma_start(x1[:, :, :], a["x"][0].rearrange("(t p) d -> p t d", p=P)).then_inc(s_xin, 16)

            @block.gpsimd
            def _(gp):
                gp.tensor_tensor(bs[:, :, :], bon[:, 0, :, :], bon[:, 1, :, :], ALU.add).then_inc(S["pch"], 1)
                gp.wait_ge(S["pch"], 1)

                def bonus(t):
                    y = yin[t % 2][:, 0, :]
                    gp.wait_ge(s_yin[t % 2], 48 * (t // 2 + 1))
                    gp.tensor_tensor(y, y, yin[t % 2][:, 1, :], ALU.add).then_inc(S["ysum"], 1)
                    if t:
                        gp.wait_ge(S["ob"], t)
                    gp.tensor_tensor(bv[:, :].rearrange("p (h d) -> p h d", h=8),
                                     vt[:, TC + t, :].rearrange("p (h d) -> p h d", h=8),
                                     bs[:, t, :].unsqueeze(2).broadcast_to([P, 8, HD]), ALU.mult).then_inc(S["pch"], 1)
                    gp.wait_ge(S["pch"], t + 2)
                    gp.tensor_tensor(bv[:, :], bv[:, :], lnx[:, 1, :], ALU.add).then_inc(S["bv"], 1)

                gp.wait_ge(S["par"], 16 * NPAR)
                for t in range(TL):
                    bonus(t)

            @block.tensor
            def _(pe):
                for n in range(8):
                    pe.wait_ge(S["diag"], n + 1)
                    if n >= 2:
                        pe.wait_ge(S["row"], n - 1)
                    pe.matmul(psY[:, n % 2, :], ones, diag[n % 2][:, :, :].rearrange("p a b -> p (a b)"),
                              start=True, stop=True).then_inc(S["rps"], 1)
                pe.wait_ge(S["par"], 16 * NPAR)

                def turn(t):
                    if t:
                        pe.wait_ge(S["ob"], t)
                    pe.matmul(psA[:, :], sgb[:, CTX + t * P:CTX + (t + 1) * P], og[:, :], start=True,
                              stop=True).then_inc(S["gate"], 1)
                    pe.wait_ge(s_yin[t % 2], 48 * (t // 2 + 1))
                    if t:
                        pe.wait_ge(S["oT"], t)
                    for k in range(4):
                        pe.transpose(psO[:, k, :], oin[t % 2][:, k * P:(k + 1) * P], ident)
                    pe.wait_ge(S["ob"], t + 1)
                    for k in range(4):
                        last = pe.transpose(psO[:, 4 + k, :], yin[t % 2][:, 0, k * P:(k + 1) * P], ident)
                    last.then_inc(S["tr"], 1)

                def project(t):
                    pe.wait_ge(S["oT"], t + 1)
                    if t == 0:
                        pe.wait_ge(S["wo"], 16)
                        pe.wait_ge(S["row"], 8)
                    else:
                        pe.wait_ge(S["x1a"], t)
                    for n in range(2):
                        for k in range(KT):
                            last = pe.matmul(psY[:, n, :], oT[t % 2][:, k, :], wo[:, k, n * 512:(n + 1) * 512],
                                             start=(k == 0), stop=(k == KT - 1))
                    last.then_inc(S["y"], 1)

                def turn_h2(t):
                    pe.wait_ge(S["h2"], t + 1)
                    if t:
                        pe.wait_ge(S["h2T"], t)
                    for k in range(KT):
                        last = pe.transpose(psH[:, k, :], h2[t % 2][:, k * P:(k + 1) * P], ident)
                    last.then_inc(S["tr2"], 1)

                def route(t):
                    pe.wait_ge(S["h2T"], t + 1)
                    if t:
                        pe.wait_ge(S["lge"], t)
                    for k in range(KT):
                        last = pe.matmul(psL[:, :], h2T[:, k, :], wrt[:, k, :], start=(k == 0), stop=(k == KT - 1))
                    last.then_inc(S["lg"], 1)

                turn(0)
                for t in range(TL):
                    project(t)
                    if t:
                        turn_h2(t - 1)
                    if t + 1 < TL:
                        turn(t + 1)
                    if t:
                        route(t - 1)
                turn_h2(TL - 1)
                route(TL - 1)

            @block.scalar
            def _(act):
                for n in range(8):
                    act.wait_ge(S["rps"], n + 1)
                    dst = (g1row, r2row, s2row, g2row)[n // 2]
                    act.activation(dst[:, (n % 2) * 512:(n % 2) * 512 + 512], psY[:, n % 2, :], ACT.Copy).then_inc(S["row"], 1)

                def pre(t):
                    act.wait_ge(S["var1"], t + 1)
                    act.activation(st6[:, 2, :], st6[:, 1, :], ACT.Sqrt, scale=1.0 / HD, bias=eps[:, 2:3]).then_inc(S["std1"], 1)

                def turned(t):
                    act.wait_ge(S["tr"], t + 1)
                    if t >= 2:
                        act.wait_ge(S["y"], t - 1)
                    act.activation(oT[t % 2][:, :, :], psO[:, :, :], ACT.Copy).then_inc(S["oT"], 1)

                def post(t):
                    act.wait_ge(S["y"], t + 1)
                    act.activation(sqj6[:, :], psY[:, :, :].rearrange("p a b -> p (a b)"), ACT.Square,
                                   accum_out=rs6[:, t, 0:1]).then_inc(S["sqa"], 1)
                    act.wait_ge(S["sqa"], 2 * t + 1)
                    act.activation(rs6[:, t, 1:2], rs6[:, t, 0:1], ACT.Sqrt, scale=1.0 / D, bias=eps[:, 0:1]).then_inc(S["std2"], 1)

                def post2(t):
                    act.wait_ge(S["x1"], t + 1)
                    act.activation(sqj6[:, :], x1[:, t, :], ACT.Square, accum_out=rs6[:, t, 3:4]).then_inc(S["sqa"], 1)
                    act.wait_ge(S["sqa"], 2 * t + 2)
                    act.activation(rs6[:, t, 4:5], rs6[:, t, 3:4], ACT.Sqrt, scale=1.0 / D, bias=eps[:, 0:1]).then_inc(S["std3"], 1)

                def feat(t):
                    act.wait_ge(S["h2"], t + 1)
                    act.wait_ge(S["tr2"], t + 1)
                    if t:
                        act.wait_ge(S["lg"], t)
                    act.activation(h2T[:, :, :], psH[:, :, :], ACT.Copy).then_inc(S["h2T"], 1)
                    act.dma_start(scratch["h2"][t * P:(t + 1) * P, :], h2[t % 2][:, :]).then_inc(s_st[t % 2], 16)

                pre(0)
                turned(0)
                pre(1)
                for t in range(TL):
                    post(t)
                    if t:
                        feat(t - 1)
                    if t + 1 < TL:
                        turned(t + 1)
                    post2(t)
                    if t + 2 < TL:
                        pre(t + 2)
                feat(TL - 1)
                for i in range(2):
                    act.wait_ge(s_st[i], 16 * TL // 2)

            @block.vector
            def _(dve):
                ch = Chain(dve, S["ch"])
                dve.tensor_tensor(g1c[:, :], mod[:, GT1:GT1 + KT, 0], vec1[:, 56:64], ALU.mult)
                dve.tensor_tensor(g2c[:, :], mod[:, GT2:GT2 + KT, 0], vec1[:, 72:80], ALU.mult)
                ch.link(dve.scalar_tensor_tensor(out=r2c[:, :], in0=mod[:, SC2:SC2 + KT, 0], scalar=1.0, in1=vec1[:, 64:72],
                                                 op0=ALU.add, op1=ALU.mult))
                for n in range(8):
                    if n >= 2:
                        dve.wait_ge(S["rps"], n - 1)
                    for i in range(4):
                        k = 4 * (n % 2) + i
                        v = (g1c[:, k:k + 1], r2c[:, k:k + 1], mod[:, SH2 + k, 0:1], g2c[:, k:k + 1])[n // 2]
                        last = dve.tensor_scalar(diag[n % 2][:, i, :], ident, v, None, ALU.mult)
                    last.then_inc(S["diag"], 1)
                dve.wait_ge(S["par"], 16 * NPAR)

                def heads(ap):
                    return ap.rearrange("p (h d) -> p h d", h=8)

                def over(ap):
                    return ap.unsqueeze(2).broadcast_to([P, 8, HD])

                def pre(t):
                    y = yin[t % 2][:, 0, :]
                    dve.wait_ge(S["ysum"], t + 1)
                    ch.link(dve.reduce_sum(st6[:, 0, :], heads(y), AX.X))
                    ch.link(dve.tensor_scalar(st6[:, 0, :], st6[:, 0, :], 1.0 / HD, None, ALU.mult))
                    ch.link(dve.tensor_tensor(heads(y), heads(y), over(st6[:, 0, :]), ALU.subtract))
                    ch.link(dve.tensor_tensor(sq6[:, :], y, y, ALU.mult))
                    dve.reduce_sum(st6[:, 1, :], heads(sq6[:, :]), AX.X).then_inc(S["var1"], 1)

                def scaled(t):
                    y = yin[t % 2][:, 0, :]
                    dve.wait_ge(S["std1"], t + 1)
                    ch.link(dve.reciprocal(st6[:, 3, :], st6[:, 2, :]))
                    ch.link(dve.tensor_tensor(heads(y), heads(y), over(st6[:, 3, :]), ALU.mult))
                    ch.link(dve.tensor_tensor(y, y, lnx[:, 0, :], ALU.mult))
                    dve.wait_ge(S["bv"], t + 1)
                    ch.link(dve.tensor_tensor(y, y, bv[:, :], ALU.add))
                    dve.wait_ge(S["gate"], t + 1)
                    dve.tensor_tensor(y, y, psA[:, :], ALU.mult).then_inc(S["ob"], 1)

                def post(t):
                    dve.wait_ge(S["std2"], t + 1)
                    ch.link(dve.reciprocal(rs6[:, t, 2:3], rs6[:, t, 1:2]))
                    if t >= 2:
                        dve.wait_ge(S["tr2"], t - 1)
                        dve.wait_ge(s_st[t % 2], 16 * (t // 2))
                    dve.scalar_tensor_tensor(out=h2[t % 2][:, :], in0=psY[:, :, :].rearrange("p a b -> p (a b)"),
                                             scalar=rs6[:, t, 2:3], in1=g1row[:, :], op0=ALU.mult,
                                             op1=ALU.mult).then_inc(S["x1a"], 1)
                    dve.wait_ge(S["x1a"], t + 1)
                    if t == 0:
                        dve.wait_ge(s_xin, 16)
                    dve.tensor_tensor(x1[:, t, :], x1[:, t, :], h2[t % 2][:, :], ALU.add).then_inc(S["x1"], 1)

                def modulated(t):
                    dve.wait_ge(S["std3"], t + 1)
                    ch.link(dve.reciprocal(rs6[:, t, 5:6], rs6[:, t, 4:5]))
                    ch.link(dve.scalar_tensor_tensor(out=h2[t % 2][:, :], in0=x1[:, t, :], scalar=rs6[:, t, 5:6],
                                                     in1=r2row[:, :], op0=ALU.mult, op1=ALU.mult))
                    dve.tensor_tensor(h2[t % 2][:, :], h2[t % 2][:, :], s2row[:, :], ALU.add).then_inc(S["h2"], 1)

                def logits(t):
                    dve.wait_ge(S["lg"], t + 1)
                    dve.tensor_tensor(logit[:, t, :], psL[:, :], brt[:, :], ALU.add).then_inc(S["lge"], 1)

                pre(0)
                scaled(0)
                pre(1)
                for t in range(TL):
                    if t + 1 < TL:
                        scaled(t + 1)
                    post(t)
                    if t:
                        logits(t - 1)
                    if t + 2 < TL:
                        pre(t + 2)
                    modulated(t)
                logits(TL - 1)

        NT = NE + NOVER
        pairw = sb(top, "pairw", [P, 2, TL])
        idxg = sb(top, "idxg", [P, NT], U32)
        idxs = sb(top, "idxs", [P, NT], U32)
        over = sb(top, "over", [1, NOVER + 1], I32)
        R = 4
        moe = ExitStack()
        wgu = [sb(moe, f"wgu{i}", [P, 2, KT, DE]) for i in range(R)]
        wd = [sb(moe, f"wd{i}", [P, 2, D]) for i in range(R)]
        hg = [sb(moe, f"hg{i}", [P, D]) for i in range(R)]
        s_w = [sem(moe, f"s8_w{i}") for i in range(R)]
        s_wd = [sem(moe, f"s8_wd{i}") for i in range(R)]
        weights = {n: a[n].rearrange("l e r n -> (l e r) n") for n in ("w_gate", "w_up", "w_down")}

        def rows_of(name, e, per):
            r = D if per == KT else DE
            return weights[name][bass.ds(e * r, r), :].rearrange("(p k) n -> p k n", k=per)

        def load_gate_up(sp, e, b, s):
            sp.dma_start(wgu[b][:, 0, :, :], rows_of("w_gate", e, KT)).then_inc(s, 16)
            sp.dma_start(wgu[b][:, 1, :, :], rows_of("w_up", e, KT)).then_inc(s, 16)

        def load_down(sp, e, b, s):
            sp.dma_start(wd[b][:, :, :], rows_of("w_down", e, 2)).then_inc(s, 16)

        with ExitStack() as c7:
            def t7(name, shape, dt=F32):
                return sb(c7, "r_" + name, shape, dt)

            k7 = t7("k7", [P, CONSTS.shape[1] - CAT["slotrow"][0]])
            slotrow, part, erow, tilerow = (const(k7, n, "slotrow") for n in ("slotrow", "partition", "erow", "tilerow"))
            gm, gs, gsm, gex, gsum = t7("gm", [P, TL]), t7("gs", [P, TL, NG]), t7("gsm", [P, TL]), t7("gex", [P, TL, NG]), t7("gsum", [P, TL])
            goh = t7("goh", [P, TL, NG])
            down = t7("down", [P, EPG])
            pick = t7("pick", [P, TL, NG, EPG])
            sel = t7("sel", [P, TL, EPG])
            em_ = t7("em", [P, 2, TL])
            sc, scm = t7("sc", [P, TL, EPG]), t7("scm", [P, TL])
            eoh = t7("eoh", [P, 2, TL, EPG])
            ohk = t7("ohk", [P, 2, TL, NE])
            oh = t7("oh", [P, TL, NE])
            rank = t7("rank", [P, TL, NE])
            tmp = t7("tmp", [P, 2, TL, NE])
            cnt, ov, ovi, ovb = (t7(n, [P, NE]) for n in ("cnt", "ov", "ovi", "ovb"))
            rk_, q_, sl, eid, bs_, til, any_, pid = (t7(n, [P, 2, TL]) for n in ("rk", "q", "sl", "eid", "bs", "til", "any", "pid"))
            asl = [t7(f"asl{i}", [P, P]) for i in range(2)]
            btl = [t7(f"btl{i}", [P, NT]) for i in range(2)]
            lst, pad, tok = (t7(n, [P, NT]) for n in ("lst", "pad", "tok"))
            ovt, ovt2 = t7("ovt", [1, NOVER, NE]), t7("ovt2", [1, NOVER, NE])
            ovid = t7("ovid", [1, NOVER + 1])
            psR = pb(c7, "ps7R", [P, TL, NE])
            psC = pb(c7, "ps7C", [P, NE])
            psP = pb(c7, "ps7P", [P, NT])
            s_k7, s_ch, s_ex, s_exd, s_oh, s_rk, s_ab, s_pp = (sem(c7, "s7_" + n) for n in ("k7", "ch", "ex", "exd", "oh", "rk", "ab", "pp"))
            block = c7.enter_context(nc.Block())

            @block.sync
            def _(sp):
                sp.dma_start(k7[:, :], a["consts"][:, CAT["slotrow"][0]:]).then_inc(s_k7, 16)
                for b in range(R):
                    load_gate_up(sp, b, b, s_w[b])
                    load_down(sp, b, b, s_wd[b])

            @block.gpsimd
            def _(gp):
                for b in range(R):
                    gp.memset(hg[b][:, :], 0.0)

            @block.scalar
            def _(act):
                act.wait_ge(s_ex, 1)
                act.activation(gex[:, :, :], gex[:, :, :], ACT.Exp).then_inc(s_exd, 1)
                act.wait_ge(s_ex, 2)
                act.activation(em_[:, 1, :], em_[:, 1, :], ACT.Exp).then_inc(s_exd, 1)

            @block.tensor
            def _(pe):
                pe.wait_ge(s_oh, 1)
                tri0 = const(cst, "tri")[:, 0:P]
                for t in range(TL):
                    pe.matmul(psR[:, t, :], tri0, oh[:, t, :], start=True, stop=(t == 0))
                    for s in range(t):
                        pe.matmul(psR[:, t, :], ones, oh[:, s, :], start=False, stop=(s == t - 1))
                for t in range(TL):
                    last = pe.matmul(psC[:, :], ones, oh[:, t, :], start=(t == 0), stop=(t == TL - 1))
                last.then_inc(s_rk, 1)
                for n in range(2 * TL):
                    pe.wait_ge(s_ab, n + 1)
                    pe.matmul(psP[:, :], asl[n % 2][:, :], btl[n % 2][:, :], start=(n == 0),
                              stop=(n == 2 * TL - 1)).then_inc(s_pp, 1)

            @block.vector
            def _(dve):
                ch = Chain(dve, s_ch)
                dve.wait_ge(s_k7, 16)

                def spread(ap, shape, axis):
                    return ap.unsqueeze(axis).broadcast_to(shape)

                def first_max(dst, src, best, score, smax, n):
                    w = [P, TL, n]
                    ch.link(dve.tensor_reduce(best, src, AX.X, ALU.max))
                    ch.link(dve.tensor_tensor(score, src, spread(best, w, 2), ALU.is_equal))
                    ch.link(dve.tensor_tensor(score, score, spread(down[:, 0:n] if n == EPG else down[:, 4:8], w, 1), ALU.mult))
                    ch.link(dve.tensor_reduce(smax, score, AX.X, ALU.max))
                    ch.link(dve.tensor_tensor(dst, score, spread(smax, w, 2), ALU.is_equal))

                ch.link(dve.tensor_scalar(down[:, :], erow[:, 0:EPG], -1.0, float(EPG), ALU.mult, ALU.add))
                lg = logit[:, :, 0:NG]
                first_max(goh[:, :, :], lg, gm[:, :], gs[:, :, :], gsm[:, :], NG)
                dve.tensor_tensor(gex[:, :, :], lg, spread(gm[:, :], [P, TL, NG], 2), ALU.subtract).then_inc(s_ex, 1)
                le = logit[:, :, NG:].rearrange("p t (g e) -> p t g e", g=NG)
                ch.link(dve.tensor_tensor(pick[:, :, :, :], le, spread(goh[:, :, :], [P, TL, NG, EPG], 3), ALU.mult))
                ch.link(dve.tensor_reduce(sel[:, :, :], pick[:, :, :, :].rearrange("p t g e -> p t e g"), AX.X, ALU.add))
                first_max(eoh[:, 0, :, :], sel[:, :, :], em_[:, 0, :], sc[:, :, :], scm[:, :], EPG)
                ch.link(dve.scalar_tensor_tensor(out=sel[:, :, :], in0=eoh[:, 0, :, :], scalar=-1e30, in1=sel[:, :, :],
                                                 op0=ALU.mult, op1=ALU.add))
                first_max(eoh[:, 1, :, :], sel[:, :, :], em_[:, 1, :], sc[:, :, :], scm[:, :], EPG)
                ch.link(dve.tensor_tensor(em_[:, 1, :], em_[:, 1, :], em_[:, 0, :], ALU.subtract))
                dve.tensor_copy(em_[:, 0, :], em_[:, 0, :]).then_inc(s_ex, 1)
                for k in range(2):
                    last = dve.tensor_tensor(ohk[:, k, :, :].rearrange("p t (g e) -> p t g e", g=NG),
                                             spread(goh[:, :, :], [P, TL, NG, EPG], 3),
                                             spread(eoh[:, k, :, :], [P, TL, NG, EPG], 2), ALU.mult)
                ch.link(last)
                dve.tensor_tensor(oh[:, :, :], ohk[:, 0, :, :], ohk[:, 1, :, :], ALU.add).then_inc(s_oh, 1)
                dve.wait_ge(s_exd, 2)
                ch.link(dve.tensor_reduce(gsum[:, :], gex[:, :, :], AX.X, ALU.add))
                ch.link(dve.tensor_scalar(gm[:, :], em_[:, 1, :], 1.0, None, ALU.add))
                ch.link(dve.tensor_tensor(gsum[:, :], gsum[:, :], gm[:, :], ALU.mult))
                ch.link(dve.reciprocal(pairw[:, 0, :], gsum[:, :]))
                ch.link(dve.tensor_tensor(pairw[:, 1, :], pairw[:, 0, :], em_[:, 1, :], ALU.mult))
                dve.wait_ge(s_rk, 1)
                dve.tensor_copy(rank[:, :, :], psR[:, :, :])
                ch.link(dve.tensor_copy(cnt[:, :], psC[:, :]))

                def chosen(dst, src):
                    ch.link(dve.tensor_tensor(tmp[:, :, :, :], ohk[:, :, :, :], src, ALU.mult))
                    ch.link(dve.tensor_reduce(dst, tmp[:, :, :, :], AX.X, ALU.add))

                full = [P, 2, TL, NE]
                chosen(rk_[:, :, :], spread(rank[:, :, :], full, 1))
                ch.link(dve.tensor_scalar(q_[:, :, :], rk_[:, :, :], float(CAP), None, ALU.is_ge))
                ch.link(dve.tensor_scalar(ov[:, :], cnt[:, :], float(CAP), None, ALU.is_gt))
                for j in range(2, (SEQ + CAP - 1) // CAP):
                    dve.scalar_tensor_tensor(out=q_[:, :, :], in0=rk_[:, :, :], scalar=float(CAP * j), in1=q_[:, :, :],
                                             op0=ALU.is_ge, op1=ALU.add)
                    ch.link(dve.scalar_tensor_tensor(out=ov[:, :], in0=cnt[:, :], scalar=float(CAP * j), in1=ov[:, :],
                                                     op0=ALU.is_gt, op1=ALU.add))
                ch.link(dve.scalar_tensor_tensor(out=sl[:, :, :], in0=q_[:, :, :], scalar=-float(CAP), in1=rk_[:, :, :],
                                                 op0=ALU.mult, op1=ALU.add))
                ch.link(dve.tensor_tensor_scan(ovi[:, :], ones[:, 0:NE], ov[:, :], 0.0, ALU.mult, ALU.add))
                ch.link(dve.tensor_tensor(ovb[:, :], ovi[:, :], ov[:, :], ALU.subtract))
                chosen(bs_[:, :, :], ovb[:, :].unsqueeze(1).unsqueeze(1).broadcast_to(full))
                chosen(eid[:, :, :], erow.unsqueeze(1).unsqueeze(1).broadcast_to(full))
                dve.tensor_scalar(any_[:, :, :], q_[:, :, :], 1.0, None, ALU.is_ge)
                ch.link(dve.tensor_tensor(til[:, :, :], bs_[:, :, :], q_[:, :, :], ALU.add))
                ch.link(dve.scalar_tensor_tensor(out=til[:, :, :], in0=til[:, :, :], scalar=float(NE - 1), in1=eid[:, :, :],
                                                 op0=ALU.add, op1=ALU.subtract))
                ch.link(dve.tensor_tensor(til[:, :, :], til[:, :, :], any_[:, :, :], ALU.mult))
                ch.link(dve.tensor_tensor(til[:, :, :], til[:, :, :], eid[:, :, :], ALU.add))
                for k in range(2):
                    for t in range(TL):
                        last = dve.tensor_scalar(pid[:, k, t:t + 1], part, float(k * SEQ + t * P + 1), None, ALU.add)
                ch.link(last)
                for n in range(2 * TL):
                    k, t = n // TL, n % TL
                    if n >= 2:
                        dve.wait_ge(s_pp, n - 1)
                    dve.tensor_scalar(asl[n % 2][:, :], slotrow, sl[:, k, t:t + 1], None, ALU.is_equal)
                    dve.tensor_scalar(btl[n % 2][:, :], tilerow, til[:, k, t:t + 1], pid[:, k, t:t + 1],
                                      ALU.is_equal, ALU.mult).then_inc(s_ab, 1)
                dve.wait_ge(s_pp, 2 * TL)
                ch.link(dve.tensor_copy(lst[:, :], psP[:, :]))
                ch.link(dve.tensor_scalar(pad[:, :], lst[:, :], 0.0, float(4 * SEQ + 1), ALU.is_equal, ALU.mult))
                ch.link(dve.scalar_tensor_tensor(out=lst[:, :], in0=lst[:, :], scalar=-1.0, in1=pad[:, :], op0=ALU.add, op1=ALU.add))
                ch.link(dve.tensor_scalar(pad[:, :], lst[:, :], float(SEQ), float(-SEQ), ALU.is_ge, ALU.mult))
                ch.link(dve.tensor_tensor(tok[:, :], lst[:, :], pad[:, :], ALU.add))
                dve.tensor_copy(idxs[:, :], lst[:, :])
                ch.link(dve.tensor_copy(idxg[:, :], tok[:, :]))
                w = [1, NOVER, NE]
                jrow = tilerow[0:1, 0:NOVER].unsqueeze(2).broadcast_to(w)
                dve.tensor_tensor(ovt[:, :, :], jrow, ovb[0:1, :].unsqueeze(1).broadcast_to(w), ALU.is_ge)
                ch.link(dve.tensor_tensor(ovt2[:, :, :], jrow, ovi[0:1, :].unsqueeze(1).broadcast_to(w), ALU.is_lt))
                ch.link(dve.tensor_tensor(ovt[:, :, :], ovt[:, :, :], ovt2[:, :, :], ALU.mult))
                ch.link(dve.tensor_tensor(ovt[:, :, :], ovt[:, :, :], erow[0:1, :].unsqueeze(1).broadcast_to(w), ALU.mult))
                dve.tensor_copy(ovid[:, NOVER:], ovi[0:1, NE - 1:NE])
                ch.link(dve.tensor_reduce(ovid[:, 0:NOVER], ovt[:, :, :], AX.X, ALU.add))
                ch.link(dve.tensor_copy(over[:, :], ovid[:, :]))

        with moe, ExitStack() as c8:
            hgT = [sb(c8, f"hgT{i}", [P, KT, P]) for i in range(2)]
            sgt = sb(c8, "sgt", [P, DE])
            hid = [sb(c8, f"hid{i}", [P, DE]) for i in range(2)]
            hidT = [sb(c8, f"hidT{i}", [P, 2, P]) for i in range(2)]
            yo = [sb(c8, f"yo{i}", [P, D]) for i in range(2)]
            ig, is_ = ([sb(c8, f"{n}{i}", [P, 1], U32) for i in range(R)] for n in ("ig", "is"))
            psT = pb(c8, "ps8T", [P, KT, P])
            psG = [pb(c8, f"ps8G{i}", [P, 2, DE]) for i in range(2)]
            psH = pb(c8, "ps8H", [P, 2, P])
            psY = pb(c8, "ps8Y", [P, 2, 512])
            S = {n: sem(c8, f"s8_{n}") for n in (
                "tr", "hgT", "gu", "sil", "hid", "trh", "hidT", "dn", "ya", "yv", "gate", "pg", "ps")}
            s_hg = [sem(c8, f"s8_hg{i}") for i in range(R)]
            s_sc = [sem(c8, f"s8_sc{i}") for i in range(2)]
            tiles = ExitStack()
            block = tiles.enter_context(nc.Block())
            EP = NE // R
            @block.sync
            def _(sp):
                with sp.Fori(1, EP) as i:
                    for b in range(R):
                        e = R * i + b
                        sp.wait_ge(S["gu"], e - R + 1)
                        load_gate_up(sp, e, b, s_w[b])
                        sp.wait_ge(S["dn"], e - R + 1)
                        load_down(sp, e, b, s_wd[b])

            @block.gpsimd
            def _(gp):
                def gather(e, b, first):
                    if not first:
                        gp.wait_ge(S["tr"], e - R + 1)
                        gp.sem_inc(S["gate"], 1)
                    gp.tensor_copy(ig[b][:, :], idxg[:, bass.ds(e, 1)]).then_inc(S["pg"], 1)
                    gp.wait_ge(S["pg"], e + 1)
                    gp.sem_inc(S["gate"], 1)
                    gp.indirect_dma_start(out=hg[b][:, :], out_offset=None, in_=scratch["h2"][:, :],
                                          in_offset=bass.IndirectOffsetOnAxis(ap=ig[b][:, 0:1], axis=0),
                                          bounds_check=SEQ - 1, oob_is_err=False).then_inc(s_hg[b], 16)

                def scatter(i, b, first):
                    e = R * i + b
                    gp.wait_ge(S["ya"], e + 1)
                    gp.wait_ge(S["yv"], e + 1)
                    if not (first and b < 2):
                        gp.wait_ge(s_sc[b % 2], 16 * (R // 2 * i + b // 2))
                    gp.sem_inc(S["gate"], 1)
                    gp.tensor_copy(is_[b % 2][:, :], idxs[:, bass.ds(e, 1)]).then_inc(S["ps"], 1)
                    gp.wait_ge(S["ps"], e + 1)
                    gp.sem_inc(S["gate"], 1)
                    gp.indirect_dma_start(out=scratch["ypair"][:, :],
                                          out_offset=bass.IndirectOffsetOnAxis(ap=is_[b % 2][:, 0:1], axis=0),
                                          in_=yo[b % 2][:, :], in_offset=None, bounds_check=2 * SEQ - 1,
                                          oob_is_err=False).then_inc(s_sc[b % 2], 16)

                for b in range(R - 1):
                    gather(b, b, True)

                def ring(i, first, last):
                    for b in range(R):
                        if not (last and b):
                            gather(R * i + b + R - 1, (b + R - 1) % R, first and b == 0)
                        scatter(i, b, first)

                ends(gp, EP, ring)
                for b in range(2):
                    gp.wait_ge(s_sc[b], 8 * NE)

            @block.tensor
            def _(pe):
                def turn(i, b, first):
                    e = R * i + b
                    pe.wait_ge(s_hg[b], 16 * (i + 1))
                    if not (first and b == 0):
                        pe.wait_ge(S["hgT"], e)
                    for k in range(KT):
                        last = pe.transpose(psT[:, k, :], hg[b][:, k::KT], ident)
                    last.then_inc(S["tr"], 1)

                def down(i, b, first):
                    e = R * i + b
                    pe.wait_ge(S["hidT"], e + 1)
                    pe.wait_ge(s_wd[b], 16 * (i + 1))
                    if not (first and b == 0):
                        pe.wait_ge(S["ya"], e)
                        pe.wait_ge(S["yv"], e)
                    for n in range(2):
                        for f in range(2):
                            last = pe.matmul(psY[:, n, :], hidT[b % 2][:, f, :], wd[b][:, f, n * 512:(n + 1) * 512],
                                             start=(f == 0), stop=(f == 1))
                    last.then_inc(S["dn"], 1)

                def ring(i, first, last_pass):
                    for b in range(R):
                        e = R * i + b
                        pe.wait_ge(S["hgT"], e + 1)
                        pe.wait_ge(s_w[b], 32 * (i + 1))
                        if not (first and b < 2):
                            pe.wait_ge(S["hid"], e - 1)
                        for k in range(KT):
                            last = pe.matmul(psG[b % 2][:, :, :], hgT[b % 2][:, k, :], wgu[b][:, :, k, :],
                                             start=(k == 0), stop=(k == KT - 1))
                        last.then_inc(S["gu"], 1)
                        if b:
                            down(i, b - 1, first)
                        elif not first:
                            down(i - 1, R - 1, False)
                        if b < R - 1:
                            turn(i, b + 1, first)
                        elif not last_pass:
                            turn(i + 1, 0, False)
                        pe.wait_ge(S["hid"], e + 1)
                        if not (first and b == 0):
                            pe.wait_ge(S["hidT"], e)
                        for f in range(2):
                            last = pe.transpose(psH[:, f, :], hid[b % 2][:, f::2], ident)
                        last.then_inc(S["trh"], 1)

                turn(0, 0, True)
                ends(pe, EP, ring)
                down(EP - 1, R - 1, False)

            @block.scalar
            def _(act):
                def feat(i, b):
                    act.wait_ge(S["tr"], R * i + b + 1)
                    if not (isinstance(i, int) and i == 0 and b < 2):
                        act.wait_ge(S["gu"], R * i + b - 1)
                    act.activation(hgT[b % 2][:, :, :], psT[:, :, :], ACT.Copy).then_inc(S["hgT"], 1)

                def y_out(i, b, first):
                    act.wait_ge(S["dn"], R * i + b + 1)
                    if not (first and b < 2):
                        act.wait_ge(s_sc[b % 2], 16 * (R // 2 * i + b // 2))
                    act.activation(yo[b % 2][:, 0:512], psY[:, 0, :], ACT.Copy).then_inc(S["ya"], 1)

                def ring(i, first, last):
                    for b in range(R):
                        e = R * i + b
                        act.wait_ge(S["gu"], e + 1)
                        if not (first and b == 0):
                            act.wait_ge(S["hid"], e)
                        act.activation(sgt[:, :], psG[b % 2][:, 0, :], ACT.Silu).then_inc(S["sil"], 1)
                        if b:
                            y_out(i, b - 1, first)
                        elif not first:
                            y_out(i - 1, R - 1, False)
                        if b < R - 1:
                            feat(i, b + 1)
                        elif not last:
                            feat(i + 1, 0)

                feat(0, 0)
                ends(act, EP, ring, lead=1)
                y_out(EP - 1, R - 1, False)

            @block.vector
            def _(dve):
                def y_out(i, b, first):
                    dve.wait_ge(S["dn"], R * i + b + 1)
                    if not (first and b < 2):
                        dve.wait_ge(s_sc[b % 2], 16 * (R // 2 * i + b // 2))
                    dve.tensor_copy(yo[b % 2][:, 512:], psY[:, 1, :]).then_inc(S["yv"], 1)

                def ring(i, first, last):
                    for b in range(R):
                        e = R * i + b
                        dve.wait_ge(S["sil"], e + 1)
                        if not (first and b < 2):
                            dve.wait_ge(S["trh"], e - 1)
                        dve.tensor_tensor(hid[b % 2][:, :], sgt[:, :], psG[b % 2][:, 1, :], ALU.mult).then_inc(S["hid"], 1)
                        if b:
                            y_out(i, b - 1, first)
                        elif not first:
                            y_out(i - 1, R - 1, False)
                        dve.wait_ge(S["trh"], e + 1)
                        if not (first and b < 2):
                            dve.wait_ge(S["dn"], e - 1)
                        dve.tensor_copy(hidT[b % 2][:, :, :], psH[:, :, :]).then_inc(S["hidT"], 1)

                ends(dve, EP, ring, lead=1)
                y_out(EP - 1, R - 1, False)

            tiles.close()
            S = {n: sem(c8, f"s9_{n}") for n in (
                "tr", "hgT", "gu", "sil", "hid", "trh", "hidT", "dn", "ya", "yv", "fin", "gate", "w", "hg", "sc", "pg")}
            block = c8.enter_context(nc.Block())

            def overflow(eng, body):
                count = eng.value_load(over[0:1, NOVER:NOVER + 1], min_val=0, max_val=NOVER)
                with eng.If(0 < count):
                    with eng.Fori(0, NOVER) as j:
                        with eng.If(j < count):
                            body(j)

            @block.sync
            def _(sp):
                def load(j):
                    sp.wait_ge(S["fin"], j + 1)
                    e = sp.value_load(over[0:1, bass.ds(j, 1)], min_val=0, max_val=NE - 1)
                    load_gate_up(sp, e, 0, S["w"])
                    load_down(sp, e, 0, S["w"])

                overflow(sp, load)

            @block.gpsimd
            def _(gp):
                gp.sem_inc(S["fin"], 1)

                def tile(j):
                    gp.tensor_copy(ig[0][:, :], idxg[:, bass.ds(j + NE, 1)])
                    gp.tensor_copy(is_[0][:, :], idxs[:, bass.ds(j + NE, 1)]).then_inc(S["pg"], 1)
                    gp.wait_ge(S["pg"], j + 1)
                    gp.sem_inc(S["gate"], 1)
                    gp.indirect_dma_start(out=hg[0][:, :], out_offset=None, in_=scratch["h2"][:, :],
                                          in_offset=bass.IndirectOffsetOnAxis(ap=ig[0][:, 0:1], axis=0),
                                          bounds_check=SEQ - 1, oob_is_err=False).then_inc(S["hg"], 16)
                    gp.wait_ge(S["ya"], j + 1)
                    gp.wait_ge(S["yv"], j + 1)
                    gp.sem_inc(S["gate"], 1)
                    gp.indirect_dma_start(out=scratch["ypair"][:, :],
                                          out_offset=bass.IndirectOffsetOnAxis(ap=is_[0][:, 0:1], axis=0),
                                          in_=yo[0][:, :], in_offset=None, bounds_check=2 * SEQ - 1,
                                          oob_is_err=False).then_inc(S["sc"], 16)
                    gp.wait_ge(S["sc"], 16 * (j + 1))
                    gp.sem_inc(S["fin"], 1)

                overflow(gp, tile)

            @block.tensor
            def _(pe):
                def tile(j):
                    pe.wait_ge(S["hg"], 16 * (j + 1))
                    for k in range(KT):
                        last = pe.transpose(psT[:, k, :], hg[0][:, k::KT], ident)
                    last.then_inc(S["tr"], 1)
                    pe.wait_ge(S["hgT"], j + 1)
                    pe.wait_ge(S["w"], 48 * (j + 1))
                    for k in range(KT):
                        last = pe.matmul(psG[0][:, :, :], hgT[0][:, k, :], wgu[0][:, :, k, :],
                                         start=(k == 0), stop=(k == KT - 1))
                    last.then_inc(S["gu"], 1)
                    pe.wait_ge(S["hid"], j + 1)
                    for f in range(2):
                        last = pe.transpose(psH[:, f, :], hid[0][:, f::2], ident)
                    last.then_inc(S["trh"], 1)
                    pe.wait_ge(S["hidT"], j + 1)
                    for n in range(2):
                        for f in range(2):
                            last = pe.matmul(psY[:, n, :], hidT[0][:, f, :], wd[0][:, f, n * 512:(n + 1) * 512],
                                             start=(f == 0), stop=(f == 1))
                    last.then_inc(S["dn"], 1)

                overflow(pe, tile)

            @block.scalar
            def _(act):
                def tile(j):
                    act.wait_ge(S["tr"], j + 1)
                    act.activation(hgT[0][:, :, :], psT[:, :, :], ACT.Copy).then_inc(S["hgT"], 1)
                    act.wait_ge(S["gu"], j + 1)
                    act.activation(sgt[:, :], psG[0][:, 0, :], ACT.Silu).then_inc(S["sil"], 1)
                    act.wait_ge(S["dn"], j + 1)
                    act.activation(yo[0][:, 0:512], psY[:, 0, :], ACT.Copy).then_inc(S["ya"], 1)

                overflow(act, tile)

            @block.vector
            def _(dve):
                def tile(j):
                    dve.wait_ge(S["sil"], j + 1)
                    dve.tensor_tensor(hid[0][:, :], sgt[:, :], psG[0][:, 1, :], ALU.mult).then_inc(S["hid"], 1)
                    dve.wait_ge(S["trh"], j + 1)
                    dve.tensor_copy(hidT[0][:, :, :], psH[:, :, :]).then_inc(S["hidT"], 1)
                    dve.wait_ge(S["dn"], j + 1)
                    dve.tensor_copy(yo[0][:, 512:], psY[:, 1, :]).then_inc(S["yv"], 1)

                overflow(dve, tile)

        with ExitStack() as c10:
            yp = [sb(c10, f"yp{i}", [P, 2, D]) for i in range(TL)]
            sqj = sb(c10, "sqj10", [P, D])
            rs = sb(c10, "rs10", [P, TL, 3])
            s_in = [sem(c10, f"s10_in{i}") for i in range(TL)]
            s_sum, s_sq, s_std, s_ch, s_res, s_out, s_w0, s_y = (
                sem(c10, "s10_" + n) for n in ("sum", "sq", "std", "ch", "res", "out", "w0", "y"))
            block = c10.enter_context(nc.Block())

            @block.sync
            def _(sp):
                for t in range(TL):
                    for k in range(2):
                        o = k * SEQ + t * P
                        sp.dma_start(yp[t][:, k, :], scratch["ypair"][o:o + P, :]).then_inc(s_in[t], 16)
                for t in range(TL):
                    sp.wait_ge(s_res, t + 1)
                    sp.dma_start(out[0, t * P:(t + 1) * P, :], x1[:, t, :]).then_inc(s_out, 16)
                sp.wait_ge(s_out, 16 * TL)

            @block.scalar
            def _(act):
                def weigh(t):
                    act.wait_ge(s_in[t], 32)
                    act.activation(yp[t][:, 0, :], yp[t][:, 0, :], ACT.Copy, scale=pairw[:, 0, t:t + 1]).then_inc(s_w0, 1)

                weigh(0)
                weigh(1)
                for t in range(TL):
                    if t + 2 < TL:
                        weigh(t + 2)
                    act.wait_ge(s_sum, t + 1)
                    act.activation(sqj[:, :], yp[t][:, 0, :], ACT.Square, accum_out=rs[:, t, 0:1]).then_inc(s_sq, 1)
                    act.wait_ge(s_sq, t + 1)
                    act.activation(rs[:, t, 1:2], rs[:, t, 0:1], ACT.Sqrt, scale=1.0 / D, bias=eps[:, 0:1]).then_inc(s_std, 1)

            @block.vector
            def _(dve):
                ch = Chain(dve, s_ch)

                def mix(t):
                    y = yp[t]
                    dve.wait_ge(s_w0, t + 1)
                    dve.scalar_tensor_tensor(out=y[:, 0, :], in0=y[:, 1, :], scalar=pairw[:, 1, t:t + 1],
                                             in1=y[:, 0, :], op0=ALU.mult, op1=ALU.add).then_inc(s_sum, 1)

                mix(0)
                for t in range(TL):
                    if t + 1 < TL:
                        mix(t + 1)
                    y = yp[t]
                    dve.wait_ge(s_std, t + 1)
                    ch.link(dve.reciprocal(rs[:, t, 2:3], rs[:, t, 1:2]))
                    dve.scalar_tensor_tensor(out=y[:, 0, :], in0=y[:, 0, :], scalar=rs[:, t, 2:3],
                                             in1=g2row[:, :], op0=ALU.mult, op1=ALU.mult).then_inc(s_y, 1)

            @block.gpsimd
            def _(gp):
                for t in range(TL):
                    gp.wait_ge(s_y, t + 1)
                    gp.tensor_tensor(x1[:, t, :], x1[:, t, :], yp[t][:, 0, :], ALU.add).then_inc(s_res, 1)


INS = ["x", "c", "ctx", "c_ctx", "w_mod", "b_mod", "g_pre1", "g_post1", "g_pre2", "g_post2", "w_in", "conv_rkv",
       "gm_ln_g", "gm_ln_b", "w_spatial", "b_spatial", "decay_w0", "decay_up", "iclr_a0", "iclr_up", "k_k", "k_a",
       "r_k", "outgate_up", "lnx_g", "lnx_b", "w_out", "w_router_grp", "b_router_grp", "w_router_exp",
       "b_router_exp", "w_gate", "w_up", "w_down"]
SCRATCH = {"oA": (SEQ, AW), "yf": (SEQ, BW), "yb": (SEQ, BW), "h2": (SEQ, D), "ypair": (2 * SEQ, D),
           "lw": (P, NTOK), "sg": (P, NTOK)}


def kernel(**inputs):
    import concourse.bacc as bacc
    from concourse.bass_utils import run_bass_kernel_spmd

    nc = bacc.Bacc("TRN2", target_bir_lowering=False, num_devices=1)
    arrays, a = {}, {}
    for name in INS:
        v = np.ascontiguousarray(inputs[name])
        arrays[f"in_{name}"] = v
        a[name] = nc.dram_tensor(f"in_{name}", v.shape, mybir.dt.from_np(v.dtype), kind="ExternalInput").ap()
    arrays["in_consts"] = CONSTS
    a["consts"] = nc.dram_tensor("in_consts", CONSTS.shape, F32, kind="ExternalInput").ap()
    out = nc.dram_tensor("out_0", (1, SEQ, D), F32, kind="ExternalOutput").ap()
    scratch = {n: nc.dram_tensor(f"scratch_{n}", s, F32, kind="Internal").ap() for n, s in SCRATCH.items()}
    program(nc, a, out, scratch)
    r = run_bass_kernel_spmd(nc, [arrays], core_ids=[0])
    return r.results[0]["out_0"]
```
